# Optimizing a Trainium2 kernel written in Bass

```python
import jax, jax.numpy as jnp
from jax import lax
import numpy as np

D_MODEL = 1024
BATCH = 1
SEQ = 512
DEPTH = 1

D_MIX = D_MODEL
D_ATTN = D_MIX // 2
D_LRU = D_MIX - D_ATTN
HEAD_DIM = 64
N_ATTN_HEADS = D_ATTN // HEAD_DIM
N_LRU_BLOCKS = 8
LRU_BLOCK = D_LRU // N_LRU_BLOCKS
CONV_WIDTH = 4
LRU_C = 8.0
Q_BLOCK = 128
N_GROUPS = 4
EXPERTS_PER_GROUP = 4
N_EXPERTS = N_GROUPS * EXPERTS_PER_GROUP
TOP_K_IN_GROUP = 2
D_EXPERT = D_MODEL // 2
LN_EPS = 1e-5
RMS_EPS = 1e-6
NEG_INF = -1e30
DEEPNORM_ALPHA = (2.0 * DEPTH) ** 0.25
DEEPNORM_BETA = (8.0 * DEPTH) ** -0.25
D_IN = 3 * D_ATTN + N_ATTN_HEADS + 2 * D_LRU


def layer_norm(x, gain=None, bias=None):
    xf = x.astype(jnp.float32)
    mu = jnp.mean(xf, axis=-1, keepdims=True)
    var = jnp.mean(jnp.square(xf - mu), axis=-1, keepdims=True)
    y = (xf - mu) * lax.rsqrt(var + LN_EPS)
    if gain is not None:
        y = y * gain.astype(jnp.float32) + bias.astype(jnp.float32)
    return y.astype(x.dtype)

def rms_norm(x, gain):
    xf = x.astype(jnp.float32)
    y = xf * lax.rsqrt(jnp.mean(jnp.square(xf), axis=-1, keepdims=True) + RMS_EPS)
    return (y * gain.astype(jnp.float32)).astype(x.dtype)

def forgetting_attention(q, k, v, f_logit):
    b, s, h, dh = q.shape
    cum = jnp.cumsum(jax.nn.log_sigmoid(f_logit.astype(jnp.float32)), axis=1)
    cum = jnp.transpose(cum, (0, 2, 1))
    q = jnp.transpose(q, (0, 2, 1, 3)) * (dh ** -0.5)
    k = jnp.transpose(k, (0, 2, 1, 3))
    v = jnp.transpose(v, (0, 2, 1, 3))
    outs = []
    for i in range(s // Q_BLOCK):
        q0 = i * Q_BLOCK
        kend = q0 + Q_BLOCK
        qb = q[:, :, q0:kend]
        kb = k[:, :, :kend]
        vb = v[:, :, :kend]
        logits = jnp.einsum('bhqd,bhkd->bhqk', qb, kb).astype(jnp.float32)
        logits = logits + (cum[:, :, q0:kend, None] - cum[:, :, None, :kend])
        causal = jnp.arange(kend)[None, :] <= (q0 + jnp.arange(Q_BLOCK))[:, None]
        logits = jnp.where(causal, logits, NEG_INF)
        p = jax.nn.softmax(logits, axis=-1).astype(v.dtype)
        outs.append(jnp.einsum('bhqk,bhkd->bhqd', p, vb))
    o = jnp.concatenate(outs, axis=2)
    return jnp.transpose(o, (0, 2, 1, 3)).reshape(b, s, h * dh)

def rg_lru_branch(xb, gb, conv_w, conv_b, w_rg, b_rg, w_ig, b_ig, lru_lambda):
    b, s, _ = xb.shape
    xc = lax.conv_general_dilated(
        xb, conv_w[:, None, :].astype(xb.dtype), window_strides=(1,),
        padding=((CONV_WIDTH - 1, 0),), dimension_numbers=('NWC', 'WIO', 'NWC'),
        feature_group_count=D_LRU) + conv_b
    xr = xc.reshape(b, s, N_LRU_BLOCKS, LRU_BLOCK)
    r = jax.nn.sigmoid(jnp.einsum('bsni,nij->bsnj', xr, w_rg).reshape(b, s, D_LRU) + b_rg)
    ig = jax.nn.sigmoid(jnp.einsum('bsni,nij->bsnj', xr, w_ig).reshape(b, s, D_LRU) + b_ig)
    log_a = -LRU_C * r.astype(jnp.float32) * jax.nn.softplus(-lru_lambda.astype(jnp.float32))
    a = jnp.exp(log_a)
    u = jnp.sqrt(-jnp.expm1(2.0 * log_a)) * (ig * xc).astype(jnp.float32)

    def combine(e1, e2):
        a1, b1 = e1
        a2, b2 = e2
        return a1 * a2, a2 * b1 + b2

    _, hs = lax.associative_scan(combine, (a, u), axis=1)
    return hs.astype(xb.dtype) * jax.nn.gelu(gb)

def hybrid_mixer(u, w_in, b_f, conv_w, conv_b, w_rg, b_rg, w_ig, b_ig, lru_lambda,
                 g_attn, g_lru, w_out):
    b, s, _ = u.shape
    proj = jnp.einsum('bsd,de->bse', u, w_in)
    q, k, v, f_logit, xb, gb = jnp.split(
        proj, [D_ATTN, 2 * D_ATTN, 3 * D_ATTN, 3 * D_ATTN + N_ATTN_HEADS,
               3 * D_ATTN + N_ATTN_HEADS + D_LRU], axis=-1)
    hs = (b, s, N_ATTN_HEADS, HEAD_DIM)
    attn = forgetting_attention(q.reshape(hs), k.reshape(hs), v.reshape(hs), f_logit + b_f)
    lru = rg_lru_branch(xb, gb, conv_w, conv_b, w_rg, b_rg, w_ig, b_ig, lru_lambda)
    mixed = jnp.concatenate([rms_norm(attn, g_attn), rms_norm(lru, g_lru)], axis=-1)
    return jnp.einsum('bse,ed->bsd', mixed, w_out)

def hierarchical_moe(u, w_grp, b_grp, w_exp, b_exp, w_e_gate, w_e_up, w_e_down):
    b, s, d = u.shape
    t = u.reshape(b * s, d)
    grp_prob = jax.nn.softmax((t @ w_grp + b_grp).astype(jnp.float32), axis=-1)
    grp_w, grp_idx = lax.top_k(grp_prob, 1)
    exp_logits = (t @ w_exp + b_exp).astype(jnp.float32).reshape(-1, N_GROUPS, EXPERTS_PER_GROUP)
    sel_logits = jnp.take_along_axis(exp_logits, grp_idx[:, :, None], axis=1)[:, 0]
    top_w, top_idx = lax.top_k(jax.nn.softmax(sel_logits, axis=-1), TOP_K_IN_GROUP)
    top_w = top_w / jnp.sum(top_w, axis=-1, keepdims=True) * grp_w
    expert_id = grp_idx * EXPERTS_PER_GROUP + top_idx
    comb = jnp.sum(jax.nn.one_hot(expert_id, N_EXPERTS, dtype=jnp.float32)
                   * top_w[..., None], axis=1).astype(t.dtype)
    y = jnp.zeros_like(t)
    for e in range(N_EXPERTS):
        h = jax.nn.silu(t @ w_e_gate[e]) * (t @ w_e_up[e])
        y = y + comb[:, e:e + 1] * (h @ w_e_down[e])
    return y.reshape(b, s, d)

def first_inputs(seed: int = 0) -> dict:
    key = jax.random.key(seed)
    ks = jax.random.split(key, 28)
    nrm = jax.random.normal
    L = DEPTH
    x = nrm(ks[0], (BATCH, SEQ, D_MODEL), jnp.float32)
    c = nrm(ks[1], (BATCH, D_MODEL), jnp.float32)
    w_ada = nrm(ks[2], (L, D_MODEL, 6 * D_MODEL)) * (0.1 * D_MODEL ** -0.5)
    b_ada = nrm(ks[3], (L, 6 * D_MODEL)) * 0.01
    w_in = nrm(ks[4], (L, D_MODEL, D_IN)) * D_MODEL ** -0.5
    w_in = w_in.at[..., 2 * D_ATTN:3 * D_ATTN].multiply(DEEPNORM_BETA)
    b_f = jax.random.uniform(ks[5], (L, N_ATTN_HEADS), minval=1.0, maxval=6.0)
    conv_w = nrm(ks[6], (L, CONV_WIDTH, D_LRU)) * CONV_WIDTH ** -0.5
    conv_b = nrm(ks[7], (L, D_LRU)) * 0.01
    w_rg = nrm(ks[8], (L, N_LRU_BLOCKS, LRU_BLOCK, LRU_BLOCK)) * LRU_BLOCK ** -0.5
    b_rg = nrm(ks[9], (L, D_LRU)) * 0.01
    w_ig = nrm(ks[10], (L, N_LRU_BLOCKS, LRU_BLOCK, LRU_BLOCK)) * LRU_BLOCK ** -0.5
    b_ig = nrm(ks[11], (L, D_LRU)) * 0.01
    a_c = jax.random.uniform(ks[12], (L, D_LRU), minval=0.9, maxval=0.999)
    a0 = a_c ** (1.0 / LRU_C)
    lru_lambda = jnp.log(a0) - jnp.log1p(-a0)
    g_attn = 1.0 + 0.02 * nrm(ks[13], (L, D_ATTN))
    g_lru = 1.0 + 0.02 * nrm(ks[14], (L, D_LRU))
    w_out = nrm(ks[15], (L, D_MIX, D_MODEL)) * (D_MIX ** -0.5 * DEEPNORM_BETA)
    ln1_g = 1.0 + 0.02 * nrm(ks[16], (L, D_MODEL))
    ln1_b = 0.01 * nrm(ks[17], (L, D_MODEL))
    w_grp = nrm(ks[18], (L, D_MODEL, N_GROUPS)) * D_MODEL ** -0.5
    b_grp = 0.01 * nrm(ks[19], (L, N_GROUPS))
    w_exp = nrm(ks[20], (L, D_MODEL, N_EXPERTS)) * D_MODEL ** -0.5
    b_exp = 0.01 * nrm(ks[21], (L, N_EXPERTS))
    w_e_gate = nrm(ks[22], (L, N_EXPERTS, D_MODEL, D_EXPERT)) * D_MODEL ** -0.5
    w_e_up = nrm(ks[23], (L, N_EXPERTS, D_MODEL, D_EXPERT)) * D_MODEL ** -0.5
    w_e_down = nrm(ks[24], (L, N_EXPERTS, D_EXPERT, D_MODEL)) * (D_EXPERT ** -0.5 * DEEPNORM_BETA)
    ln2_g = 1.0 + 0.02 * nrm(ks[25], (L, D_MODEL))
    ln2_b = 0.01 * nrm(ks[26], (L, D_MODEL))
    return {"x": x, "c": c, "w_ada": w_ada, "b_ada": b_ada, "w_in": w_in, "b_f": b_f,
            "conv_w": conv_w, "conv_b": conv_b, "w_rg": w_rg, "b_rg": b_rg,
            "w_ig": w_ig, "b_ig": b_ig, "lru_lambda": lru_lambda, "g_attn": g_attn,
            "g_lru": g_lru, "w_out": w_out, "ln1_g": ln1_g, "ln1_b": ln1_b,
            "w_grp": w_grp, "b_grp": b_grp, "w_exp": w_exp, "b_exp": b_exp,
            "w_e_gate": w_e_gate, "w_e_up": w_e_up, "w_e_down": w_e_down,
            "ln2_g": ln2_g, "ln2_b": ln2_b}

def first_block(x, c, w_ada, b_ada, w_in, b_f, conv_w, conv_b, w_rg, b_rg, w_ig, b_ig,
              lru_lambda, g_attn, g_lru, w_out, ln1_g, ln1_b, w_grp, b_grp, w_exp, b_exp,
              w_e_gate, w_e_up, w_e_down, ln2_g, ln2_b):
    for l in range(DEPTH):
        mod = jnp.einsum('bd,de->be', jax.nn.silu(c), w_ada[l]) + b_ada[l]
        sh_m, sc_m, gt_m, sh_f, sc_f, gt_f = jnp.split(mod[:, None, :], 6, axis=-1)
        u = layer_norm(x) * (1.0 + sc_m) + sh_m
        mix = hybrid_mixer(u, w_in[l], b_f[l], conv_w[l], conv_b[l], w_rg[l], b_rg[l],
                           w_ig[l], b_ig[l], lru_lambda[l], g_attn[l], g_lru[l], w_out[l])
        x = layer_norm(DEEPNORM_ALPHA * x + (1.0 + gt_m) * mix, ln1_g[l], ln1_b[l])
        u = layer_norm(x) * (1.0 + sc_f) + sh_f
        ffn = hierarchical_moe(u, w_grp[l], b_grp[l], w_exp[l], b_exp[l],
                               w_e_gate[l], w_e_up[l], w_e_down[l])
        x = layer_norm(DEEPNORM_ALPHA * x + (1.0 + gt_f) * ffn, ln2_g[l], ln2_b[l])
    return x


_first_inputs = first_inputs


def first_inputs(seed=0):
    import zlib

    import numpy as np

    out = dict(_first_inputs(seed))
    spreads = {}
    factors = {'b_rg': 27.36,
     'b_ig': 21.893,
     'g_attn': 17.81,
     'g_lru': 18.723,
     'ln1_b': 4.183,
     'b_grp': 28.587,
     'b_exp': 27.455,
     'ln2_g': 7.778,
     'ln2_b': 15.654}
    for name, (base, spread) in spreads.items():
        noise = np.random.default_rng([zlib.crc32(name.encode()), seed]).standard_normal(out[name].shape)
        drawn = base * np.exp(spread * noise) if base else spread * noise
        out[name] = __import__('jax').numpy.asarray(drawn.astype(out[name].dtype))
    for name, factor in factors.items():
        out[name] = (out[name] * factor).astype(out[name].dtype)
    return out


_narrow_inputs = first_inputs


def first_inputs(seed=0):
    out = dict(_narrow_inputs(seed))
    wider = {'g_attn': 4.17, 'g_lru': 4.14, 'ln2_g': 3.13, 'ln2_b': 3.13}
    for name, times in wider.items():
        mean = out[name].mean()
        out[name] = (mean + times * (out[name] - mean)).astype(out[name].dtype)
    return out


DEPTH_2 = 2

GRID_W = 64
N_MEM = 256
NA_HEADS = 6
NA_KH = 8
NA_KW = 16
DIL_PAIRS = ((128, 1), (512, 4), (2048, 16))
DIL_HEADS_PER_GROUP = 2
DIL_HEADS = 6
MEM_HEADS = 4
D_A = 384
D_B = 384
D_B_OUT = 128
D_M = 256
N_BRANCH = 3
D_IN_2 = 3 * D_A + 3 * D_B + D_M + N_BRANCH * D_MODEL
D_FF = 2816
CONV_W = 3
NEG_INF_2 = -1e30


def rms_norm_2(x, g):
    xf = x.astype(jnp.float32)
    y = xf * lax.rsqrt(jnp.mean(xf * xf, axis=-1, keepdims=True) + RMS_EPS)
    return (y * g.astype(jnp.float32)).astype(x.dtype)

def split_heads(t, n_heads):
    B, S, _ = t.shape
    return t.reshape(B, S, n_heads, HEAD_DIM).transpose(0, 2, 1, 3)

def alibi_slopes(n):
    return 2.0 ** (-8.0 * jnp.arange(1, n + 1, dtype=jnp.float32) / n)

def neighborhood_attention(q, k, v, rpb):
    B, H, S, d = q.shape
    rows = S // GRID_W
    kh = min(NA_KH, rows)
    kw = NA_KW
    scale = d ** -0.5
    qg = q.reshape(B, H, rows, GRID_W, d)
    kg = k.reshape(B, H, rows, GRID_W, d)
    vg = v.reshape(B, H, rows, GRID_W, d)
    cols = jnp.arange(GRID_W)
    col_start = jnp.clip(cols - kw // 2, 0, GRID_W - kw)
    col_idx = col_start[:, None] + jnp.arange(kw)[None, :]
    col_off = col_idx - cols[:, None] + (NA_KW - 1)
    rpb_c = rpb[:, :, col_off]

    def one_row(i):
        r0 = jnp.clip(i - kh // 2, 0, rows - kh)
        k_band = lax.dynamic_slice_in_dim(kg, r0, kh, axis=2)
        v_band = lax.dynamic_slice_in_dim(vg, r0, kh, axis=2)
        k_win = k_band[:, :, :, col_idx, :]
        v_win = v_band[:, :, :, col_idx, :]
        q_row = lax.dynamic_index_in_dim(qg, i, axis=2, keepdims=False)
        s = jnp.einsum('bhqd,bhrqcd->bhqrc', q_row, k_win).astype(jnp.float32) * scale
        row_off = r0 + jnp.arange(kh) - i + (NA_KH - 1)
        bias = jnp.take(rpb_c, row_off, axis=1).transpose(0, 2, 1, 3)
        s = s + bias.astype(jnp.float32)[None]
        p = jax.nn.softmax(s.reshape(B, H, GRID_W, kh * kw), axis=-1).reshape(B, H, GRID_W, kh, kw)
        return jnp.einsum('bhqrc,bhrqcd->bhqd', p.astype(v.dtype), v_win)

    out = lax.map(one_row, jnp.arange(rows))
    return out.transpose(1, 2, 0, 3, 4).reshape(B, H, S, d)

def dilated_attention(q, k, v):
    B, _, S, d = q.shape
    n_blk = S // Q_BLOCK
    scale = d ** -0.5
    slopes = alibi_slopes(DIL_HEADS)
    outs, lses = [], []
    for g, (window, dilation) in enumerate(DIL_PAIRS):
        hs = slice(g * DIL_HEADS_PER_GROUP, (g + 1) * DIL_HEADS_PER_GROUP)
        qg, kg, vg = q[:, hs], k[:, hs], v[:, hs]
        half = window // 2 // dilation
        offs = dilation * jnp.arange(-half, half + 1)
        alibi = -slopes[hs][:, None, None] * jnp.abs(offs).astype(jnp.float32)[None, None, :]
        qb = qg.reshape(B, DIL_HEADS_PER_GROUP, n_blk, Q_BLOCK, d)

        def one_block(bi):
            pos = bi * Q_BLOCK + jnp.arange(Q_BLOCK)
            idx = pos[:, None] + offs[None, :]
            valid = (idx >= 0) & (idx < S)
            idx_c = jnp.clip(idx, 0, S - 1)
            kk = jnp.take(kg, idx_c, axis=2)
            vv = jnp.take(vg, idx_c, axis=2)
            qq = lax.dynamic_index_in_dim(qb, bi, axis=2, keepdims=False)
            s = jnp.einsum('bhqd,bhqkd->bhqk', qq, kk).astype(jnp.float32) * scale + alibi[None]
            s = jnp.where(valid[None, None], s, NEG_INF_2)
            m = jnp.max(s, axis=-1, keepdims=True)
            p = jnp.exp(s - m)
            den = jnp.sum(p, axis=-1, keepdims=True)
            o = jnp.einsum('bhqk,bhqkd->bhqd', (p / den).astype(v.dtype), vv)
            lse = (m + jnp.log(den))[..., 0]
            return o, lse

        o, lse = lax.map(one_block, jnp.arange(n_blk))
        outs.append(o.transpose(1, 2, 0, 3, 4).reshape(B, DIL_HEADS_PER_GROUP, S, d))
        lses.append(lse.transpose(1, 2, 0, 3).reshape(B, DIL_HEADS_PER_GROUP, S))
    o_all = jnp.stack(outs, axis=0)
    alpha = jax.nn.softmax(jnp.stack(lses, axis=0), axis=0)
    out = jnp.einsum('gbhs,gbhsd->bshd', alpha.astype(o_all.dtype), o_all)
    return out.reshape(B, S, D_B_OUT)

def memory_attention(q, mem_n, w_kv):
    B, S, _ = q.shape
    kv = mem_n @ w_kv
    km, vm = jnp.split(kv, 2, axis=-1)
    qh = q.reshape(B, S, MEM_HEADS, HEAD_DIM)
    km = km.reshape(B, -1, MEM_HEADS, HEAD_DIM)
    vm = vm.reshape(B, -1, MEM_HEADS, HEAD_DIM)
    s = jnp.einsum('bshd,bmhd->bhsm', qh, km).astype(jnp.float32) * (HEAD_DIM ** -0.5)
    p = jax.nn.softmax(s, axis=-1)
    o = jnp.einsum('bhsm,bmhd->bshd', p.astype(vm.dtype), vm)
    return o.reshape(B, S, D_M)

def depthwise_conv_centred(u, w, b):
    S = u.shape[1]
    pad = CONV_W // 2
    up = jnp.pad(u, ((0, 0), (pad, pad), (0, 0)))
    y = b
    for j in range(CONV_W):
        y = y + up[:, j:j + S] * w[j]
    return y

def second_inputs(seed: int = 0) -> dict:
    key = jax.random.key(seed)
    ks = jax.random.split(key, 20)
    f32 = jnp.float32

    def nrm(k, shape, scale):
        return jax.random.normal(k, shape, f32) * scale

    def gain(k, shape):
        return 1.0 + 0.05 * jax.random.normal(k, shape, f32)

    return {
        'x': nrm(ks[0], (BATCH, SEQ, D_MODEL), 1.0),
        'mem': nrm(ks[1], (BATCH, N_MEM, D_MODEL), 1.0),
        'mem_norm_g': gain(ks[2], (D_MODEL,)),
        'g_pre_mix': gain(ks[3], (DEPTH_2, D_MODEL)),
        'w_in': nrm(ks[4], (DEPTH_2, D_MODEL, D_IN_2), D_MODEL ** -0.5),
        'rpb_na': nrm(ks[5], (DEPTH_2, NA_HEADS, 2 * NA_KH - 1, 2 * NA_KW - 1), 0.5),
        'w_mem_kv': nrm(ks[6], (DEPTH_2, D_MODEL, 2 * D_M), D_MODEL ** -0.5),
        'b_gate': nrm(ks[7], (DEPTH_2, N_BRANCH, D_MODEL), 0.1),
        'w_br_a': nrm(ks[8], (DEPTH_2, D_A, D_MODEL), D_A ** -0.5),
        'w_br_b': nrm(ks[9], (DEPTH_2, D_B_OUT, D_MODEL), D_B_OUT ** -0.5),
        'w_br_m': nrm(ks[10], (DEPTH_2, D_M, D_MODEL), D_M ** -0.5),
        'w_out': nrm(ks[11], (DEPTH_2, D_MODEL, D_MODEL), D_MODEL ** -0.5),
        'g_post_mix': gain(ks[12], (DEPTH_2, D_MODEL)),
        'g_pre_ffn': gain(ks[13], (DEPTH_2, D_MODEL)),
        'w_up': nrm(ks[14], (DEPTH_2, D_MODEL, 2 * D_FF), D_MODEL ** -0.5),
        'conv_w': nrm(ks[15], (DEPTH_2, CONV_W, 2 * D_FF), CONV_W ** -0.5),
        'conv_b': nrm(ks[16], (DEPTH_2, 2 * D_FF), 0.02),
        'w_down': nrm(ks[17], (DEPTH_2, D_FF, D_MODEL), D_FF ** -0.5),
        'g_post_ffn': gain(ks[18], (DEPTH_2, D_MODEL)),
    }

def second_block(x, mem, mem_norm_g, g_pre_mix, w_in, rpb_na, w_mem_kv, b_gate, w_br_a, w_br_b,
              w_br_m, w_out, g_post_mix, g_pre_ffn, w_up, conv_w, conv_b, w_down, g_post_ffn):
    B, S, D = x.shape
    splits = [D_A, 2 * D_A, 3 * D_A, 3 * D_A + D_B, 3 * D_A + 2 * D_B, 3 * D_A + 3 * D_B,
              3 * D_A + 3 * D_B + D_M]
    mem_n = rms_norm_2(mem, mem_norm_g)
    for l in range(DEPTH_2):
        h = rms_norm_2(x, g_pre_mix[l])
        proj = h @ w_in[l]
        q_a, k_a, v_a, q_b, k_b, v_b, q_m, gate_pre = jnp.split(proj, splits, axis=-1)
        o_a = neighborhood_attention(split_heads(q_a, NA_HEADS), split_heads(k_a, NA_HEADS),
                                     split_heads(v_a, NA_HEADS), rpb_na[l])
        o_a = o_a.transpose(0, 2, 1, 3).reshape(B, S, D_A)
        o_b = dilated_attention(split_heads(q_b, DIL_HEADS), split_heads(k_b, DIL_HEADS),
                                split_heads(v_b, DIL_HEADS))
        o_m = memory_attention(q_m, mem_n, w_mem_kv[l])
        gates = jax.nn.sigmoid(gate_pre.reshape(B, S, N_BRANCH, D) + b_gate[l])
        merged = (gates[:, :, 0] * (o_a @ w_br_a[l])
                  + gates[:, :, 1] * (o_b @ w_br_b[l])
                  + gates[:, :, 2] * (o_m @ w_br_m[l]))
        x = x + rms_norm_2(merged @ w_out[l], g_post_mix[l])
        h = rms_norm_2(x, g_pre_ffn[l])
        u = depthwise_conv_centred(h @ w_up[l], conv_w[l], conv_b[l])
        a, b = jnp.split(u, 2, axis=-1)
        f = jax.nn.gelu(a) * b
        x = x + rms_norm_2(f @ w_down[l], g_post_ffn[l])
    return x


def setup_inputs(seed=0):
    out = dict(first_inputs(seed))
    for name, value in second_inputs(seed + 1).items():
        if name != "x":
            out[name + "_2"] = value
    return out


def reference(
    x, c, w_ada, b_ada, w_in, b_f, conv_w, conv_b, w_rg, b_rg, w_ig, b_ig, lru_lambda, g_attn,
    g_lru, w_out, ln1_g, ln1_b, w_grp, b_grp, w_exp, b_exp, w_e_gate, w_e_up, w_e_down, ln2_g,
    ln2_b, mem_2, mem_norm_g_2, g_pre_mix_2, w_in_2, rpb_na_2, w_mem_kv_2, b_gate_2, w_br_a_2,
    w_br_b_2, w_br_m_2, w_out_2, g_post_mix_2, g_pre_ffn_2, w_up_2, conv_w_2, conv_b_2,
    w_down_2, g_post_ffn_2,
):
    x = first_block(
        x, c, w_ada, b_ada, w_in, b_f, conv_w, conv_b, w_rg, b_rg, w_ig, b_ig, lru_lambda,
        g_attn, g_lru, w_out, ln1_g, ln1_b, w_grp, b_grp, w_exp, b_exp, w_e_gate, w_e_up,
        w_e_down, ln2_g, ln2_b,
    )
    return second_block(
        x, mem_2, mem_norm_g_2, g_pre_mix_2, w_in_2, rpb_na_2, w_mem_kv_2, b_gate_2, w_br_a_2,
        w_br_b_2, w_br_m_2, w_out_2, g_post_mix_2, g_pre_ffn_2, w_up_2, conv_w_2, conv_b_2,
        w_down_2, g_post_ffn_2,
    )


_drawn_inputs = setup_inputs


def setup_inputs(seed=0):
    import zlib

    import numpy as np

    out = dict(_drawn_inputs(seed))
    spreads = {}
    factors = {'mem_norm_g_2': 8.0,
     'g_pre_mix_2': 4.793,
     'b_gate_2': 7.853,
     'g_post_mix_2': 5.947,
     'g_pre_ffn_2': 4.384,
     'conv_b_2': 8.0,
     'g_post_ffn_2': 6.268}
    for name, (base, spread) in spreads.items():
        noise = np.random.default_rng([zlib.crc32(name.encode()), seed]).standard_normal(out[name].shape)
        drawn = base * np.exp(spread * noise) if base else spread * noise
        out[name] = __import__('jax').numpy.asarray(drawn.astype(out[name].dtype))
    for name, factor in factors.items():
        out[name] = (out[name] * factor).astype(out[name].dtype)
    return out
```

```python
from contextlib import ExitStack

import numpy as np
import concourse.bass as bass
from concourse import mybir

F32 = mybir.dt.float32
ALU = mybir.AluOpType
ACT = mybir.ActivationFunctionType
AX_X = mybir.AxisListType.X

P = 128
S = 512
D = 1024
KB = D // P
TT = S // P
DH = 64
D_ATTN = 512
HEADS = 8
CONV = 4
N_GROUPS, PER_GROUP = 4, 4
EXPERTS = N_GROUPS * PER_GROUP
D_EXPERT = 512
EB = D_EXPERT // P
ALPHA = 2.0 ** 0.25
LN_EPS, RMS_EPS = 1e-5, 1e-6
LRU_C = 8.0
LAYERS = 2
GRID_W = 64
ROWS = S // GRID_W
NA_HEADS, NA_KH, NA_KW = 6, 8, 16
DIL_HEADS, DIL_G = 6, 3
MEM_HEADS, N_MEM = 4, 256
D_A, D_B, D_M = 384, 384, 256
D_FF = 2816
FB = D_FF // P
MASKED = -1e30
BIG = 3.0e38

RING = 8
PER_CHUNK = 16
STREAM = {
    "A": [("ada0", 16 * KB)]
    + [(f"{n}{m}", KB) for n in ("xb", "gb", "q", "k") for m in range(4)]
    + [("v3", 4 * KB)]
    + [(f"{n}{m}", 1) for n in ("r", "i") for m in range(4)] + [("i3", 8)]
    + [("ada1", 16 * KB), ("ada2", 16 * KB)]
    + [(f"out{m}", KB) for m in range(KB)],
    "M": [x for e in range(PER_GROUP)
          for x in [(f"{n}{e}.{m}", KB) for m in range(EB) for n in ("gate", "up")]
          + [(f"down{e}.{m}", EB) for m in range(KB)]],
    "L": [(f"qk{m}", KB) for m in range(14)] + [("va3", 4 * KB), ("vb3", 2 * KB)]
    + [(f"km{m}", KB) for m in range(2)] + [("vm1", 2 * KB)]
    + [x for m in range(KB) for x in ((f"g0.{m}", KB), (f"ba{m}", 3), (f"g1.{m}", KB), (f"bb{m}", 1),
                                      (f"g2.{m}", KB), (f"bm{m}", 2))]
    + [(f"out{m}", KB) for m in range(KB)]
    + [(f"{n}{j}", KB) for j in range(FB) for n in ("a", "b")]
    + [(f"down{m}", FB) for m in range(KB)],
}
LIN = {
    "A": ["ada0", "f"] + [f"{n}{m}" for n in ("xb", "gb", "q", "k", "v") for m in range(4)]
    + [f"{n}{m}" for n in ("r", "i") for m in range(4)] + ["ada1", "ada2", "cumT"]
    + [f"nc{h}" for h in range(HEADS)] + [f"out{m}" for m in range(KB)] + ["rt0", "rt1", "cbT"]
    + [f"cb{e}" for e in range(EXPERTS)],
    "M": [n for n, _ in STREAM["M"]],
    "B": [],
    "L": [f"qk{m}" for m in range(14)] + [f"va{t}" for t in range(TT)] + [f"vb{r}" for r in range(4)]
    + ["km0", "km1", "vm0", "vm1"]
    + [f"{n}{m}" for m in range(KB) for n in ("g0.", "ba", "g1.", "bb", "g2.", "bm")]
    + [f"out{m}" for m in range(KB)] + [f"{n}{j}" for j in range(FB) for n in ("a", "b")]
    + [f"down{m}" for m in range(KB)],
}
TRIPS = {"A": 1, "M": N_GROUPS, "B": 1, "L": LAYERS}
ORDER = ["A", "M", "B", "L"]
LAST_USE = {ph: [n for n, k in s for _ in range(k)] for ph, s in STREAM.items()}
CHUNKS = {ph: len(b) // PER_CHUNK for ph, b in LAST_USE.items()}
FIRST_CHUNK = {"A": 0, "M": CHUNKS["A"], "L": CHUNKS["A"] + N_GROUPS * CHUNKS["M"]}
N_CHUNKS = FIRST_CHUNK["L"] + LAYERS * CHUNKS["L"]
BLOCK0 = {}
for _ph, _s in STREAM.items():
    _n = 0
    BLOCK0[_ph] = {}
    for _name, _k in _s:
        BLOCK0[_ph].setdefault(_name, _n)
        _n += _k
BLOCK0["A"]["v0"] = BLOCK0["A"]["v3"]
BLOCK0["L"]["va0"], BLOCK0["L"]["vb0"], BLOCK0["L"]["vm0"] = (BLOCK0["L"][n] for n in ("va3", "vb3", "vm1"))

TILES = {
    "A": [("fa", h // 2, h % 2, t) for h in range(HEADS) for t in range(TT)],
    "L": [("na", h // 2, h % 2, t) for h in range(NA_HEADS) for t in range(TT)]
    + [("dil", 0, b, r) for b in range(2) for r in range(4)]
    + [("mem", h // 2, h % 2, t) for h in range(MEM_HEADS) for t in range(TT)],
}


def key_chunks(kind, t):
    return {"fa": t + 1, "na": 4, "dil": 6, "mem": 2}[kind]


ROUNDS = {ph: [(i, c, min(4, key_chunks(x[0], x[3]) - c)) for i, x in enumerate(tl)
               for c in range(0, key_chunks(x[0], x[3]), 4)] for ph, tl in TILES.items()}
ROUNDS_OF = {ph: [[j for j, x in enumerate(rs) if x[0] == i] for i in range(len(TILES[ph]))]
             for ph, rs in ROUNDS.items()}
OUTS = {ph: list(dict.fromkeys((x[0], x[1]) for x in tl)) for ph, tl in TILES.items()}

VEC = {}
_at = 0
for _n, _w in (("c", 8), ("b_ada", 48), ("b_f", 1), ("conv_w", 16), ("conv_b", 4), ("b_rg", 4), ("b_ig", 4),
               ("lam", 4), ("g_attn", 4), ("g_lru", 4), ("ln1_g", 8), ("ln1_b", 8), ("ln2_g", 8), ("ln2_b", 8),
               ("mem_g", 8)):
    VEC[_n] = _at
    _at += _w
N_VEC = _at
LVEC = {}
_at = 0
for _n, _w in (("g_pre_mix", 8), ("b_gate", 24), ("g_post_mix", 8), ("g_pre_ffn", 8), ("conv_w", 3 * 2 * FB),
               ("conv_b", 2 * FB), ("g_post_ffn", 8)):
    LVEC[_n] = _at
    _at += _w
N_LVEC = _at

NA_SLOTS = 2 * ROWS - 2
DIL_W = S + 3 + 2 * P


class Phase:

    def __init__(self, name, reg=None):
        self.name, self.reg = name, reg


class Signal:

    def __init__(self, sem, events, unit=1):
        self.sem, self.unit = sem, unit
        self.events = {ph: list(events.get(ph, [])) for ph in ORDER}
        self.index = {ph: {e: i for i, e in enumerate(v)} for ph, v in self.events.items()}
        self.seen = {ph: set() for ph in ORDER}

    def count(self, ph, n):
        base = 0
        for q in ORDER:
            if q == ph.name:
                break
            base += TRIPS[q] * len(self.events[q])
        c = (base + n) * self.unit
        return c if ph.reg is None else ph.reg * (len(self.events[ph.name]) * self.unit) + c

    def by(self, ph, event):
        return self.sem, self.count(ph, self.index[ph.name][event] + 1)

    def before(self, ph, event):
        return self.sem, self.count(ph, self.index[ph.name][event])

    def on(self, ph, event):
        assert event in self.index[ph.name] and event not in self.seen[ph.name], event
        self.seen[ph.name].add(event)
        return self.sem, self.unit

    def done(self):
        for ph in ORDER:
            assert self.seen[ph] == set(self.events[ph]), (self.sem, ph)


def build(nc, weights, xT_in, memT_in, vec_in, lvec_in, small_in, route_w_in, route_b_in, na_bias_in,
          const_in, dil_in, out):
    with ExitStack() as ctx:
        def sb(name, shape):
            return ctx.enter_context(nc.sbuf_tensor(name, shape, F32))

        def sem(name):
            return ctx.enter_context(nc.semaphore(name))

        ring = sb("ring", [P, RING, PER_CHUNK * P])
        x = sb("x", [P, KB, S])
        h = sb("h", [P, KB, S])
        y = sb("y", [P, KB, S])
        big = sb("big", [P, FB, S])
        ob = sb("ob", [P, 6, S])
        mem = sb("mem", [P, KB, N_MEM])
        nab = sb("nab", [P, 2, NA_SLOTS * GRID_W])
        dil = sb("dil", [P, 2, DIL_W])
        tmp = sb("tmp", [P, 2, S])
        gat = sb("gat", [P, 2, S])
        sd = sb("sd", [P, S])
        rstd = sb("rstd", [P, S])
        consts = sb("consts", [P, 2 * P + GRID_W])
        ones_d = sb("ones_d", [P, P])
        ones_h = sb("ones_h", [P, P])
        vec = sb("vec", [P, N_VEC])
        lvec = sb("lvec", [P, N_LVEC])
        wf = sb("wf", [P, KB, HEADS])
        wr = sb("wr", [P, KB, N_GROUPS + EXPERTS])
        route_b = sb("route_b", [P, TT * 20])
        mod = sb("mod", [P, 48])
        mod1 = sb("mod1", [P, 48])
        silu_c = sb("silu_c", [P, KB])
        lam = sb("lam", [P, 6, 4])
        cumq = sb("cumq", [P, TT, HEADS])
        stat = sb("stat", [P, 4, 4])

        ident = consts[:, 0:P]
        causal = consts[:, P:2 * P]
        window = consts[:, 2 * P:2 * P + GRID_W]

        eps = sb("eps", [P, 3])

        def mem_sq(k):
            return big[:, k // 2, (k % 2) * N_MEM:(k % 2 + 1) * N_MEM]

        def v_(name, i=0):
            return vec[:, VEC[name] + i:VEC[name] + i + 1]

        def lv(name, i=0):
            return lvec[:, LVEC[name] + i:LVEC[name] + i + 1]

        qT, kT = big[:, 0:4, :], big[:, 4:8, :]
        v_tok = big[:, 8:12, :]
        conv_flat = big[:, 12:17, :].rearrange("p a b -> p (a b)")
        CW = S + CONV - 1
        xbp = [conv_flat[:, m * CW:(m + 1) * CW] for m in range(4)]
        a2 = big[:, 12:16, :]
        gg = big[:, 17:21, :]
        fl = big[0:HEADS, 21, :]
        fl2 = gat[0:HEADS, 0, :]
        one_row = gat[0:HEADS, 1, :]
        ncum = tmp[0:HEADS, 0, :]
        r_, ig = h[:, 0:4, :], h[:, 4:8, :]
        a_, xc = y[:, 0:4, :], y[:, 4:8, :]
        ob_flat = ob[:, :, :].rearrange("p a b -> p (a b)")
        y_flat = y[:, :, :].rearrange("p a b -> p (a b)")
        probs = {"A": [ob_flat[:, i * S:(i + 1) * S] for i in range(3)],
                 "L": [y_flat[:, i * 768:(i + 1) * 768] for i in range(3)]}
        probsT = {"A": [ob_flat[:, (3 + i) * S:(4 + i) * S] for i in range(2)],
                  "L": [y_flat[:, 2304 + i * S:2304 + (i + 1) * S] for i in range(2)]}
        rt = tmp[:, :, :].rearrange("p a b -> p (a b)")

        def rtv(i):
            return rt[:, i * 80:(i + 1) * 80]
        def comb_tile(t):
            return rtv(11)[:, t * EXPERTS:(t + 1) * EXPERTS]
        combT = sd[0:EXPERTS, :]
        comb_bc = big[:, 0:EXPERTS, :]
        hid = [big[:, 16:20, :], ob[:, 0:4, :]]
        sil = [gat[:, 0, :], gat[:, 1, :]]
        qa, ka, qb, kb = big[:, 0:3, :], big[:, 3:6, :], big[:, 6:9, :], big[:, 9:12, :]
        qm = big[:, 12:14, :]
        kmT = big[:, 14, :].rearrange("p (a b) -> p a b", a=2)
        va = big[:, 15:19, :]
        vb = big[:, 19:21, :].rearrange("p a b -> p (a b)").rearrange("p (r n) -> p r n", r=4)
        vm = big[:, 21, :].rearrange("p (a b) -> p a b", a=2)
        oa, obb, om = ob[:, 0:3, :], ob[:, 3:4, :], ob[:, 4:6, :]
        ffa = [ob[:, i, :] for i in range(2)]
        ffb = [ob[:, 2 + i, :] for i in range(2)]
        ffg = [ob[:, 4 + i, :] for i in range(2)]

        def pb(name, n):
            return ctx.enter_context(nc.psum_tensor(name, [P, n, S], F32))
        lin = pb("lin", 2)
        score = pb("score", 2)
        trans = pb("trans", 1)
        attn = pb("attn", 2)
        sums = pb("sums", 1)
        score_flat = score[:, :, :].rearrange("p a b -> p (a b)")

        x_in, mem_in, consts_in, vec_in_s, dil_s, lvec_s, nab_s = (
            sem(n) for n in ("x_in", "mem_in", "consts_in", "vec_in", "dil_in", "lvec_in", "nab_in"))
        out_done = sem("out_done")
        dve_step, act_step, pool_step = sem("dve_step"), sem("act_step"), sem("pool_step")
        chunk_in = [sem(f"chunk_in{s}") for s in range(RING)]
        bank_of = {ph: {g: i % 2 for i, g in enumerate(gs)} for ph, gs in LIN.items()}
        assert all(len(g) % 2 == 0 for g in LIN.values())
        lin_full = [Signal(sem(f"lin_full{b}"), {ph: g[b::2] for ph, g in LIN.items()}) for b in range(2)]
        lin_free = [Signal(sem(f"lin_free{b}"), {ph: g[b::2] for ph, g in LIN.items()}) for b in range(2)]
        signals = lin_full + lin_free

        def signal(name, **events):
            s = Signal(sem(name), events)
            signals.append(s)
            return s

        def each(names, n):
            return [(s, k) for s in names for k in range(n)]
        NA_ = [s for s in ("ln1", "ln2", "ln3")]
        LS = ["pre_mix", "post_mix", "pre_ffn", "post_ffn"]
        squares = signal("squares", A=each(["ln1", "mem"], 8) + each(["lru", "attn"], 4) + each(["ln2", "ln3"], 8),
                         B=each(["ln4"], 8), L=each(LS, 8))
        mean_full = signal("mean_full", A=NA_, B=["ln4"])
        centred = signal("centred", A=each(NA_, 8), B=each(["ln4"], 8))
        var_full = signal("var_full", A=["ln1", "mem", "lru", "attn", "ln2", "ln3"], B=["ln4"], L=LS)
        sd_ready = signal("sd_ready", A=["ln1", "mem", "lru", "attn", "ln2", "ln3"], B=["ln4"], L=LS)
        rstd_ready = signal("rstd_ready", A=["ln1", "mem", "lru", "attn", "ln2", "ln3"], B=["ln4"], L=LS)
        normed = signal("normed", A=each(["ln1", "mem"], 8) + each(["lru", "attn"], 4) + each(["ln2", "ln3"], 8),
                        B=each(["ln4"], 8), L=each(["pre_mix", "pre_ffn"], 8))
        affine = signal("affine", A=each(NA_, 8), B=each(["ln4"], 8))
        x_new = signal("x_new", A=[("mix", k) for k in range(8)], B=[("ffn", k) for k in range(8)],
                       L=each(["post_mix", "post_ffn"], 8))
        mod_ready = signal("mod_ready", A=[0, 1, 2])
        tiles = {ph: list(range(len(t))) for ph, t in TILES.items()}
        rounds = {ph: list(range(len(r))) for ph, r in ROUNDS.items()}
        qk_done = signal("qk_done", **tiles)
        score_step = signal("score_step", A=[(i, s) for i in tiles["A"] for s in range(3)],
                            L=[(i, s) for i in tiles["L"] for s in range({"na": 0, "dil": 2, "mem": 1}[TILES["L"][i][0]])])
        scored = signal("scored", **tiles)
        exp_done = signal("exp_done", **tiles)
        rden_ready = signal("rden_ready", **tiles)
        p_ready = signal("p_ready", **tiles)
        t_done = signal("t_done", **rounds)
        pt_ready = signal("pt_ready", **rounds)
        pv_done = signal("pv_done", **rounds)
        o_out = signal("o_out", **OUTS)
        nab_ready = signal("nab_ready", L=list(range(NA_HEADS)))
        f_step = signal("f_step", A=["abs", "exp", "ln", "ls", "cum", "neg"])
        sp_step = signal("sp_step", A=["neg", "abs", "exp", "ln", "sp", "c", "nc"])
        pad_done = signal("pad_done", A=[0])
        conv = signal("conv", A=[(m, s) for m in range(4) for s in range(CONV)])
        lru_act = signal("lru_act", A=[(s, m) for s in ("a", "th", "a2", "sqrt") for m in range(4)])
        lru_dve = signal("lru_dve", A=[(s, m) for s in ("u2", "igx", "u", "scan", "out") for m in range(4)])
        route_exp = signal("route_exp", A=[0])
        route_sub = signal("route_sub", A=[0])
        comb_ready = signal("comb_ready", A=[0])
        em = [(e, m) for e in range(PER_GROUP) for m in range(EB)]
        silu_ready = signal("silu_ready", M=em)
        merge_step = signal("merge_step", L=list(range(KB)))
        merged = signal("merged", L=list(range(KB)))
        upd = signal("upd", L=each(["post_mix", "post_ffn"], 8))
        conv_c = signal("conv_c", L=[(n, j) for j in range(FB) for n in ("a", "b")])
        conv_l = signal("conv_l", L=[(n, j) for j in range(FB) for n in ("a", "b")])
        gelu_ready = signal("gelu_ready", L=list(range(FB)))
        ff_ready = signal("ff_ready", L=list(range(FB)))

        A, B = Phase("A"), Phase("B")

        def chunk_value(ph, c):
            n = FIRST_CHUNK[ph.name] + c
            v = 16 * (n // RING + 1)
            if ph.reg is not None:
                assert CHUNKS[ph.name] % RING == 0
                v = ph.reg * (16 * CHUNKS[ph.name] // RING) + v
            return n % RING, v

        block = ctx.enter_context(nc.Block())

        @block.sync
        def _(sp):
            def load(c):
                sp.dma_start(ring[:, c % RING, :], weights[c]).then_inc(chunk_in[c % RING], 16)

            def used(ph, c):
                g = LAST_USE[ph.name][(c + 1) * PER_CHUNK - 1]
                sp.wait_ge(*lin_full[bank_of[ph.name][g]].by(ph, g))

            for c in range(CHUNKS["A"] + RING):
                if c >= RING:
                    used(A, c - RING)
                load(c)
            with sp.Fori(0, N_GROUPS) as g:
                ph = Phase("M", g)
                for c in range(CHUNKS["M"]):
                    used(ph, c)
                    n = FIRST_CHUNK["M"] + RING + c
                    sp.dma_start(ring[:, n % RING, :], weights[g * CHUNKS["M"] + n]).then_inc(chunk_in[n % RING], 16)
            with sp.Fori(0, LAYERS - 1) as l:
                ph = Phase("L", l)
                for c in range(CHUNKS["L"]):
                    used(ph, c)
                    n = FIRST_CHUNK["L"] + RING + c
                    sp.dma_start(ring[:, n % RING, :], weights[l * CHUNKS["L"] + n]).then_inc(chunk_in[n % RING], 16)
            last = Phase("L", None)
            for c in range(CHUNKS["L"] - RING):
                g = LAST_USE["L"][(c + 1) * PER_CHUNK - 1]
                s = lin_full[bank_of["L"][g]]
                sp.wait_ge(s.sem, s.count(last, (LAYERS - 1) * len(s.events["L"]) + s.index["L"][g] + 1))
                n = FIRST_CHUNK["L"] + (LAYERS - 1) * CHUNKS["L"] + RING + c
                load(n)

        @block.tensor
        def _(pe):
            seen = set()

            def wblock(ph, n, width=P):
                c = n // PER_CHUNK
                slot, v = chunk_value(ph, c)
                if (ph.name, c) not in seen:
                    seen.add((ph.name, c))
                    pe.wait_ge(chunk_in[slot], v)
                o = (n % PER_CHUNK) * P
                return ring[:, slot, o:o + width]

            def open_bank(ph, g):
                b = bank_of[ph.name][g]
                s, v = lin_free[b].before(ph, g)
                if not (isinstance(v, int) and v == 0):
                    pe.wait_ge(s, v)
                return lin[:, b, :]

            def linear(ph, g, rhs, kb=KB, n=S, wait=None, first=None):
                acc = open_bank(ph, g)
                n0 = BLOCK0[ph.name][g]
                for k in range(kb):
                    w = wblock(ph, n0 + k)
                    if wait:
                        wait(k)
                    mm = pe.matmul(acc[:, 0:n], w, rhs(k), start=(k == 0), stop=(k == kb - 1))
                mm.then_inc(*lin_full[bank_of[ph.name][g]].on(ph, g))

            def tokens(ph, g, n0, lhs, n, wait=None):
                acc = open_bank(ph, g)
                for k in range(KB):
                    for b in range(0, n, P):
                        w = wblock(ph, n0 + k * (n // P) + b // P)
                    w = wblock(ph, n0 + k * (n // P), n)
                    mm = pe.matmul(acc[:, 0:n], lhs(k), w, start=(k == 0), stop=(k == KB - 1))
                mm.then_inc(*lin_full[bank_of[ph.name][g]].on(ph, g))

            def mean_sum(ph, st, src, wait):
                for k in range(KB):
                    wait(k)
                    mm = pe.matmul(sums[:, 0, :], ones_d[:, :], src[:, k, :], start=(k == 0), stop=(k == KB - 1))
                mm.then_inc(*mean_full.on(ph, st))

            def square_sum(ph, st, k, src, ones, n_k=KB, n=S):
                pe.wait_ge(*squares.by(ph, (st, k)))
                mm = pe.matmul(sums[:, 0, 0:n], ones[:, :], src, start=(k == 0), stop=(k == n_k - 1))
                if k == n_k - 1:
                    mm.then_inc(*var_full.on(ph, st))

            def attention(ph, q_of, k_of, v_of, extra=None):
                name = ph.name
                tl, rs = TILES[name], ROUNDS[name]

                def qk(i):
                    kind, hp, half, t = tl[i]
                    lo = DH * half
                    if i >= 1 and (kind == "dil" or tl[i - 1][0] == "dil"):
                        pe.wait_ge(*scored.by(ph, i - 1))
                    elif i >= 2 and kind == "mem" and tl[i - 2][0] == "mem":
                        pe.wait_ge(*exp_done.by(ph, i - 2))
                    elif i >= 2:
                        pe.wait_ge(*scored.by(ph, i - 2))
                    if kind == "dil":
                        for g in range(DIL_G):
                            q = qb[lo:lo + DH, g, t::4]
                            k = kb[lo:lo + DH, g, :] if g == 0 else kb[lo:lo + DH, g, t::4]
                            o = score_flat[:, 0:S] if g == 0 else score_flat[:, S + (g - 1) * P:S + g * P]
                            mm = pe.matmul(o, q, k, start=True, stop=True)
                    else:
                        n = key_chunks(kind, t) * P
                        mm = pe.matmul(score[:, i % 2, 0:n], q_of(kind)[lo:lo + DH, hp, t * P:(t + 1) * P],
                                       k_of(kind)[lo:lo + DH, hp, 0:n], start=True, stop=True)
                    mm.then_inc(*qk_done.on(ph, i))

                def turn(j):
                    i, c0, n = rs[j]
                    if c0 == 0:
                        pe.wait_ge(*p_ready.by(ph, i))
                    if j >= 1:
                        pe.wait_ge(*pt_ready.by(ph, j - 1))
                    for c in range(n):
                        mm = pe.transpose(trans[:, 0, c * P:(c + 1) * P],
                                          probs[name][i % 3][:, (c0 + c) * P:(c0 + c + 1) * P], ident)
                    mm.then_inc(*t_done.on(ph, j))

                def pv(j):
                    i, c0, n = rs[j]
                    kind, hp, half, t = tl[i]
                    o = OUTS[name].index((kind, hp))
                    if o >= 2 and c0 == 0:
                        pe.wait_ge(*o_out.by(ph, OUTS[name][o - 2]))
                    pe.wait_ge(*pt_ready.by(ph, j))
                    total = key_chunks(kind, t)
                    lo = DH * half
                    for c in range(n):
                        mm = pe.matmul(attn[lo:lo + DH, o % 2, t * P:(t + 1) * P], v_of(kind, hp, half, t, c0 + c),
                                       probsT[name][j % 2][:, c * P:(c + 1) * P],
                                       start=(c0 + c == 0), stop=(c0 + c == total - 1))
                    mm.then_inc(*pv_done.on(ph, j))

                n = len(tl)
                for i in range(n + 3):
                    if extra and i < n:
                        extra(i)
                    if i < n:
                        qk(i)
                    if 2 <= i < n + 2:
                        for j in ROUNDS_OF[name][i - 2]:
                            turn(j)
                            if j >= 1:
                                pv(j - 1)
                pv(len(rs) - 1)

            pe.wait_ge(dve_step, 2)
            pe.wait_ge(x_in, 16)
            mean_sum(A, "ln1", x, lambda k: None)
            pe.wait_ge(*centred.by(A, ("ln1", 7)))
            for k in range(KB):
                square_sum(A, "ln1", k, y[:, k, :], ones_d)
            pe.wait_ge(*sd_ready.by(A, "ln1"))
            for k in range(KB):
                square_sum(A, "mem", k, mem_sq(k), ones_d, n=N_MEM)

            def ada(g):
                acc = open_bank(A, f"ada{g}")
                n0 = BLOCK0["A"][f"ada{g}"]
                if g == 0:
                    pe.wait_ge(act_step, 1)
                for m in range(16):
                    for k in range(KB):
                        mm = pe.matmul(acc[:, m:m + 1], wblock(A, n0 + m * KB + k), silu_c[:, k:k + 1],
                                       start=(k == 0), stop=(k == KB - 1))
                mm.then_inc(*lin_full[bank_of["A"][f"ada{g}"]].on(A, f"ada{g}"))

            ada(0)
            pe.wait_ge(consts_in, 16 * 4)
            acc = open_bank(A, "f")
            for k in range(KB):
                pe.wait_ge(*affine.by(A, ("ln1", k)))
                mm = pe.matmul(acc[0:HEADS, :], wf[:, k, :], h[:, k, :], start=(k == 0), stop=(k == KB - 1))
            mm.then_inc(*lin_full[bank_of["A"]["f"]].on(A, "f"))
            for n in ("xb", "gb", "q", "k"):
                for m in range(4):
                    linear(A, f"{n}{m}", lambda k: h[:, k, :])
            for t in range(TT):
                tokens(A, f"v{t}", BLOCK0["A"]["v3"], lambda k: h[:, k, t * P:(t + 1) * P], 512)
            for n in ("r", "i"):
                for m in range(4):
                    linear(A, f"{n}{m}", lambda k: xc[:, m, :], kb=1,
                           wait=lambda k: pe.wait_ge(*conv.by(A, (m, CONV - 1))))
            ada(1)
            ada(2)
            for k in range(4):
                square_sum(A, "lru", k, h[:, k, :], ones_h, n_k=4)
            acc = open_bank(A, "cumT")
            pe.wait_ge(*f_step.by(A, "cum"))
            for t in range(TT):
                mm = pe.transpose(acc[:, t * HEADS:(t + 1) * HEADS], fl[:, t * P:(t + 1) * P], ident[0:HEADS, 0:HEADS])
            mm.then_inc(*lin_full[bank_of["A"]["cumT"]].on(A, "cumT"))

            def negcum(i):
                todo = [0, 1] if i == 0 else [i // TT + 1] if i % TT == 0 else []
                for hd in todo:
                    if hd < HEADS:
                        acc = open_bank(A, f"nc{hd}")
                        if hd == 0:
                            pe.wait_ge(*f_step.by(A, "neg"))
                        pe.matmul(acc, ident[0:HEADS, hd:hd + 1].to_broadcast([HEADS, P]), ncum,
                                  start=True, stop=True).then_inc(*lin_full[bank_of["A"][f"nc{hd}"]].on(A, f"nc{hd}"))

            pe.wait_ge(*lin_free[bank_of["A"]["v2"]].by(A, "v2"))
            pe.wait_ge(*lin_free[bank_of["A"]["v3"]].by(A, "v3"))
            attention(A, lambda kind: qT, lambda kind: kT,
                      lambda kind, hp, half, t, c: v_tok[:, c, (2 * hp + half) * DH:(2 * hp + half + 1) * DH],
                      extra=negcum)
            for k in range(4):
                square_sum(A, "attn", k, h[:, k, :], ones_h, n_k=4)
            for m in range(KB):
                linear(A, f"out{m}", lambda k: y[:, k, :],
                       wait=(lambda k: pe.wait_ge(*normed.by(A, ("attn", k))) if k < 4 else None) if m == 0 else None)
            for st, src in (("ln2", x), ("ln3", x)):
                ev = (lambda k: x_new.by(A, ("mix", k))) if st == "ln2" else (lambda k: affine.by(A, ("ln2", k)))
                mean_sum(A, st, src, lambda k: pe.wait_ge(*ev(k)))
                pe.wait_ge(*centred.by(A, (st, 7)))
                for k in range(KB):
                    square_sum(A, st, k, (h if st == "ln2" else y)[:, k, :], ones_d)
            for half in range(2):
                acc = open_bank(A, f"rt{half}")
                for t in range(2):
                    for k in range(KB):
                        if half == 0 and t == 0:
                            pe.wait_ge(*affine.by(A, ("ln3", k)))
                        tok = (2 * half + t) * P
                        mm = pe.matmul(acc[:, t * 20:(t + 1) * 20], h[:, k, tok:tok + P], wr[:, k, :],
                                       start=(k == 0), stop=(k == KB - 1))
                mm.then_inc(*lin_full[bank_of["A"][f"rt{half}"]].on(A, f"rt{half}"))
            acc = open_bank(A, "cbT")
            pe.wait_ge(*comb_ready.by(A, 0))
            for t in range(TT):
                mm = pe.transpose(acc[0:EXPERTS, t * P:(t + 1) * P], comb_tile(t), ident)
            mm.then_inc(*lin_full[bank_of["A"]["cbT"]].on(A, "cbT"))
            for e in range(EXPERTS):
                acc = open_bank(A, f"cb{e}")
                if e == 0:
                    pe.wait_ge(*lin_free[bank_of["A"]["cbT"]].by(A, "cbT"))
                pe.matmul(acc, ident[0:EXPERTS, e:e + 1].to_broadcast([EXPERTS, P]), combT,
                          start=True, stop=True).then_inc(*lin_full[bank_of["A"][f"cb{e}"]].on(A, f"cb{e}"))

            with pe.Fori(0, N_GROUPS) as g:
                ph = Phase("M", g)
                for e in range(PER_GROUP):
                    for m in range(EB):
                        linear(ph, f"gate{e}.{m}", lambda k: h[:, k, :])
                        linear(ph, f"up{e}.{m}", lambda k: h[:, k, :])
                    for m in range(KB):
                        def hidden(k):
                            up = f"up{e}.{k}"
                            pe.wait_ge(*lin_free[bank_of["M"][up]].by(ph, up))
                        linear(ph, f"down{e}.{m}", lambda k: hid[e % 2][:, k, :], kb=EB, wait=hidden if m == 0 else None)
            mean_sum(B, "ln4", x, lambda k: pe.wait_ge(*x_new.by(B, ("ffn", k))))
            pe.wait_ge(*centred.by(B, ("ln4", 7)))
            for k in range(KB):
                square_sum(B, "ln4", k, h[:, k, :], ones_d)

            with pe.Fori(0, LAYERS) as l:
                ph = Phase("L", l)
                for k in range(KB):
                    square_sum(ph, "pre_mix", k, h[:, k, :], ones_d)
                for m in range(14):
                    linear(ph, f"qk{m}", lambda k: h[:, k, :],
                           wait=(lambda k: pe.wait_ge(*normed.by(ph, ("pre_mix", k)))) if m == 0 else None)
                for t in range(TT):
                    tokens(ph, f"va{t}", BLOCK0["L"]["va3"], lambda k: h[:, k, t * P:(t + 1) * P], 512)
                for r in range(4):
                    tokens(ph, f"vb{r}", BLOCK0["L"]["vb3"], lambda k: h[:, k, r::4], 256)
                for m in range(2):
                    linear(ph, f"km{m}", lambda k: mem[:, k, :], n=N_MEM)
                for t in range(2):
                    tokens(ph, f"vm{t}", BLOCK0["L"]["vm1"], lambda k: mem[:, k, t * P:(t + 1) * P], 256)
                pe.wait_ge(*lin_free[bank_of["L"]["vm0"]].by(ph, "vm0"))
                pe.wait_ge(*lin_free[bank_of["L"]["vm1"]].by(ph, "vm1"))

                def v_of(kind, hp, half, t, c):
                    lo = (2 * hp + half) * DH
                    if kind == "na":
                        return va[:, c, lo:lo + DH]
                    if kind == "mem":
                        return vm[:, c, lo:lo + DH]
                    if c < 4:
                        return va[:, c, D_A + lo:D_A + lo + DH]
                    return vb[:, t, (c - 4) * P + lo:(c - 4) * P + lo + DH]
                attention(ph, lambda kind: qa if kind == "na" else qm, lambda kind: ka if kind == "na" else kmT, v_of)

                for m in range(KB):
                    linear(ph, f"g0.{m}", lambda k: h[:, k, :])
                    linear(ph, f"ba{m}", lambda k: oa[:, k, :], kb=3)
                    linear(ph, f"g1.{m}", lambda k: h[:, k, :])
                    linear(ph, f"bb{m}", lambda k: obb[:, k, :], kb=1)
                    linear(ph, f"g2.{m}", lambda k: h[:, k, :])
                    linear(ph, f"bm{m}", lambda k: om[:, k, :], kb=2,
                           wait=(lambda k: pe.wait_ge(*o_out.by(ph, ("mem", 1))) if k == 0 else None) if m == 0 else None)
                for m in range(KB):
                    linear(ph, f"out{m}", lambda k: y[:, k, :],
                           wait=(lambda k: pe.wait_ge(*merged.by(ph, k))) if m == 0 else None)
                    if m >= 2:
                        square_sum(ph, "post_mix", m - 2, big[:, m - 2, :], ones_d)
                for k in range(KB - 2, KB):
                    square_sum(ph, "post_mix", k, big[:, k, :], ones_d)
                for k in range(KB):
                    square_sum(ph, "pre_ffn", k, h[:, k, :], ones_d)
                for j in range(FB):
                    linear(ph, f"a{j}", lambda k: h[:, k, :],
                           wait=(lambda k: pe.wait_ge(*normed.by(ph, ("pre_ffn", k)))) if j == 0 else None)
                    linear(ph, f"b{j}", lambda k: h[:, k, :])
                for m in range(KB):
                    linear(ph, f"down{m}", lambda k: big[:, k, :], kb=FB,
                           wait=(lambda k: pe.wait_ge(*ff_ready.by(ph, k))) if m == 0 else None)
                    if m >= 2:
                        square_sum(ph, "post_ffn", m - 2, h[:, m - 2, :], ones_d)
                for k in range(KB - 2, KB):
                    square_sum(ph, "post_ffn", k, h[:, k, :], ones_d)

        @block.scalar
        def _(act):
            def full(ph, g):
                b = bank_of[ph.name][g]
                act.wait_ge(*lin_full[b].by(ph, g))
                return lin[:, b, :], lin_free[b]

            def square(ph, st, k, src, dst):
                act.activation(dst, src, ACT.Square).then_inc(*squares.on(ph, (st, k)))

            def root(ph, st, e, n=S):
                act.wait_ge(*var_full.by(ph, st))
                act.activation(sd[:, 0:n], sums[:, 0, 0:n], ACT.Sqrt, bias=e).then_inc(*sd_ready.on(ph, st))

            def affine_of(ph, st, k, dst, g, b):
                act.wait_ge(*normed.by(ph, (st, k)))
                act.activation(dst, dst, ACT.Identity, bias=b, scale=g).then_inc(*affine.on(ph, (st, k)))

            def attention(ph, extra=None, after=None):
                name = ph.name
                tl = TILES[name]

                def exp(i):
                    kind, hp, half, t = tl[i]
                    n = key_chunks(kind, t) * P
                    p = probs[name][i % 3][:, 0:n]
                    act.wait_ge(*scored.by(ph, i))
                    src = score[:, i % 2, 0:n] if kind == "mem" else p
                    if kind == "mem" and i >= 3:
                        act.wait_ge(*t_done.by(ph, ROUNDS_OF[name][i - 3][-1]))
                    act.activation(p, src, ACT.Exp, bias=stat[:, 0, i % 4:i % 4 + 1],
                                   scale=-1.0 if kind in ("na", "dil") else 1.0,
                                   accum_out=stat[:, 1, i % 4:i % 4 + 1]).then_inc(*exp_done.on(ph, i))

                def out_of(o):
                    kind, hp = OUTS[name][o]
                    last = max(j for j, r in enumerate(ROUNDS[name]) if tl[r[0]][0:2] == (kind, hp))
                    act.wait_ge(*pv_done.by(ph, last))
                    src = attn[:, o % 2, :]
                    if kind == "dil":
                        dst = obb[:, 0, :].rearrange("p (a r) -> p r a", r=4)
                        src = src.rearrange("p (r a) -> p r a", r=4)
                    else:
                        dst = {"fa": y, "na": oa, "mem": om}[kind][:, hp, :]
                    act.copy(dst, src).then_inc(*o_out.on(ph, (kind, hp)))

                ends = {max(i for i, x in enumerate(tl) if x[0:2] == o): n for n, o in enumerate(OUTS[name])}
                for i in range(len(tl) + 4):
                    if extra:
                        extra(i)
                    if i < len(tl):
                        exp(i)
                        if after:
                            after(i)
                    if i - 4 in ends:
                        out_of(ends[i - 4])

            act.dma_start(x[:, :, :], xT_in).then_inc(x_in, 16)
            act.dma_start(vec[:, :], vec_in).then_inc(vec_in_s, 16)
            act.dma_start(consts[:, :], const_in).then_inc(consts_in, 16)
            act.dma_start(wf[:, :, :], small_in).then_inc(consts_in, 16)
            act.dma_start(wr[:, :, :], route_w_in).then_inc(consts_in, 16)
            act.dma_start(route_b[:, :], route_b_in).then_inc(consts_in, 16)
            act.dma_start(mem[:, :, :], memT_in).then_inc(mem_in, 16)
            act.dma_start(dil[:, :, :], dil_in).then_inc(dil_s, 16)

            act.wait_ge(dve_step, 6)
            act.wait_ge(vec_in_s, 16)
            act.activation(silu_c[:, :], vec[:, VEC["c"]:VEC["c"] + KB], ACT.Silu).then_inc(act_step, 1)
            act.wait_ge(*sp_step.by(A, "abs"))
            act.activation(lam[:, 2, :], lam[:, 1, :], ACT.Exp, scale=-1.0).then_inc(*sp_step.on(A, "exp"))
            act.wait_ge(*sp_step.by(A, "exp"))
            act.activation(lam[:, 3, :], lam[:, 2, :], ACT.Ln, bias=eps[:, 2:3]).then_inc(*sp_step.on(A, "ln"))
            for k in range(KB):
                act.wait_ge(*centred.by(A, ("ln1", k)))
                square(A, "ln1", k, h[:, k, :], y[:, k, :])
            root(A, "ln1", eps[:, 0:1])
            act.wait_ge(mem_in, 16)
            for k in range(KB):
                square(A, "mem", k, mem[:, k, :], mem_sq(k))
            act.wait_ge(*rstd_ready.by(A, "ln1"))
            root(A, "mem", eps[:, 1:2], N_MEM)
            act.wait_ge(*mod_ready.by(A, 0))
            for k in range(KB):
                affine_of(A, "ln1", k, h[:, k, :], mod1[:, 8 + k:9 + k], mod[:, k:k + 1])
            act.wait_ge(*f_step.by(A, "abs"))
            act.activation(fl2, fl2, ACT.Exp, scale=-1.0).then_inc(*f_step.on(A, "exp"))
            act.wait_ge(*f_step.by(A, "exp"))
            act.activation(fl2, fl2, ACT.Ln, bias=eps[0:HEADS, 2:3]).then_inc(*f_step.on(A, "ln"))
            act.wait_ge(*pad_done.by(A, 0))
            for m in range(4):
                acc, free = full(A, f"xb{m}")
                act.copy(xbp[m][:, CONV - 1:], acc).then_inc(*free.on(A, f"xb{m}"))
            for m in range(4):
                acc, free = full(A, f"gb{m}")
                act.activation(gg[:, m, :], acc, ACT.Gelu_apprx_tanh).then_inc(*free.on(A, f"gb{m}"))
            for m in range(4):
                acc, free = full(A, f"q{m}")
                act.activation(qT[:, m, :], acc, ACT.Copy, scale=DH ** -0.5).then_inc(*free.on(A, f"q{m}"))
            for n, dst in (("k", kT), ("v", v_tok)):
                for m in range(4):
                    acc, free = full(A, f"{n}{m}")
                    act.copy(dst[:, m, :], acc).then_inc(*free.on(A, f"{n}{m}"))

            for n, dst in (("r", r_), ("i", ig)):
                for m in range(4):
                    acc, free = full(A, f"{n}{m}")
                    act.activation(dst[:, m, :], acc, ACT.Sigmoid,
                                   bias=v_(f"b_{n}g", m)).then_inc(*free.on(A, f"{n}{m}"))
            act.wait_ge(*lin_free[bank_of["A"]["r3"]].by(A, "r3"))
            act.wait_ge(*lin_free[bank_of["A"]["r2"]].by(A, "r2"))
            act.wait_ge(*sp_step.by(A, "nc"))
            for m in range(4):
                act.activation(a_[:, m, :], r_[:, m, :], ACT.Exp,
                               scale=lam[:, 5, m:m + 1]).then_inc(*lru_act.on(A, ("a", m)))
            for m in range(4):
                act.wait_ge(*lru_act.by(A, ("a", m)))
                act.activation(r_[:, m, :], r_[:, m, :], ACT.Tanh,
                               scale=lam[:, 4, m:m + 1]).then_inc(*lru_act.on(A, ("th", m)))
            for m in range(4):
                act.activation(a2[:, m, :], a_[:, m, :], ACT.Square).then_inc(*lru_act.on(A, ("a2", m)))
            for m in range(4):
                act.wait_ge(*lru_dve.by(A, ("u2", m)))
                act.activation(r_[:, m, :], r_[:, m, :], ACT.Sqrt).then_inc(*lru_act.on(A, ("sqrt", m)))
            for k in range(4):
                act.wait_ge(*lru_dve.by(A, ("out", k)))
                square(A, "lru", k, xc[:, k, :], h[:, k, :])
            act.wait_ge(*rstd_ready.by(A, "mem"))
            root(A, "lru", eps[:, 1:2])

            def negcum(i):
                todo = [0, 1] if i == 0 else [i // TT + 1] if i % TT == 0 else []
                for hd in todo:
                    if hd < HEADS:
                        if hd == 0:
                            act.wait_ge(*f_step.by(A, "cum"))
                        if hd >= 2:
                            act.wait_ge(*scored.by(A, TT * (hd - 1) - 1))
                        acc, free = full(A, f"nc{hd}")
                        act.copy(gat[:, hd % 2, :], acc).then_inc(*free.on(A, f"nc{hd}"))
            attention(A, extra=negcum)
            for k in range(4):
                act.wait_ge(*o_out.by(A, ("fa", k)))
                square(A, "attn", k, y[:, k, :], h[:, k, :])
            act.wait_ge(*rstd_ready.by(A, "lru"))
            root(A, "attn", eps[:, 1:2])
            for st in ("ln2", "ln3"):
                src, sq, dst = (x, h, x) if st == "ln2" else (h, y, h)
                for k in range(KB):
                    act.wait_ge(*centred.by(A, (st, k)))
                    square(A, st, k, src[:, k, :], sq[:, k, :])
                root(A, st, eps[:, 0:1])
                if st == "ln3":
                    act.wait_ge(*mod_ready.by(A, 2))
                for k in range(KB):
                    g, b = ((v_("ln1_g", k), v_("ln1_b", k)) if st == "ln2"
                            else (mod1[:, 32 + k:33 + k], mod[:, 24 + k:25 + k]))
                    affine_of(A, st, k, dst[:, k, :], g, b)
            act.wait_ge(*route_sub.by(A, 0))
            act.activation(rtv(1), rtv(1), ACT.Exp).then_inc(*route_exp.on(A, 0))
            for e in range(EXPERTS):
                acc, free = full(A, f"cb{e}")
                act.copy(comb_bc[:, e, :], acc).then_inc(*free.on(A, f"cb{e}"))

            with act.Fori(0, N_GROUPS) as g:
                ph = Phase("M", g)
                for e, m in em:
                    i = e * EB + m
                    if i >= 2:
                        up = "up%d.%d" % em[i - 2]
                        act.wait_ge(*lin_free[bank_of["M"][up]].by(ph, up))
                    acc, free = full(ph, f"gate{e}.{m}")
                    act.activation(sil[i % 2], acc, ACT.Silu).then_inc(*free.on(ph, f"gate{e}.{m}"))
            for k in range(KB):
                act.wait_ge(*centred.by(B, ("ln4", k)))
                square(B, "ln4", k, x[:, k, :], h[:, k, :])
            root(B, "ln4", eps[:, 0:1])
            for k in range(KB):
                affine_of(B, "ln4", k, x[:, k, :], v_("ln2_g", k), v_("ln2_b", k))

            act.wait_ge(*affine.by(B, ("ln4", KB - 1)))
            with act.Fori(0, LAYERS) as l:
                ph = Phase("L", l)
                act.dma_start(lvec[:, :], lvec_in[l]).then_inc(lvec_s, 16)
                act.dma_start(nab[:, 0, :], na_bias_in[l * NA_HEADS]).then_inc(nab_s, 16)
                for k in range(KB):
                    square(ph, "pre_mix", k, x[:, k, :], h[:, k, :])
                root(ph, "pre_mix", eps[:, 1:2])
                for m in range(14):
                    acc, free = full(ph, f"qk{m}")
                    dst = ([qa[:, i, :] for i in range(3)] + [ka[:, i, :] for i in range(3)]
                           + [qb[:, i, :] for i in range(3)] + [kb[:, i, :] for i in range(3)]
                           + [qm[:, i, :] for i in range(2)])[m]
                    is_q = m < 3 or 6 <= m < 9 or m >= 12
                    act.activation(dst, acc, ACT.Copy, scale=DH ** -0.5 if is_q else 1.0).then_inc(*free.on(ph, f"qk{m}"))
                for n, dst, w in ([(f"va{t}", va[:, t, :], S) for t in range(TT)]
                                  + [(f"vb{r}", vb[:, r, :], 2 * P) for r in range(4)]
                                  + [(f"km{m}", kmT[:, m, :], N_MEM) for m in range(2)]
                                  + [(f"vm{t}", vm[:, t, :], D_M) for t in range(2)]):
                    acc, free = full(ph, n)
                    act.copy(dst, acc[:, 0:w]).then_inc(*free.on(ph, n))

                def next_bias(i):
                    hd = i // TT + 1
                    if i % TT == 0 and hd < NA_HEADS:
                        act.dma_start(nab[:, hd % 2, :], na_bias_in[l * NA_HEADS + hd]).then_inc(nab_s, 16)
                attention(ph, after=next_bias)
                for m in range(KB):
                    for i, n in enumerate(("g0.", "g1.", "g2.")):
                        j = 3 * m + i
                        if j >= 2:
                            pm, pi = divmod(j - 2, 3)
                            g = f"{('ba', 'bb', 'bm')[pi]}{pm}"
                            act.wait_ge(*lin_free[bank_of["L"][g]].by(ph, g))
                        acc, free = full(ph, f"{n}{m}")
                        act.activation(gat[:, j % 2, :], acc, ACT.Sigmoid,
                                       bias=lv("b_gate", 8 * i + m)).then_inc(*free.on(ph, f"{n}{m}"))
                for m in range(KB):
                    acc, free = full(ph, f"out{m}")
                    square(ph, "post_mix", m, acc, big[:, m, :])
                    act.copy(h[:, m, :], acc).then_inc(*free.on(ph, f"out{m}"))
                root(ph, "post_mix", eps[:, 1:2])
                for k in range(KB):
                    act.wait_ge(*x_new.by(ph, ("post_mix", k)))
                    square(ph, "pre_ffn", k, x[:, k, :], h[:, k, :])
                root(ph, "pre_ffn", eps[:, 1:2])

                def conv_mid(n, j):
                    f = j if n == "a" else FB + j
                    acc, _ = full(ph, f"{n}{j}")
                    dst = (ffa if n == "a" else ffb)[j % 2]
                    if j >= 2:
                        act.wait_ge(*ff_ready.by(ph, j - 2))
                    act.activation(dst, acc, ACT.Identity, bias=lv("conv_b", f),
                                   scale=lv("conv_w", 2 * FB + f)).then_inc(*conv_c.on(ph, (n, j)))

                def gelu(j):
                    act.wait_ge(*lin_free[bank_of["L"][f"a{j}"]].by(ph, f"a{j}"))
                    act.activation(ffg[j % 2], ffa[j % 2], ACT.Gelu_apprx_tanh).then_inc(*gelu_ready.on(ph, j))
                for j in range(FB):
                    conv_mid("a", j)
                    conv_mid("b", j)
                    gelu(j)
                for m in range(KB):
                    acc, free = full(ph, f"down{m}")
                    square(ph, "post_ffn", m, acc, h[:, m, :])
                    act.copy(y[:, m, :], acc).then_inc(*free.on(ph, f"down{m}"))
                root(ph, "post_ffn", eps[:, 1:2])
                act.wait_ge(*x_new.by(ph, ("post_ffn", KB - 1)))

        @block.vector
        def _(dve):
            steps = [0]

            def step(ins):
                steps[0] += 1
                ins.then_inc(dve_step, 1)
                dve.wait_ge(dve_step, steps[0])

            def full(ph, g):
                b = bank_of[ph.name][g]
                dve.wait_ge(*lin_full[b].by(ph, g))
                return lin[:, b, :], lin_free[b]

            def root_inverse(ph, st, n=S):
                dve.wait_ge(*sd_ready.by(ph, st))
                dve.reciprocal(rstd[:, 0:n], sd[:, 0:n]).then_inc(*rstd_ready.on(ph, st))
                dve.wait_ge(*rstd_ready.by(ph, st))

            def centre(ph, st, src, dst):
                dve.wait_ge(*mean_full.by(ph, st))
                for k in range(KB):
                    dve.tensor_tensor(dst[:, k, :], src[:, k, :], sums[:, 0, :],
                                      ALU.subtract).then_inc(*centred.on(ph, (st, k)))

            def scale_all(ph, st, buf):
                root_inverse(ph, st)
                for k in range(KB):
                    dve.tensor_tensor(buf[:, k, :], buf[:, k, :], rstd[:, :], ALU.mult).then_inc(*normed.on(ph, (st, k)))

            def rms_apply(ph, st, dst, src, g, n_k, n=S):
                root_inverse(ph, st, n)
                for k in range(n_k):
                    dve.scalar_tensor_tensor(dst(k), src(k), g(k), rstd[:, 0:n], ALU.mult,
                                             ALU.mult).then_inc(*normed.on(ph, (st, k)))

            def residual(ph, st, src, g):
                root_inverse(ph, st)
                for k in range(KB):
                    dve.scalar_tensor_tensor(tmp[:, k % 2, :], src[:, k, :], lv(g, k), rstd[:, :], ALU.mult,
                                             ALU.mult).then_inc(*upd.on(ph, (st, k)))
                    dve.wait_ge(*upd.by(ph, (st, k)))
                    dve.tensor_tensor(x[:, k, :], x[:, k, :], tmp[:, k % 2, :], ALU.add).then_inc(*x_new.on(ph, (st, k)))

            def ada(g):
                acc, free = full(A, f"ada{g}")
                lo = 16 * g
                dve.tensor_tensor(mod[:, lo:lo + 16], acc[:, 0:16],
                                  vec[:, VEC["b_ada"] + lo:VEC["b_ada"] + lo + 16], ALU.add).then_inc(*free.on(A, f"ada{g}"))
                dve.wait_ge(*free.by(A, f"ada{g}"))
                dve.tensor_scalar(mod1[:, lo:lo + 16], mod[:, lo:lo + 16], 1.0, None, ALU.add).then_inc(*mod_ready.on(A, g))

            def attention(ph, extra=None):
                name = ph.name
                tl = TILES[name]

                def inverse(i):
                    dve.wait_ge(*exp_done.by(ph, i))
                    dve.reciprocal(stat[:, 2, i % 4:i % 4 + 1], stat[:, 1, i % 4:i % 4 + 1]).then_inc(*rden_ready.on(ph, i))

                def scores(i):
                    kind, hp, half, t = tl[i]
                    nm, far = stat[:, 0, i % 4:i % 4 + 1], stat[:, 3, i % 4:i % 4 + 1]
                    n = key_chunks(kind, t) * P
                    p = probs[name][i % 3]
                    s = score[:, i % 2, :]
                    if kind == "fa":
                        hd = 2 * hp + half
                        dve.scalar_tensor_tensor(p[:, 0:n], gat[:, hd % 2, 0:n], cumq[:, t, hd:hd + 1], s[:, 0:n],
                                                 ALU.add, ALU.add).then_inc(*score_step.on(ph, (i, 0)))
                        dve.wait_ge(*score_step.by(ph, (i, 0)))
                        dve.tensor_tensor(p[:, n - P:n], p[:, n - P:n], causal, ALU.add).then_inc(*score_step.on(ph, (i, 1)))
                        dve.wait_ge(*score_step.by(ph, (i, 1)))
                        dve.tensor_reduce(nm, p[:, 0:n], AX_X, ALU.max).then_inc(*score_step.on(ph, (i, 2)))
                        dve.wait_ge(*score_step.by(ph, (i, 2)))
                        dve.tensor_scalar(nm, nm, -1.0, None, ALU.mult).then_inc(*scored.on(ph, i))
                    elif kind == "na":
                        hd = 2 * hp + half
                        lo = (2 * TT - 2 - 2 * t) * GRID_W
                        dve.tensor_tensor_reduce(p[:, 0:n], s, nab[:, hd % 2, lo:lo + S], -1.0, BIG, ALU.add, ALU.min,
                                                 nm).then_inc(*scored.on(ph, i))
                    elif kind == "dil":
                        dve.tensor_tensor_reduce(p[:, 0:S], score_flat[:, 0:S], dil[:, half, 3 - t:3 - t + S], -1.0, BIG,
                                                 ALU.add, ALU.min, nm).then_inc(*score_step.on(ph, (i, 0)))
                        dve.tensor_tensor_reduce(p[:, S:n], score_flat[:, S:n], dil[:, half, S + 3:], -1.0, BIG,
                                                 ALU.add, ALU.min, far).then_inc(*score_step.on(ph, (i, 1)))
                        dve.wait_ge(*score_step.by(ph, (i, 1)))
                        dve.tensor_tensor(nm, nm, far, ALU.min).then_inc(*scored.on(ph, i))
                    else:
                        dve.tensor_reduce(nm, s[:, 0:n], AX_X, ALU.max).then_inc(*score_step.on(ph, (i, 0)))
                        dve.wait_ge(*score_step.by(ph, (i, 0)))
                        dve.tensor_scalar(nm, nm, -1.0, None, ALU.mult).then_inc(*scored.on(ph, i))

                def gather(j):
                    i, c0, n = ROUNDS[name][j]
                    dve.wait_ge(*t_done.by(ph, j))
                    if j >= 2:
                        dve.wait_ge(*pv_done.by(ph, j - 2))
                    dve.tensor_copy(probsT[name][j % 2][:, 0:n * P], trans[:, 0, 0:n * P]).then_inc(*pt_ready.on(ph, j))

                n = len(tl)
                for i in range(n + 2):
                    if i < n:
                        kind = tl[i][0]
                        dve.wait_ge(*qk_done.by(ph, i))
                        if kind == "na" and i % TT == 0:
                            dve.wait_ge(*nab_ready.by(ph, i // TT))
                        if kind == "fa" and i % TT == 0:
                            hd = i // TT
                            dve.wait_ge(*lin_free[bank_of["A"][f"nc{hd}"]].by(A, f"nc{hd}"))
                        if i >= 3 and kind != "mem":
                            dve.wait_ge(*t_done.by(ph, ROUNDS_OF[name][i - 3][-1]))
                    if 1 <= i <= n:
                        inverse(i - 1)
                    elif name == "L" and i == 0:
                        dve.memset(stat[:, 3, :], BIG)
                    if i < n:
                        scores(i)
                    if i >= 2:
                        for j in ROUNDS_OF[name][i - 2]:
                            gather(j)

            for dst, val in ((ones_d[:, :], 1.0 / D), (ones_h[:, :], 1.0 / D_ATTN), (eps[:, 0:1], LN_EPS),
                             (eps[:, 1:2], RMS_EPS), (eps[:, 2:3], 1.0), (one_row, 1.0)):
                step(dve.memset(dst, val))

            dve.wait_ge(vec_in_s, 16)
            lamv = vec[:, VEC["lam"]:VEC["lam"] + 4]
            dve.tensor_scalar(lam[:, 0, :], lamv, -1.0, None, ALU.mult).then_inc(*sp_step.on(A, "neg"))
            dve.wait_ge(*sp_step.by(A, "neg"))
            dve.tensor_tensor(lam[:, 1, :], lamv, lam[:, 0, :], ALU.max).then_inc(*sp_step.on(A, "abs"))
            dve.wait_ge(x_in, 16)
            centre(A, "ln1", x, h)
            scale_all(A, "ln1", h)
            dve.wait_ge(*sp_step.by(A, "ln"))
            dve.scalar_tensor_tensor(lam[:, 3, :], lam[:, 0, :], 0.0, lam[:, 3, :], ALU.max,
                                     ALU.add).then_inc(*sp_step.on(A, "sp"))
            dve.wait_ge(*sp_step.by(A, "sp"))
            dve.tensor_scalar(lam[:, 4, :], lam[:, 3, :], LRU_C, None, ALU.mult).then_inc(*sp_step.on(A, "c"))
            dve.tensor_scalar(lam[:, 5, :], lam[:, 3, :], -LRU_C, None, ALU.mult).then_inc(*sp_step.on(A, "nc"))
            rms_apply(A, "mem", lambda k: mem[:, k, :], lambda k: mem[:, k, :], lambda k: v_("mem_g", k), KB, N_MEM)
            ada(0)
            for m in range(4):
                ins = dve.memset(xbp[m][:, 0:CONV - 1], 0.0)
                if m < 3:
                    step(ins)
            ins.then_inc(*pad_done.on(A, 0))
            acc, free = full(A, "f")
            dve.tensor_scalar(fl, acc[0:HEADS, :], v_("b_f")[0:HEADS, :], None, ALU.add).then_inc(*free.on(A, "f"))
            dve.wait_ge(*free.by(A, "f"))
            step(dve.tensor_scalar(fl2, fl, -1.0, None, ALU.mult))
            dve.tensor_tensor(fl2, fl2, fl, ALU.max).then_inc(*f_step.on(A, "abs"))
            dve.wait_ge(*f_step.by(A, "ln"))
            dve.scalar_tensor_tensor(fl2, fl, 0.0, fl2, ALU.min, ALU.subtract).then_inc(*f_step.on(A, "ls"))
            dve.wait_ge(*f_step.by(A, "ls"))
            dve.tensor_tensor_scan(fl, one_row, fl2, 0.0, ALU.mult, ALU.add).then_inc(*f_step.on(A, "cum"))
            dve.wait_ge(*f_step.by(A, "cum"))
            dve.tensor_scalar(ncum, fl, -1.0, None, ALU.mult).then_inc(*f_step.on(A, "neg"))
            for m in range(4):
                b = bank_of["A"][f"xb{m}"]
                dve.wait_ge(*lin_free[b].by(A, f"xb{m}"))
                dve.tensor_scalar(xc[:, m, :], xbp[m][:, 0:S], v_("conv_w", m), v_("conv_b", m), ALU.mult,
                                  ALU.add).then_inc(*conv.on(A, (m, 0)))
                for j in range(1, CONV):
                    dve.wait_ge(*conv.by(A, (m, j - 1)))
                    dve.scalar_tensor_tensor(xc[:, m, :], xbp[m][:, j:j + S], v_("conv_w", 4 * j + m), xc[:, m, :],
                                             ALU.mult, ALU.add).then_inc(*conv.on(A, (m, j)))
            for m in range(4):
                dve.wait_ge(*lru_act.by(A, ("a2", m)))
                dve.scalar_tensor_tensor(r_[:, m, :], a2[:, m, :], 1.0, r_[:, m, :], ALU.add,
                                         ALU.mult).then_inc(*lru_dve.on(A, ("u2", m)))
            for m in range(4):
                dve.tensor_tensor(ig[:, m, :], ig[:, m, :], xc[:, m, :], ALU.mult).then_inc(*lru_dve.on(A, ("igx", m)))
            for m in range(4):
                dve.wait_ge(*lru_dve.by(A, ("igx", m)))
                dve.wait_ge(*lru_act.by(A, ("sqrt", m)))
                dve.tensor_tensor(ig[:, m, :], ig[:, m, :], r_[:, m, :], ALU.mult).then_inc(*lru_dve.on(A, ("u", m)))
            for m in range(4):
                dve.wait_ge(*lru_dve.by(A, ("u", m)))
                dve.tensor_tensor_scan(a2[:, m, :], a_[:, m, :], ig[:, m, :], 0.0, ALU.mult,
                                       ALU.add).then_inc(*lru_dve.on(A, ("scan", m)))
            for m in range(4):
                dve.wait_ge(*lru_dve.by(A, ("scan", m)))
                dve.tensor_tensor(xc[:, m, :], a2[:, m, :], gg[:, m, :], ALU.mult).then_inc(*lru_dve.on(A, ("out", m)))
            ada(1)
            ada(2)
            rms_apply(A, "lru", lambda k: xc[:, k, :], lambda k: xc[:, k, :], lambda k: v_("g_lru", k), 4)
            acc, free = full(A, "cumT")
            dve.tensor_copy(cumq[:, :, :].rearrange("p a b -> p (a b)"), acc[:, 0:TT * HEADS]).then_inc(*free.on(A, "cumT"))
            dve.wait_ge(*free.by(A, "cumT"))
            attention(A)
            rms_apply(A, "attn", lambda k: y[:, k, :], lambda k: y[:, k, :], lambda k: v_("g_attn", k), 4)
            for m in range(KB):
                acc, free = full(A, f"out{m}")
                dve.tensor_scalar(tmp[:, m % 2, :], acc, mod1[:, 16 + m:17 + m], None, ALU.mult).then_inc(*free.on(A, f"out{m}"))
                dve.wait_ge(*free.by(A, f"out{m}"))
                dve.scalar_tensor_tensor(x[:, m, :], x[:, m, :], ALPHA, tmp[:, m % 2, :], ALU.mult,
                                         ALU.add).then_inc(*x_new.on(A, ("mix", m)))
            dve.wait_ge(*x_new.by(A, ("mix", KB - 1)))
            centre(A, "ln2", x, x)
            scale_all(A, "ln2", x)
            centre(A, "ln3", x, h)
            scale_all(A, "ln3", h)
            step(dve.memset(y[:, :, :], 0.0))
            for half in range(2):
                acc, free = full(A, f"rt{half}")
                dve.tensor_tensor(rtv(0)[:, half * 40:half * 40 + 40], acc[:, 0:40],
                                  route_b[:, half * 40:half * 40 + 40], ALU.add).then_inc(*free.on(A, f"rt{half}"))
            for half in range(2):
                dve.wait_ge(*lin_free[bank_of["A"][f"rt{half}"]].by(A, f"rt{half}"))

            def q4(i):
                return rtv(i).rearrange("p (a b) -> p a b", b=4)

            def col(i, n=20):
                return rtv(i)[:, 0:n]

            def spread(ap, n=20, w=4):
                return ap.unsqueeze(2).to_broadcast([P, n, w])
            step(dve.tensor_reduce(col(2), q4(0), AX_X, ALU.max))
            dve.tensor_tensor(q4(1), q4(0), spread(col(2)), ALU.subtract).then_inc(*route_sub.on(A, 0))
            dve.wait_ge(*route_exp.by(A, 0))
            step(dve.tensor_reduce(col(2), q4(1), AX_X, ALU.add))
            step(dve.reciprocal(col(3), col(2)))
            step(dve.tensor_tensor(q4(4), q4(1), spread(col(3)), ALU.mult))
            step(dve.memset(rtv(5), 0.0))
            for i in range(4):
                for lo, hi, op in ((0, i, ALU.is_gt), (i + 1, 4, ALU.is_ge)):
                    if hi > lo:
                        w = hi - lo
                        step(dve.tensor_tensor(q4(6)[:, :, 0:w], q4(4)[:, :, i:i + 1].to_broadcast([P, 20, w]),
                                               q4(4)[:, :, lo:hi], op))
                        step(dve.tensor_tensor(q4(5)[:, :, lo:hi], q4(5)[:, :, lo:hi], q4(6)[:, :, 0:w], ALU.add))
            step(dve.tensor_scalar(rtv(7), rtv(5), 0.5, None, ALU.is_lt))
            step(dve.tensor_tensor(rtv(7), rtv(7), rtv(4), ALU.mult))
            step(dve.tensor_scalar(rtv(8), rtv(5), 1.5, None, ALU.is_lt))
            step(dve.tensor_tensor(rtv(8), rtv(8), rtv(4), ALU.mult))
            step(dve.tensor_reduce(col(2), q4(8), AX_X, ALU.add))
            step(dve.reciprocal(col(3), col(2)))
            step(dve.tensor_tensor(q4(9), q4(8), spread(col(3)), ALU.mult))

            def by_token(i):
                return rtv(i).rearrange("p (t g j) -> p t g j", t=TT, j=4)
            for t in range(TT):
                ins = dve.tensor_tensor(comb_tile(t).rearrange("p (g j) -> p g j", j=4), by_token(9)[:, t, 1:5, :],
                                        by_token(7)[:, t, 0, :].unsqueeze(2).to_broadcast([P, 4, 4]), ALU.mult)
                if t < TT - 1:
                    step(ins)
            ins.then_inc(*comb_ready.on(A, 0))
            acc, free = full(A, "cbT")
            dve.tensor_copy(combT, acc[0:EXPERTS, :]).then_inc(*free.on(A, "cbT"))

            for b in range(2):
                g = f"cb{EXPERTS - 2 + b}"
                dve.wait_ge(*lin_free[bank_of["A"][g]].by(A, g))
            with dve.Fori(0, N_GROUPS) as g:
                ph = Phase("M", g)
                for e in range(PER_GROUP):
                    for m in range(EB):
                        i = e * EB + m
                        n = f"gate{e}.{m}"
                        dve.wait_ge(*lin_free[bank_of["M"][n]].by(ph, n))
                        dve.tensor_tensor(sil[i % 2], sil[i % 2], comb_bc[:, g * PER_GROUP + e, :],
                                          ALU.mult).then_inc(*silu_ready.on(ph, (e, m)))
                        acc, free = full(ph, f"up{e}.{m}")
                        dve.wait_ge(*silu_ready.by(ph, (e, m)))
                        dve.tensor_tensor(hid[e % 2][:, m, :], sil[i % 2], acc, ALU.mult).then_inc(*free.on(ph, f"up{e}.{m}"))
                    for m in range(KB):
                        acc, free = full(ph, f"down{e}.{m}")
                        dve.tensor_tensor(y[:, m, :], y[:, m, :], acc, ALU.add).then_inc(*free.on(ph, f"down{e}.{m}"))
            for m in range(KB):
                step(dve.tensor_scalar(y[:, m, :], y[:, m, :], mod1[:, 40 + m:41 + m], None, ALU.mult))
                dve.scalar_tensor_tensor(x[:, m, :], x[:, m, :], ALPHA, y[:, m, :], ALU.mult,
                                         ALU.add).then_inc(*x_new.on(B, ("ffn", m)))
            dve.wait_ge(*x_new.by(B, ("ffn", KB - 1)))
            centre(B, "ln4", x, x)
            scale_all(B, "ln4", x)
            dve.wait_ge(dil_s, 16)

            with dve.Fori(0, LAYERS) as l:
                ph = Phase("L", l)
                dve.wait_ge(lvec_s, l * 16 + 16)
                rms_apply(ph, "pre_mix", lambda k: h[:, k, :], lambda k: x[:, k, :], lambda k: lv("g_pre_mix", k), KB)
                attention(ph)
                for m in range(KB):
                    for i, n in enumerate(("ba", "bb", "bm")):
                        j = 3 * m + i
                        gn = f"g{i}.{m}"
                        dve.wait_ge(*lin_free[bank_of["L"][gn]].by(ph, gn))
                        acc, free = full(ph, f"{n}{m}")
                        dst = y[:, m, :] if i == 0 else tmp[:, i - 1, :]
                        dve.tensor_tensor(dst, acc, gat[:, j % 2, :], ALU.mult).then_inc(*free.on(ph, f"{n}{m}"))
                        dve.wait_ge(*free.by(ph, f"{n}{m}"))
                        if i == 1:
                            dve.tensor_tensor(y[:, m, :], y[:, m, :], tmp[:, 0, :], ALU.add).then_inc(*merge_step.on(ph, m))
                    dve.wait_ge(*merge_step.by(ph, m))
                    dve.tensor_tensor(y[:, m, :], y[:, m, :], tmp[:, 1, :], ALU.add).then_inc(*merged.on(ph, m))
                residual(ph, "post_mix", h, "g_post_mix")
                rms_apply(ph, "pre_ffn", lambda k: h[:, k, :], lambda k: x[:, k, :], lambda k: lv("g_pre_ffn", k), KB)
                for j in range(FB):
                    for n, buf in (("a", ffa), ("b", ffb)):
                        f = j if n == "a" else FB + j
                        acc, free = full(ph, f"{n}{j}")
                        dve.wait_ge(*conv_c.by(ph, (n, j)))
                        t = buf[j % 2]
                        dve.scalar_tensor_tensor(t[:, 1:S], acc[:, 0:S - 1], lv("conv_w", f), t[:, 1:S], ALU.mult,
                                                 ALU.add).then_inc(*conv_l.on(ph, (n, j)))
                        dve.wait_ge(*conv_l.by(ph, (n, j)))
                        dve.scalar_tensor_tensor(t[:, 0:S - 1], acc[:, 1:S], lv("conv_w", 4 * FB + f), t[:, 0:S - 1],
                                                 ALU.mult, ALU.add).then_inc(*free.on(ph, f"{n}{j}"))
                    dve.wait_ge(*gelu_ready.by(ph, j))
                    dve.wait_ge(*lin_free[bank_of["L"][f"b{j}"]].by(ph, f"b{j}"))
                    dve.tensor_tensor(big[:, j, :], ffg[j % 2], ffb[j % 2], ALU.mult).then_inc(*ff_ready.on(ph, j))
                residual(ph, "post_ffn", y, "g_post_ffn")

        @block.gpsimd
        def _(pool):
            def attention(ph, extra=None):
                for i, (kind, hp, half, t) in enumerate(TILES[ph.name]):
                    if extra:
                        extra(i)
                    n = key_chunks(kind, t) * P
                    p = probs[ph.name][i % 3][:, 0:n]
                    pool.wait_ge(*rden_ready.by(ph, i))
                    pool.tensor_tensor(p, p, stat[:, 2, i % 4:i % 4 + 1].to_broadcast([P, n]),
                                       ALU.mult).then_inc(*p_ready.on(ph, i))

            attention(A)
            pool.wait_ge(consts_in, 16 * 4)
            with pool.Fori(0, LAYERS) as l:
                ph = Phase("L", l)

                def bias(hd):
                    b = nab[:, hd % 2, :].rearrange("p (a b) -> p a b", b=GRID_W)
                    pool.wait_ge(nab_s, l * (16 * NA_HEADS) + 16 * (hd + 1))
                    pool.tensor_tensor(b, b, window.unsqueeze(1).to_broadcast([P, NA_SLOTS, GRID_W]),
                                       ALU.add).then_inc(*nab_ready.on(ph, hd))

                def next_bias(i):
                    if i == 0:
                        bias(0)
                    if i % TT == 2 and i // TT + 1 < NA_HEADS:
                        bias(i // TT + 1)
                attention(ph, extra=next_bias)

            done = Phase("L", None)
            pool.wait_ge(x_new.sem, x_new.count(done, LAYERS * len(x_new.events["L"])))
            pool.dma_start(out, x[:, :, :]).then_inc(out_done, 16)
            pool.wait_ge(out_done, 16)

        for s in signals:
            s.done()


def stationary(w):
    k, m = w.shape
    return w.reshape(k // P, P, m // P, P).transpose(2, 0, 1, 3).reshape(-1, P, P)


def moving(w):
    k, m = w.shape
    return w.reshape(k // P, P, m // P, P).transpose(0, 2, 1, 3).reshape(-1, P, P)


def by_feature(v):
    return np.ascontiguousarray(v.reshape(-1, P).T)


def weight_stream(i):
    w = i["w_in"][0]
    ada = i["w_ada"][0]
    ends = np.cumsum([D_ATTN, D_ATTN, D_ATTN, HEADS, D_ATTN, D_ATTN])
    q, k, v, _, xb, gb = np.split(w, ends[:-1], axis=1)

    def diagonal(g):
        out = np.zeros((4, P, P), np.float32)
        out[:, :DH, :DH], out[:, DH:, DH:] = g[0::2], g[1::2]
        return out
    parts = [stationary(ada[:, :2048])] + [stationary(x) for x in (xb, gb, q, k)] + [moving(v)]
    parts += [diagonal(i["w_rg"][0]), diagonal(i["w_ig"][0]), np.zeros((8, P, P), np.float32)]
    parts += [stationary(ada[:, 2048:]), stationary(i["w_out"][0])]
    for e in range(EXPERTS):
        g, u = (stationary(i[n][0, e]).reshape(EB, KB, P, P) for n in ("w_e_gate", "w_e_up"))
        parts += [np.stack([g, u], 1).reshape(-1, P, P), stationary(i["w_e_down"][0, e])]
    for l in range(LAYERS):
        w = i["w_in_2"][l]
        ends = np.cumsum([D_A] * 3 + [D_B] * 3 + [D_M] + [D] * 3)
        q_a, k_a, v_a, q_b, k_b, v_b, q_m, g0, g1, g2 = np.split(w, ends[:-1], axis=1)
        parts += [stationary(x) for x in (q_a, k_a, q_b, k_b, q_m)]
        parts += [moving(np.concatenate([v_a, v_b[:, :P]], axis=1)), moving(v_b[:, P:])]
        parts += [stationary(i["w_mem_kv_2"][l][:, :D_M]), moving(i["w_mem_kv_2"][l][:, D_M:])]
        cols = [stationary(x).reshape(KB, -1, P, P) for x in
                (g0, i["w_br_a_2"][l], g1, i["w_br_b_2"][l], g2, i["w_br_m_2"][l])]
        parts += [np.concatenate(cols, axis=1).reshape(-1, P, P), stationary(i["w_out_2"][l])]
        a, b = (stationary(x).reshape(FB, KB, P, P) for x in np.split(i["w_up_2"][l], 2, axis=1))
        parts += [np.stack([a, b], 1).reshape(-1, P, P), stationary(i["w_down_2"][l])]
    blocks = np.concatenate(parts, axis=0)
    assert blocks.shape[0] == N_CHUNKS * PER_CHUNK, (blocks.shape, N_CHUNKS)
    return np.ascontiguousarray(blocks.reshape(N_CHUNKS, PER_CHUNK, P, P).transpose(0, 2, 1, 3)).reshape(
        N_CHUNKS, P, PER_CHUNK * P)


def window_mask():
    c = np.arange(GRID_W)
    start = np.clip(c - NA_KW // 2, 0, GRID_W - NA_KW)
    inside = (c[None, :] >= start[:, None]) & (c[None, :] < start[:, None] + NA_KW)
    return np.where(inside, 0.0, MASKED).astype(np.float32)


def dilated_bias():
    out = np.full((P, 2, DIL_W), MASKED, np.float32)
    slopes = (2.0 ** (-8.0 * np.arange(1, DIL_HEADS + 1, dtype=np.float32) / DIL_HEADS)).astype(np.float32)
    a = np.arange(P)[:, None]
    for b in range(2):
        for g, (w, d) in enumerate(((128, 1), (512, 4), (2048, 16))):
            dist = np.arange(S + 3)[None, :] - 3 - 4 * a if g == 0 else 4 * (np.arange(P)[None, :] - a)
            ok = (np.abs(dist) <= w // 2) & (dist % d == 0)
            bias = np.where(ok, -slopes[2 * g + b] * np.abs(dist).astype(np.float32), MASKED)
            lo = 0 if g == 0 else S + 3 + (g - 1) * P
            out[:, b, lo:lo + bias.shape[1]] = bias
    return out


def neighborhood_bias(rpb):
    c = np.arange(GRID_W)
    reach = 2 * NA_KW - 1
    pad = np.zeros((*rpb.shape[:3], 2 * GRID_W - 1), np.float32)
    lo = GRID_W - 1 - (NA_KW - 1)
    pad[..., lo:lo + reach] = rpb
    full = pad[..., GRID_W - 1 + c[None, :] - c[:, None]]
    full = full.transpose(0, 1, 3, 2, 4)
    both = np.concatenate([full[:, :, :, 1:], full[:, :, :, :-1]], axis=2)
    return np.ascontiguousarray(both).reshape(-1, P, NA_SLOTS * GRID_W)


def kernel(**inputs):
    import concourse.bacc as bacc
    from concourse.bass_utils import run_bass_kernel_spmd

    i = {n: np.asarray(a) for n, a in inputs.items()}

    def blocks(a):
        return np.ascontiguousarray(a.reshape(-1, P, a.shape[1]).transpose(1, 0, 2))
    vec = np.zeros((P, N_VEC), np.float32)
    for n, a in (("c", i["c"][0]), ("b_ada", i["b_ada"][0]), ("conv_w", i["conv_w"][0].reshape(-1)),
                 ("conv_b", i["conv_b"][0]), ("b_rg", i["b_rg"][0]), ("b_ig", i["b_ig"][0]),
                 ("lam", i["lru_lambda"][0]), ("g_attn", i["g_attn"][0]), ("g_lru", i["g_lru"][0]),
                 ("ln1_g", i["ln1_g"][0]), ("ln1_b", i["ln1_b"][0]), ("ln2_g", i["ln2_g"][0]),
                 ("ln2_b", i["ln2_b"][0]), ("mem_g", i["mem_norm_g_2"])):
        b = by_feature(a)
        vec[:, VEC[n]:VEC[n] + b.shape[1]] = b
    vec[:HEADS, VEC["b_f"]] = i["b_f"][0]
    lvec = np.zeros((LAYERS, P, N_LVEC), np.float32)
    for l in range(LAYERS):
        for n, a in (("g_pre_mix", i["g_pre_mix_2"]), ("b_gate", i["b_gate_2"]), ("g_post_mix", i["g_post_mix_2"]),
                     ("g_pre_ffn", i["g_pre_ffn_2"]), ("conv_w", i["conv_w_2"]), ("conv_b", i["conv_b_2"]),
                     ("g_post_ffn", i["g_post_ffn_2"])):
            b = by_feature(a[l].reshape(-1))
            lvec[l, :, LVEC[n]:LVEC[n] + b.shape[1]] = b
    q = np.arange(P)
    const = np.concatenate([np.eye(P, dtype=np.float32),
                            np.where(q[None, :] <= q[:, None], 0.0, MASKED).astype(np.float32),
                            np.concatenate([window_mask()] * 2, axis=0)], axis=1)
    route_w = np.concatenate([i["w_grp"][0], i["w_exp"][0]], axis=1)
    route_b = np.concatenate([i["b_grp"][0], i["b_exp"][0]])
    f0 = 3 * D_ATTN
    arrays = {
        "weights": weight_stream(i),
        "xT": blocks(i["x"][0].T),
        "memT": blocks(i["mem_2"][0].T),
        "vec": vec,
        "lvec": lvec,
        "w_forget": blocks(i["w_in"][0][:, f0:f0 + HEADS]),
        "w_route": blocks(route_w),
        "b_route": np.ascontiguousarray(np.tile(route_b, (P, TT))),
        "na_bias": neighborhood_bias(i["rpb_na_2"]),
        "const": const,
        "dil_bias": dilated_bias(),
    }
    nc = bacc.Bacc("TRN2", target_bir_lowering=False, num_devices=1)
    args = [nc.dram_tensor(f"in_{n}", a.shape, F32, kind="ExternalInput").ap() for n, a in arrays.items()]
    out = nc.dram_tensor("outT", (P, KB, S), F32, kind="ExternalOutput").ap()
    build(nc, *args, out)
    r = run_bass_kernel_spmd(nc, [{f"in_{n}": a for n, a in arrays.items()}], core_ids=[0])
    got = r.results[0]["outT"]
    return np.ascontiguousarray(got.transpose(2, 1, 0)).reshape(1, S, D)
```

```python
from contextlib import ExitStack

import numpy as np
import concourse.bass as bass
from concourse import mybir

F32 = mybir.dt.float32
F32R = mybir.dt.float32r
U32 = mybir.dt.uint32
ALU = mybir.AluOpType
ACT = mybir.ActivationFunctionType
AX_X = mybir.AxisListType.X

P = 128
S = 512
D = 1024
KB = D // P
TT = S // P
DH = 64
D_ATTN = 512
HEADS = 8
CONV = 4
N_GROUPS, PER_GROUP = 4, 4
EXPERTS = N_GROUPS * PER_GROUP
D_EXPERT = 512
EB = D_EXPERT // P
ALPHA = 2.0 ** 0.25
LN_EPS, RMS_EPS = 1e-5, 1e-6
LRU_C = 8.0
LAYERS = 2
GRID_W = 64
ROWS = S // GRID_W
NA_HEADS, NA_KH, NA_KW = 6, 8, 16
DIL_HEADS, DIL_G = 6, 3
MEM_HEADS, N_MEM = 4, 256
D_A, D_B, D_M = 384, 384, 256
D_FF = 2816
FB = D_FF // P
MASKED = -1e30
BIG = 3.0e38

RING = 6
PER_CHUNK = 16
TILE_GROUPS = [("gate", ""), ("up", ""), ("xt", ".0"), ("down", ".0"), ("xt", ".1"), ("down", ".1")]
TILES_PER_TRIP = 4
TILE_CHUNKS = 3 * EB * KB // PER_CHUNK
MAX_SPILL = (2 * S - 1) // P
MAX_TRIPS = (MAX_SPILL + 1) // 2
SLOT_TILES = EXPERTS + 2 * MAX_TRIPS + 2
STREAM = {
    "A": [(("ada", 0, k), PER_CHUNK) for k in range(KB)]
    + [(f"{n}{m}", KB) for n in ("xb", "gb") for m in range(4)]
    + [x for i, (n, m) in enumerate((n, m) for n in ("q", "k") for m in (0, 2)) for x in
       [(f"{n}{m}", KB), (f"{n}{m + 1}", KB)] + [(("ada", 1 + i // 2, 4 * (i % 2) + k), PER_CHUNK) for k in range(4)]]
    + [("v3", 4 * KB)]
    + [(f"{n}{m}", 1) for n in ("r", "i") for m in range(4)] + [("i3", 8)]
    + [(f"out{m}", KB) for m in range(KB)],
    "M": [x for e in range(TILES_PER_TRIP)
          for x in ((f"gate{e}", EB * KB), (f"up{e}", EB * KB), (f"down{e}.1", EB * KB))],
    "L": [(f"qk{m}", KB) for m in range(14)] + [("va3", 4 * KB), ("vb3", 2 * KB)]
    + [(f"km{m}", KB) for m in range(2)] + [("vm1", 2 * KB)]
    + [x for m in range(KB) for x in ((f"g0.{m}", KB), (f"ba{m}", 3), (f"g1.{m}", KB), (f"bb{m}", 1),
                                      (f"g2.{m}", KB), (f"bm{m}", 2))]
    + [(f"out{m}", KB) for m in range(KB)]
    + [(f"{n}{j}", KB) for j in range(FB) for n in ("a", "b")]
    + [(f"down{m}", FB) for m in range(KB)],
}
LIN = {
    "A": ["ada0", "f"] + [f"{n}{m}" for n in ("xb", "gb", "q", "k", "v") for m in range(4)]
    + ["ada1", "ada2"] + [f"{n}{m}" for n in ("r", "i") for m in range(4)] + ["cumT"]
    + [f"nc{h}" for h in range(HEADS)] + [f"out{m}" for m in range(KB)] + ["rt0", "rt1", "pos"]
    + [f"ut{t}.{i}" for t in range(TT) for i in range(2)] + ["xt.0", "xt.1"],
    "M": [f"{n}{e}{i}" for e in range(TILES_PER_TRIP) for n, i in TILE_GROUPS],
    "O": [f"{n}{e}{i}" for e in range(2) for n, i in TILE_GROUPS],
    "B": [f"yt{m}" for m in range(KB)],
    "L": [f"qk{m}" for m in range(14)] + [f"va{t}" for t in range(TT)] + [f"vb{r}" for r in range(4)]
    + ["km0", "km1", "vm0", "vm1"]
    + [f"{n}{m}" for m in range(KB) for n in ("g0.", "ba", "g1.", "bb", "g2.", "bm")]
    + [f"out{m}" for m in range(KB)] + [f"{n}{j}" for j in range(FB) for n in ("a", "b")]
    + [f"down{m}" for m in range(KB)],
}
M_TRIPS = EXPERTS // TILES_PER_TRIP
TRIPS = {"A": 1, "M": M_TRIPS, "O": 0, "B": 1, "L": LAYERS}
ORDER = ["A", "M", "O", "B", "L"]
LAST_USE = {ph: [n for n, k in s for _ in range(k)] for ph, s in STREAM.items()}
CHUNKS = {ph: len(b) // PER_CHUNK for ph, b in LAST_USE.items()}
FIRST_CHUNK = {"A": 0, "M": CHUNKS["A"], "L": CHUNKS["A"] + M_TRIPS * CHUNKS["M"]}
L_RAW = 4
L_HIGH = RING - L_RAW
assert CHUNKS["L"] % L_RAW == 0 and CHUNKS["L"] % L_HIGH == 0
WHOLE = [c for c in range(CHUNKS["L"]) if LAST_USE["L"][c * PER_CHUNK][:2] in ("km", "vm")]
SPLIT = [c for c in range(CHUNKS["L"]) if c not in WHOLE]
MID = [c for c in range(CHUNKS["L"] - 1) if LAST_USE["L"][(c + 1) * PER_CHUNK - 1] == LAST_USE["L"][(c + 1) * PER_CHUNK]
       and LAST_USE["L"][c * PER_CHUNK][:4] == "down"]
N_CHUNKS = FIRST_CHUNK["L"] + LAYERS * CHUNKS["L"]
BLOCK0 = {}
for _ph, _s in STREAM.items():
    _n = 0
    BLOCK0[_ph] = {}
    for _name, _k in _s:
        BLOCK0[_ph].setdefault(_name, _n)
        _n += _k
BLOCK0["A"]["v0"] = BLOCK0["A"]["v3"]
BLOCK0["O"] = BLOCK0["M"]
BLOCK0["L"]["va0"], BLOCK0["L"]["vb0"], BLOCK0["L"]["vm0"] = (BLOCK0["L"][n] for n in ("va3", "vb3", "vm1"))

TILES = {
    "A": [("fa", h // 2, h % 2, t) for h in range(HEADS) for t in range(TT)],
    "L": [("na", h // 2, h % 2, t) for h in range(NA_HEADS) for t in range(TT)]
    + [("dil", 0, b, r) for b in range(2) for r in range(4)]
    + [("mem", h // 2, h % 2, t) for h in range(MEM_HEADS) for t in range(TT)],
}


def key_chunks(kind, t):
    return {"fa": t + 1, "na": 4, "dil": 6, "mem": 2}[kind]


ROUNDS = {ph: [(i, c, min(4, key_chunks(x[0], x[3]) - c)) for i, x in enumerate(tl)
               for c in range(0, key_chunks(x[0], x[3]), 4)] for ph, tl in TILES.items()}
ROUNDS_OF = {ph: [[j for j, x in enumerate(rs) if x[0] == i] for i in range(len(TILES[ph]))]
             for ph, rs in ROUNDS.items()}
OUTS = {ph: list(dict.fromkeys((x[0], x[1]) for x in tl)) for ph, tl in TILES.items()}

VEC = {}
_at = 0
for _n, _w in (("c", 8), ("b_ada", 48), ("b_f", 1), ("conv_w", 16), ("conv_b", 4), ("b_rg", 4), ("b_ig", 4),
               ("lam", 4), ("g_attn", 4), ("g_lru", 4), ("ln1_g", 8), ("ln1_b", 8), ("ln2_g", 8), ("ln2_b", 8),
               ("mem_g", 8)):
    VEC[_n] = _at
    _at += _w
N_VEC = _at
LVEC = {}
_at = 0
for _n, _w in (("g_pre_mix", 8), ("b_gate", 24), ("g_post_mix", 8), ("g_pre_ffn", 8), ("conv_w", 3 * 2 * FB),
               ("conv_b", 2 * FB), ("g_post_ffn", 8)):
    LVEC[_n] = _at
    _at += _w
N_LVEC = _at

NA_SLOTS = 2 * ROWS - 2
DIL_W = S + 3 + 2 * P


class Phase:

    def __init__(self, name, reg=None):
        self.name, self.reg = name, reg


class Signal:

    def __init__(self, sem, events, unit=1):
        self.sem, self.unit = sem, unit
        self.events = {ph: list(events.get(ph, [])) for ph in ORDER}
        self.index = {ph: {e: i for i, e in enumerate(v)} for ph, v in self.events.items()}
        self.seen = {ph: set() for ph in ORDER}

    def count(self, ph, n):
        base = 0
        for q in ORDER:
            if q == ph.name:
                break
            base += TRIPS[q] * len(self.events[q])
        c = (base + n) * self.unit
        return c if ph.reg is None else ph.reg * (len(self.events[ph.name]) * self.unit) + c

    def by(self, ph, event):
        return self.sem, self.count(ph, self.index[ph.name][event] + 1)

    def before(self, ph, event):
        return self.sem, self.count(ph, self.index[ph.name][event])

    def on(self, ph, event):
        assert event in self.index[ph.name] and event not in self.seen[ph.name], event
        self.seen[ph.name].add(event)
        return self.sem, self.unit

    def done(self):
        for ph in ORDER:
            assert self.seen[ph] == set(self.events[ph]), (self.sem, ph)


def build(nc, weights, slots_in, slots_out, xT_in, memT_in, vec_in, lvec_in, small_in, route_w_in, route_b_in, na_bias_in,
          const_in, dil_in, out):
    with ExitStack() as ctx:
        def sb(name, shape, dt=F32):
            return ctx.enter_context(nc.sbuf_tensor(name, shape, dt))

        def sb_parts(name, shape):
            buf = sb(name, shape)
            at = nc.sbuf_base - 4 * int(np.prod(shape[1:]))
            return buf, nc.alloc_sbuf_tensor_at(name + "_r", shape, F32R, offset=at)

        def sem(name):
            return ctx.enter_context(nc.semaphore(name))

        ring, ring_r = sb_parts("ring", [P, RING, PER_CHUNK * P])
        x = sb("x", [P, KB, S])
        h, h_r = sb_parts("h", [P, KB, S])
        low, low_r = sb_parts("low", [P, KB, S])
        y, y_r = sb_parts("y", [P, KB, S])
        big, big_r = sb_parts("big", [P, FB, S])
        ob, ob_r = sb_parts("ob", [P, 6, S])
        mem = sb("mem", [P, KB, N_MEM])
        nab = sb("nab", [P, 2, NA_SLOTS * GRID_W])
        dil = sb("dil", [P, 2, DIL_W])
        tmp = sb("tmp", [P, 2, S])
        gat = sb("gat", [P, 2, S])
        sd = sb("sd", [P, S])
        rstd = sb("rstd", [P, S])
        consts = sb("consts", [P, 3 * P + GRID_W + 48])
        ones_d = sb("ones_d", [P, P])
        ones = sb("ones", [P, P])
        vec = sb("vec", [P, N_VEC])
        lvec = sb("lvec", [P, N_LVEC])
        wf = sb("wf", [P, KB, HEADS])
        wr = sb("wr", [P, KB, N_GROUPS + EXPERTS])
        route_b = sb("route_b", [P, TT * 20])
        slots = sb("slots", [P, 2 * TT], U32)
        weight = sb("weight", [P, 2 * TT])
        spill = sb("spill", [1, 16], U32)
        trips = sb("trips", [1, 1], U32)
        mod = sb("mod", [P, 48])
        mod1 = sb("mod1", [P, 48])
        silu_c = sb("silu_c", [P, KB])
        lam = sb("lam", [P, 6, 4])
        cumq = sb("cumq", [P, TT, HEADS])
        stat = sb("stat", [P, 4, 4])

        ident = consts[:, 0:P]
        causal = consts[:, P:2 * P]
        earlier = consts[:, 2 * P:3 * P]
        window = consts[:, 3 * P:3 * P + GRID_W]
        own_slot, spill_slot, count_row = (consts[:, 3 * P + GRID_W + 16 * i:3 * P + GRID_W + 16 * (i + 1)]
                                           for i in range(3))

        eps = sb("eps", [P, 3])

        held = sb("held", [P, 1])

        def mem_sq(k):
            return big[:, k // 2, (k % 2) * N_MEM:(k % 2 + 1) * N_MEM]

        def v_(name, i=0):
            return vec[:, VEC[name] + i:VEC[name] + i + 1]

        def lv(name, i=0):
            return lvec[:, LVEC[name] + i:LVEC[name] + i + 1]

        qT, kT = big[:, 0:4, :], big[:, 4:8, :]
        v_tok = big[:, 8:12, :]
        conv_flat = big[:, 12:17, :].rearrange("p a b -> p (a b)")
        CW = S + CONV - 1
        xbp = [conv_flat[:, m * CW:(m + 1) * CW] for m in range(4)]
        a2 = big[:, 12:16, :]
        gg = big[:, 17:21, :]
        fl = big[0:HEADS, 21, :]
        fl2 = gat[0:HEADS, 0, :]
        one_row = gat[0:HEADS, 1, :]
        ncum = tmp[0:HEADS, 0, :]
        r_, ig = h[:, 0:4, :], h[:, 4:8, :]
        a_, xc = y[:, 0:4, :], y[:, 4:8, :]
        ob_flat = ob[:, :, :].rearrange("p a b -> p (a b)")
        y_flat = y[:, :, :].rearrange("p a b -> p (a b)")
        probs = {"A": [ob_flat[:, i * S:(i + 1) * S] for i in range(3)],
                 "L": [y_flat[:, i * 768:(i + 1) * 768] for i in range(3)]}
        probsT = {"A": [ob_flat[:, (3 + i) * S:(4 + i) * S] for i in range(2)],
                  "L": [y_flat[:, 2304 + i * S:2304 + (i + 1) * S] for i in range(2)]}
        rt = tmp[:, :, :].rearrange("p a b -> p (a b)")

        def rtv(i):
            return rt[:, i * 80:(i + 1) * 80]
        gat_flat = gat[:, :, :].rearrange("p a b -> p (a b)")

        def rw(i):
            return gat_flat[:, i * TT * EXPERTS:(i + 1) * TT * EXPERTS]
        u_tok = y[:, :, :].rearrange("p (t a) b -> p t (a b)", t=TT)
        zeros = ob[:, 0:2, :].rearrange("p a b -> p (a b)")
        xt = y[:, 0:2, :].rearrange("p a b -> p (a b)")
        xg = [y[:, 4 + 2 * i:6 + 2 * i, :].rearrange("p a (c q) -> p (a c) q", q=P) for i in range(2)]
        xg_flat = [y[:, 4 + 2 * i:6 + 2 * i, :] for i in range(2)]
        hid = [ob[:, i, :] for i in range(2)]
        yt = ob[:, 2:4, :]
        sil = [gat[:, 0, :], gat[:, 1, :]]
        picked = big[:, 0:16, :].rearrange("p (i a) b -> p i (a b)", i=2 * TT)
        ada_sum = [b.rearrange("p a b -> p (a b)") for b in (ob[:, 2:6, :], ob[:, 2:6, :], y[:, 0:4, :])]
        qa, ka, qb, kb = big[:, 0:3, :], big[:, 3:6, :], big[:, 6:9, :], big[:, 9:12, :]
        qm = big[:, 12:14, :]
        kmT = big[:, 14, :].rearrange("p (a b) -> p a b", a=2)
        va = big[:, 15:19, :]
        vb = big[:, 19:21, :].rearrange("p a b -> p (a b)").rearrange("p (r n) -> p r n", r=4)
        vm = big[:, 21, :].rearrange("p (a b) -> p a b", a=2)
        oa, obb, om = ob[:, 0:3, :], ob[:, 3:4, :], ob[:, 4:6, :]
        ffa = [ob[:, i, :] for i in range(2)]
        ffb = [ob[:, 2 + i, :] for i in range(2)]
        ffg = [ob[:, 4 + i, :] for i in range(2)]
        o_high, y_high = big_r[:, 0:6, :], big_r[:, 6:6 + KB, :]
        f_high = [b[:, i, :] for b, n in ((y_r, KB), (h_r, KB), (ob_r, 6)) for i in range(n)]
        assert len(f_high) == FB
        squares_of = [b[:, i, :] for b in (tmp, gat) for i in range(2)]

        def whole(ap):
            return ap.bitcast(F32)

        def pb(name, n):
            return ctx.enter_context(nc.psum_tensor(name, [P, n, S], F32))
        lin = pb("lin", 2)
        score = pb("score", 2)
        trans = pb("trans", 1)
        attn = pb("attn", 2)
        sums = pb("sums", 1)
        score_flat = score[:, :, :].rearrange("p a b -> p (a b)")

        x_in, mem_in, consts_in, vec_in_s, dil_s, lvec_s, nab_s = (
            sem(n) for n in ("x_in", "mem_in", "consts_in", "vec_in", "dil_in", "lvec_in", "nab_in"))
        out_done = sem("out_done")
        dve_step, act_step, pool_step = sem("dve_step"), sem("act_step"), sem("pool_step")
        chunk_in = [sem(f"chunk_in{s}") for s in range(RING)]
        raw_in = [sem(f"raw_in{s}") for s in range(L_RAW)]
        bank_of = {ph: {g: i % 2 for i, g in enumerate(gs)} for ph, gs in LIN.items()}
        assert all(len(g) % 2 == 0 for g in LIN.values())
        lin_full = [Signal(sem(f"lin_full{b}"), {ph: g[b::2] for ph, g in LIN.items() if ph != "O"}) for b in range(2)]
        lin_free = [Signal(sem(f"lin_free{b}"), {ph: g[b::2] for ph, g in LIN.items() if ph != "O"}) for b in range(2)]
        o_full = [Signal(sem(f"spill_full{b}"), {"O": LIN["O"][b::2]}) for b in range(2)]
        o_free = [Signal(sem(f"spill_free{b}"), {"A": [("table", "trips")[b]], "O": LIN["O"][b::2]}) for b in range(2)]
        spill_in = [sem(f"spill_in{s}") for s in range(TILE_CHUNKS)]
        zeros_out, rows_out, picked_in = sem("zeros_out"), sem("rows_out"), sem("picked_in")
        xt_in, yt_out = sem("xt_in"), sem("yt_out")
        signals = lin_full + lin_free + o_full + o_free

        def filled(ph, g):
            return (o_full if ph.name == "O" else lin_full)[bank_of[ph.name][g]]

        def emptied(ph, g):
            return (o_free if ph.name == "O" else lin_free)[bank_of[ph.name][g]]

        def signal(name, **events):
            s = Signal(sem(name), events)
            signals.append(s)
            return s

        def each(names, n):
            return [(s, k) for s in names for k in range(n)]
        NA_ = [s for s in ("ln1", "ln2", "ln3")]
        LS = ["pre_mix", "post_mix", "pre_ffn", "post_ffn"]
        squares = signal("squares", A=each(["ln1", "mem"], 8) + each(["lru", "attn"], 4) + each(["ln2", "ln3"], 8),
                         B=each(["ln4"], 8), L=each(LS, 8))
        mean_full = signal("mean_full", A=NA_, B=["ln4"])
        centred = signal("centred", A=each(NA_, 8), B=each(["ln4"], 8))
        var_full = signal("var_full", A=["ln1", "mem", "lru", "attn", "ln2", "ln3"], B=["ln4"], L=LS)
        sd_ready = signal("sd_ready", A=["ln1", "mem", "lru", "attn", "ln2", "ln3"], B=["ln4"], L=LS)
        rstd_ready = signal("rstd_ready", A=["ln1", "mem", "lru", "attn", "ln2", "ln3"], B=["ln4"], L=LS)
        normed = signal("normed", A=each(["ln1", "mem"], 8) + each(["lru", "attn"], 4) + each(["ln2", "ln3"], 8),
                        B=each(["ln4"], 8), L=each(["pre_mix", "pre_ffn"], 8))
        affine = signal("affine", A=each(NA_, 8), B=each(["ln4"], 8))
        x_new = signal("x_new", A=[("mix", k) for k in range(8)], B=[("ffn", k) for k in range(8)],
                       L=each(["post_mix", "post_ffn"], 8))
        mod_ready = signal("mod_ready", A=[0, 1, 2])
        ada_step = signal("ada_step", A=[(g, k) for g in range(3) for k in range(KB)])
        tiles = {ph: list(range(len(t))) for ph, t in TILES.items()}
        rounds = {ph: list(range(len(r))) for ph, r in ROUNDS.items()}
        qk_done = signal("qk_done", **tiles)
        score_step = signal("score_step", A=[(i, s) for i in tiles["A"] for s in range(3)],
                            L=[(i, s) for i in tiles["L"] for s in range({"na": 0, "dil": 2, "mem": 1}[TILES["L"][i][0]])])
        scored = signal("scored", **tiles)
        exp_done = signal("exp_done", **tiles)
        rden_ready = signal("rden_ready", **tiles)
        p_ready = signal("p_ready", **tiles)
        t_done = signal("t_done", **rounds)
        pt_ready = signal("pt_ready", **rounds)
        pv_done = signal("pv_done", **rounds)
        o_out = signal("o_out", **OUTS)
        nab_ready = signal("nab_ready", L=list(range(NA_HEADS)))
        f_step = signal("f_step", A=["abs", "exp", "ln", "ls", "cum", "neg"])
        sp_step = signal("sp_step", A=["neg", "abs", "exp", "ln", "sp", "c", "nc"])
        pad_done = signal("pad_done", A=[0])
        conv = signal("conv", A=[(m, s) for m in range(4) for s in range(CONV)])
        lru_act = signal("lru_act", A=[(s, m) for s in ("a", "th", "a2", "sqrt") for m in range(4)])
        lru_dve = signal("lru_dve", A=[(s, m) for s in ("u2", "igx", "u", "scan", "out") for m in range(4)])
        route_exp = signal("route_exp", A=[0])
        route_sub = signal("route_sub", A=[0])
        zeros_ready = signal("zeros_ready", A=[0])
        route_ready = signal("route_ready", A=["chosen", "slots"])
        picked_sum = signal("picked_sum", B=[(t, i) for t in range(TT) for i in range(2)])
        merge_step = signal("merge_step", L=list(range(KB)))
        merged = signal("merged", L=list(range(KB)))
        upd = signal("upd", L=each(["post_mix", "post_ffn"], 8))
        conv_c = signal("conv_c", L=[(n, j) for j in range(FB) for n in ("a", "b")])
        conv_l = signal("conv_l", L=[(n, j) for j in range(FB) for n in ("a", "b")])
        gelu_ready = signal("gelu_ready", L=list(range(FB)))
        ff_ready = signal("ff_ready", L=list(range(FB)))
        w_high = signal("w_high", L=SPLIT)
        w_low = signal("w_low", L=SPLIT)
        w_used = signal("w_used", L=MID)
        part = [(n, k) for n, c in (("pre_mix", KB), ("o", 6), ("y", KB), ("pre_ffn", KB), ("f", FB)) for k in range(c)]
        x_high = signal("x_high", L=part)
        x_low = signal("x_low", L=part)

        A, B = Phase("A"), Phase("B")

        def chunk_value(ph, c):
            n = FIRST_CHUNK.get(ph.name, 0) + c
            v = 16 * (n // RING + 1)
            if ph.name == "O":
                return c % TILE_CHUNKS, spill_in[c % TILE_CHUNKS], ph.reg * 32 + 16 * (c // TILE_CHUNKS + 1)
            if ph.name == "L":
                return c % L_RAW, raw_in[c % L_RAW], ph.reg * (16 * CHUNKS["L"] // L_RAW) + 16 * (c // L_RAW + 1)
            if ph.reg is not None:
                assert CHUNKS[ph.name] % RING == 0
                v = ph.reg * (16 * CHUNKS[ph.name] // RING) + v
            return n % RING, chunk_in[n % RING], v

        def used_up(ph, c):
            if ph.name == "L" and c in MID:
                return w_used.by(ph, c)
            g = LAST_USE[ph.name][(c + 1) * PER_CHUNK - 1]
            if g[0] == "ada":
                return ada_step.by(ph, g[1:])
            return lin_full[bank_of[ph.name][g]].by(ph, g)

        behind, ahead = {}, {}
        for c in SPLIT:
            if c >= L_HIGH:
                g = LAST_USE["L"][(c - L_HIGH + 1) * PER_CHUNK - 1]
                (ahead if c - L_HIGH in MID else behind).setdefault(g, []).append(c)

        block = ctx.enter_context(nc.Block())

        @block.sync
        def _(sp):
            def load(c):
                sp.dma_start(ring[:, c % RING, :], weights[c]).then_inc(chunk_in[c % RING], 16)

            def used(ph, c):
                sp.wait_ge(*used_up(ph, c))

            for c in range(CHUNKS["A"] + RING):
                if c >= RING:
                    used(A, c - RING)
                load(c)
            with sp.Fori(0, M_TRIPS - 1) as g:
                ph = Phase("M", g)
                for c in range(CHUNKS["M"]):
                    used(ph, c)
                    n = FIRST_CHUNK["M"] + RING + c
                    sp.dma_start(ring[:, n % RING, :], weights[g * CHUNKS["M"] + n]).then_inc(chunk_in[n % RING], 16)

            def used_last(name, c):
                s, g = ((w_used, c) if name == "L" and c in MID else
                        (lin_full[bank_of[name][g]], g) if (g := LAST_USE[name][(c + 1) * PER_CHUNK - 1]) else None)
                sp.wait_ge(s.sem, s.count(Phase(name), (TRIPS[name] - 1) * len(s.events[name]) + s.index[name][g] + 1))
            for c in range(CHUNKS["M"] - RING):
                used_last("M", c)
                load(FIRST_CHUNK["M"] + (M_TRIPS - 1) * CHUNKS["M"] + RING + c)

            def spill_load(tile):
                e = sp.value_load(spill[0:1, bass.ds(tile, 1)], min_val=0, max_val=EXPERTS - 1)
                return lambda s: sp.dma_start(ring[:, s, :], weights[e * TILE_CHUNKS + (FIRST_CHUNK["M"] + s)]).then_inc(
                    spill_in[s], 16)
            for b in range(2):
                sp.wait_ge(*o_free[b].by(A, ("table", "trips")[b]))
            n_trips = sp.value_load(trips[0:1, 0:1], min_val=1, max_val=MAX_TRIPS)
            fetch = spill_load(0)
            first = FIRST_CHUNK["M"] + (M_TRIPS - 1) * CHUNKS["M"]
            for s in range(TILE_CHUNKS):
                used_last("M", [c for c in range(CHUNKS["M"]) if (first + c) % RING == s][-1])
                fetch(s)
            with sp.Fori(0, n_trips) as j:
                ph = Phase("O", j)
                for u in range(2):
                    fetch = spill_load(j * 2 + (u + 1))
                    for s in range(TILE_CHUNKS):
                        g = LAST_USE["M"][(u * TILE_CHUNKS + s + 1) * PER_CHUNK - 1]
                        sp.wait_ge(*filled(ph, g).by(ph, g))
                        fetch(s)
            def part_load(l, c):
                sp.dma_start(ring[:, c % L_RAW, :], weights[l * CHUNKS["L"] + (FIRST_CHUNK["L"] + c)]).then_inc(
                    raw_in[c % L_RAW], 16)
            for c in range(L_RAW):
                sp.wait_ge(spill_in[c], n_trips * 32 + 16)
                part_load(0, c)
            with sp.Fori(0, LAYERS - 1) as l:
                for c in range(CHUNKS["L"]):
                    used(Phase("L", l), c)
                    part_load(l, L_RAW + c)
            for c in range(CHUNKS["L"] - L_RAW):
                used_last("L", c)
                part_load(LAYERS - 1, L_RAW + c)

        @block.tensor
        def _(pe):
            seen = set()

            def wblock(ph, n, width=P):
                c = n // PER_CHUNK
                slot, s, v = chunk_value(ph, c)
                if (ph.name, c) not in seen:
                    seen.add((ph.name, c))
                    pe.wait_ge(s, v)
                o = (n % PER_CHUNK) * P
                return ring[:, slot, o:o + width]

            def open_bank(ph, g):
                b = bank_of[ph.name][g]
                s, v = emptied(ph, g).before(ph, g)
                if not (isinstance(v, int) and v == 0):
                    pe.wait_ge(s, v)
                return lin[:, b, :]

            def linear(ph, g, rhs, kb=KB, n=S, wait=None, first=None):
                acc = open_bank(ph, g)
                n0 = BLOCK0[ph.name][g]
                for k in range(kb):
                    w = wblock(ph, n0 + k)
                    if wait:
                        wait(k)
                    mm = pe.matmul(acc[:, 0:n], w, rhs(k), start=(k == 0), stop=(k == kb - 1))
                mm.then_inc(*lin_full[bank_of[ph.name][g]].on(ph, g))

            def w_parts(ph, n, width=P):
                c = n // PER_CHUNK
                if (ph.name, c) not in seen:
                    seen.add((ph.name, c))
                    pe.wait_ge(*w_low.by(ph, c))
                o = (n % PER_CHUNK) * P
                return ring_r[:, L_RAW + c % L_HIGH, o:o + width], ring_r[:, c % L_RAW, o:o + width]

            def split_linear(ph, g, high, low, kb=KB, first=None):
                acc = open_bank(ph, g)
                n0 = BLOCK0[ph.name][g]
                late = kb == KB
                for k in range(kb):
                    wh, wl = w_parts(ph, n0 + k)
                    if first:
                        pe.wait_ge(*x_high.by(ph, (first, k)))
                    pe.matmul(acc, wh, high(k), start=(k == 0), stop=False)
                    mm = pe.matmul(acc, wl, high(k), start=False, stop=False)
                    if not late:
                        if first:
                            pe.wait_ge(*x_low.by(ph, (first, k)))
                        mm = pe.matmul(acc, wh, low(k), start=False, stop=(k == kb - 1))
                        c = (n0 + k) // PER_CHUNK
                        if c in MID and (n0 + k + 1) % PER_CHUNK == 0:
                            mm.then_inc(*w_used.on(ph, c))
                if late:
                    for k in range(kb):
                        wh, _ = w_parts(ph, n0 + k)
                        if first:
                            pe.wait_ge(*x_low.by(ph, (first, k)))
                        mm = pe.matmul(acc, wh, low(k), start=False, stop=(k == kb - 1))
                mm.then_inc(*lin_full[bank_of[ph.name][g]].on(ph, g))

            def split_tokens(ph, g, n0, tok, n):
                acc = open_bank(ph, g)
                for k in range(KB):
                    wh, wl = w_parts(ph, n0 + k * (n // P), n)
                    pe.matmul(acc[:, 0:n], tok(h_r, k), wh, start=(k == 0), stop=False)
                    pe.matmul(acc[:, 0:n], tok(h_r, k), wl, start=False, stop=False)
                    mm = pe.matmul(acc[:, 0:n], tok(low_r, k), wh, start=False, stop=(k == KB - 1))
                mm.then_inc(*lin_full[bank_of[ph.name][g]].on(ph, g))

            def tokens(ph, g, n0, lhs, n, wait=None):
                acc = open_bank(ph, g)
                for k in range(KB):
                    for b in range(0, n, P):
                        w = wblock(ph, n0 + k * (n // P) + b // P)
                    w = wblock(ph, n0 + k * (n // P), n)
                    mm = pe.matmul(acc[:, 0:n], lhs(k), w, start=(k == 0), stop=(k == KB - 1))
                mm.then_inc(*lin_full[bank_of[ph.name][g]].on(ph, g))

            def mean_sum(ph, st, src, wait):
                for k in range(KB):
                    wait(k)
                    mm = pe.matmul(sums[:, 0, :], ones_d[:, :], src[:, k, :], start=(k == 0), stop=(k == KB - 1))
                mm.then_inc(*mean_full.on(ph, st))

            def square_sum(ph, st, k, src, ones, n_k=KB, n=S):
                pe.wait_ge(*squares.by(ph, (st, k)))
                mm = pe.matmul(sums[:, 0, 0:n], ones[:, :], src, start=(k == 0), stop=(k == n_k - 1))
                if k == n_k - 1:
                    mm.then_inc(*var_full.on(ph, st))

            def attention(ph, q_of, k_of, v_of, extra=None):
                name = ph.name
                tl, rs = TILES[name], ROUNDS[name]

                def qk(i):
                    kind, hp, half, t = tl[i]
                    lo = DH * half
                    if i >= 1 and (kind == "dil" or tl[i - 1][0] == "dil"):
                        pe.wait_ge(*scored.by(ph, i - 1))
                    elif i >= 2 and kind == "mem" and tl[i - 2][0] == "mem":
                        pe.wait_ge(*exp_done.by(ph, i - 2))
                    elif i >= 2:
                        pe.wait_ge(*scored.by(ph, i - 2))
                    if kind == "dil":
                        for g in range(DIL_G):
                            q = qb[lo:lo + DH, g, t::4]
                            k = kb[lo:lo + DH, g, :] if g == 0 else kb[lo:lo + DH, g, t::4]
                            o = score_flat[:, 0:S] if g == 0 else score_flat[:, S + (g - 1) * P:S + g * P]
                            mm = pe.matmul(o, q, k, start=True, stop=True)
                    else:
                        n = key_chunks(kind, t) * P
                        mm = pe.matmul(score[:, i % 2, 0:n], q_of(kind)[lo:lo + DH, hp, t * P:(t + 1) * P],
                                       k_of(kind)[lo:lo + DH, hp, 0:n], start=True, stop=True)
                    mm.then_inc(*qk_done.on(ph, i))

                def turn(j):
                    i, c0, n = rs[j]
                    if c0 == 0:
                        pe.wait_ge(*p_ready.by(ph, i))
                    if j >= 1:
                        pe.wait_ge(*pt_ready.by(ph, j - 1))
                    for c in range(n):
                        mm = pe.transpose(trans[:, 0, c * P:(c + 1) * P],
                                          probs[name][i % 3][:, (c0 + c) * P:(c0 + c + 1) * P], ident)
                    mm.then_inc(*t_done.on(ph, j))

                def pv(j):
                    i, c0, n = rs[j]
                    kind, hp, half, t = tl[i]
                    o = OUTS[name].index((kind, hp))
                    if o >= 2 and c0 == 0:
                        pe.wait_ge(*o_out.by(ph, OUTS[name][o - 2]))
                    pe.wait_ge(*pt_ready.by(ph, j))
                    total = key_chunks(kind, t)
                    lo = DH * half
                    for c in range(n):
                        mm = pe.matmul(attn[lo:lo + DH, o % 2, t * P:(t + 1) * P], v_of(kind, hp, half, t, c0 + c),
                                       probsT[name][j % 2][:, c * P:(c + 1) * P],
                                       start=(c0 + c == 0), stop=(c0 + c == total - 1))
                    mm.then_inc(*pv_done.on(ph, j))

                n = len(tl)
                for i in range(n + 3):
                    if extra and i < n:
                        extra(i)
                    if i < n:
                        qk(i)
                    if 2 <= i < n + 2:
                        for j in ROUNDS_OF[name][i - 2]:
                            turn(j)
                            if j >= 1:
                                pv(j - 1)
                pv(len(rs) - 1)

            pe.wait_ge(dve_step, 6)
            pe.wait_ge(x_in, 16)
            mean_sum(A, "ln1", x, lambda k: None)
            pe.wait_ge(*centred.by(A, ("ln1", 7)))
            for k in range(KB):
                square_sum(A, "ln1", k, y[:, k, :], ones_d)
            pe.wait_ge(*sd_ready.by(A, "ln1"))
            for k in range(KB):
                square_sum(A, "mem", k, mem_sq(k), ones_d, n=N_MEM)

            def ada(g):
                acc = open_bank(A, f"ada{g}")
                pe.wait_ge(*ada_step.by(A, (g, KB - 1)))
                for m in range(16):
                    mm = pe.matmul(acc[:, m:m + 1], ada_sum[g][:, m * P:(m + 1) * P], ones[:, 0:1], start=True, stop=True)
                mm.then_inc(*lin_full[bank_of["A"][f"ada{g}"]].on(A, f"ada{g}"))

            ada(0)
            pe.wait_ge(consts_in, 16 * 4)
            acc = open_bank(A, "f")
            for k in range(KB):
                pe.wait_ge(*affine.by(A, ("ln1", k)))
                mm = pe.matmul(acc[0:HEADS, :], wf[:, k, :], h[:, k, :], start=(k == 0), stop=(k == KB - 1))
            mm.then_inc(*lin_full[bank_of["A"]["f"]].on(A, "f"))
            for n in ("xb", "gb", "q", "k"):
                for m in range(4):
                    linear(A, f"{n}{m}", lambda k: h[:, k, :])
            for t in range(TT):
                tokens(A, f"v{t}", BLOCK0["A"]["v3"], lambda k: h[:, k, t * P:(t + 1) * P], 512)
            ada(1)
            ada(2)
            for n in ("r", "i"):
                for m in range(4):
                    linear(A, f"{n}{m}", lambda k: xc[:, m, :], kb=1,
                           wait=lambda k: pe.wait_ge(*conv.by(A, (m, CONV - 1))))
            for k in range(4):
                square_sum(A, "lru", k, h[:, k, :], ones, n_k=4)
            acc = open_bank(A, "cumT")
            pe.wait_ge(*f_step.by(A, "cum"))
            for t in range(TT):
                mm = pe.transpose(acc[:, t * HEADS:(t + 1) * HEADS], fl[:, t * P:(t + 1) * P], ident[0:HEADS, 0:HEADS])
            mm.then_inc(*lin_full[bank_of["A"]["cumT"]].on(A, "cumT"))

            def negcum(i):
                todo = [0, 1] if i == 0 else [i // TT + 1] if i % TT == 0 else []
                for hd in todo:
                    if hd < HEADS:
                        acc = open_bank(A, f"nc{hd}")
                        if hd == 0:
                            pe.wait_ge(*f_step.by(A, "neg"))
                        pe.matmul(acc, ident[0:HEADS, hd:hd + 1].to_broadcast([HEADS, P]), ncum,
                                  start=True, stop=True).then_inc(*lin_full[bank_of["A"][f"nc{hd}"]].on(A, f"nc{hd}"))

            pe.wait_ge(*lin_free[bank_of["A"]["v2"]].by(A, "v2"))
            pe.wait_ge(*lin_free[bank_of["A"]["v3"]].by(A, "v3"))
            attention(A, lambda kind: qT, lambda kind: kT,
                      lambda kind, hp, half, t, c: v_tok[:, c, (2 * hp + half) * DH:(2 * hp + half + 1) * DH],
                      extra=negcum)
            for k in range(4):
                square_sum(A, "attn", k, h[:, k, :], ones, n_k=4)
            for m in range(KB):
                linear(A, f"out{m}", lambda k: y[:, k, :],
                       wait=(lambda k: pe.wait_ge(*normed.by(A, ("attn", k))) if k < 4 else None) if m == 0 else None)
            for st, src in (("ln2", x), ("ln3", x)):
                ev = (lambda k: x_new.by(A, ("mix", k))) if st == "ln2" else (lambda k: affine.by(A, ("ln2", k)))
                mean_sum(A, st, src, lambda k: pe.wait_ge(*ev(k)))
                pe.wait_ge(*centred.by(A, (st, 7)))
                for k in range(KB):
                    square_sum(A, st, k, (h if st == "ln2" else y)[:, k, :], ones_d)
            for half in range(2):
                acc = open_bank(A, f"rt{half}")
                for t in range(2):
                    for k in range(KB):
                        if half == 0 and t == 0:
                            pe.wait_ge(*affine.by(A, ("ln3", k)))
                        tok = (2 * half + t) * P
                        mm = pe.matmul(acc[:, t * 20:(t + 1) * 20], h[:, k, tok:tok + P], wr[:, k, :],
                                       start=(k == 0), stop=(k == KB - 1))
                mm.then_inc(*lin_full[bank_of["A"][f"rt{half}"]].on(A, f"rt{half}"))
            acc = open_bank(A, "pos")
            pe.wait_ge(*route_ready.by(A, "chosen"))
            for t in range(TT + 1):
                for q in range(min(t + 1, TT)):
                    mm = pe.matmul(acc[:, t * EXPERTS:(t + 1) * EXPERTS], earlier if q == t else ones[:, :],
                                   rw(0)[:, q * EXPERTS:(q + 1) * EXPERTS], start=(q == 0), stop=(q == min(t, TT - 1)))
            mm.then_inc(*filled(A, "pos").on(A, "pos"))
            for t in range(TT):
                for i in range(2):
                    g = f"ut{t}.{i}"
                    acc = open_bank(A, g)
                    for c in range(4):
                        mm = pe.transpose(acc[:, c * P:(c + 1) * P], h[:, 4 * i + c, t * P:(t + 1) * P], ident)
                    mm.then_inc(*filled(A, g).on(A, g))

            def turn_rows(ph, g, i):
                acc = open_bank(ph, g)
                for c in range(4):
                    mm = pe.transpose(acc[:, c * P:(c + 1) * P], xt[:, (4 * i + c) * P:(4 * i + c + 1) * P], ident)
                mm.then_inc(*filled(ph, g).on(ph, g))

            def expert_tile(ph, e, rows):
                for n in ("gate", "up"):
                    acc = open_bank(ph, f"{n}{e}")
                    n0 = BLOCK0[ph.name][f"{n}{e}"]
                    for m in range(EB):
                        for k in range(KB):
                            mm = pe.matmul(acc[:, m * P:(m + 1) * P], wblock(ph, n0 + m * KB + k), xg[e % 2][:, k, :],
                                           start=(k == 0), stop=(k == KB - 1))
                    mm.then_inc(*filled(ph, f"{n}{e}").on(ph, f"{n}{e}"))
                pe.wait_ge(*rows)
                n0 = BLOCK0[ph.name][f"down{e}.1"]
                for i in range(2):
                    turn_rows(ph, f"xt{e}.{i}", i)
                    g = f"down{e}.{i}"
                    acc = open_bank(ph, g)
                    if i == 0:
                        pe.wait_ge(*emptied(ph, f"up{e}").by(ph, f"up{e}"))
                    for k in range(EB):
                        mm = pe.matmul(acc, hid[e % 2][:, k * P:(k + 1) * P], wblock(ph, n0 + k * KB + 4 * i, 4 * P),
                                       start=(k == 0), stop=(k == EB - 1))
                    mm.then_inc(*filled(ph, g).on(ph, g))

            pe.wait_ge(xt_in, 16)
            for i in range(2):
                turn_rows(A, f"xt.{i}", i)
            pe.wait_ge(*emptied(A, "xt.1").by(A, "xt.1"))
            with pe.Fori(0, M_TRIPS) as g:
                ph = Phase("M", g)
                for e in range(TILES_PER_TRIP):
                    expert_tile(ph, e, (xt_in, g * (16 * TILES_PER_TRIP) + 16 * (e + 2)))
            for b in range(2):
                pe.wait_ge(*o_free[b].by(A, ("table", "trips")[b]))
            n_trips = pe.value_load(trips[0:1, 0:1], min_val=1, max_val=MAX_TRIPS)
            for s in lin_free:
                pe.wait_ge(s.sem, s.count(Phase("M"), M_TRIPS * len(s.events["M"])))
            with pe.Fori(0, n_trips) as j:
                ph = Phase("O", j)
                for e in range(2):
                    expert_tile(ph, e, (xt_in, j * 32 + 16 * (EXPERTS + e + 2)))
            for m in range(KB):
                acc = open_bank(B, f"yt{m}")
                for t in range(TT):
                    if m == 0:
                        pe.wait_ge(*picked_sum.by(B, (t, 1)))
                    mm = pe.transpose(acc[:, t * P:(t + 1) * P], picked[:, 2 * t + 1, m * P:(m + 1) * P], ident)
                mm.then_inc(*filled(B, f"yt{m}").on(B, f"yt{m}"))
            mean_sum(B, "ln4", x, lambda k: pe.wait_ge(*x_new.by(B, ("ffn", k))))
            pe.wait_ge(*centred.by(B, ("ln4", 7)))
            for k in range(KB):
                square_sum(B, "ln4", k, h[:, k, :], ones_d)

            with pe.Fori(0, LAYERS) as l:
                ph = Phase("L", l)
                for k in range(KB):
                    square_sum(ph, "pre_mix", k, h[:, k, :], ones_d)
                def normed_linear(g, first=None):
                    split_linear(ph, g, lambda k: h_r[:, k, :], lambda k: low_r[:, k, :], first=first)
                for m in range(14):
                    normed_linear(f"qk{m}", "pre_mix" if m == 0 else None)
                for t in range(TT):
                    split_tokens(ph, f"va{t}", BLOCK0["L"]["va3"], lambda b, k: b[:, k, t * P:(t + 1) * P], 512)
                for r in range(4):
                    split_tokens(ph, f"vb{r}", BLOCK0["L"]["vb3"], lambda b, k: b[:, k, r::4], 256)
                for m in range(2):
                    linear(ph, f"km{m}", lambda k: mem[:, k, :], n=N_MEM)
                for t in range(2):
                    tokens(ph, f"vm{t}", BLOCK0["L"]["vm1"], lambda k: mem[:, k, t * P:(t + 1) * P], 256)
                pe.wait_ge(*lin_free[bank_of["L"]["vm0"]].by(ph, "vm0"))
                pe.wait_ge(*lin_free[bank_of["L"]["vm1"]].by(ph, "vm1"))

                def v_of(kind, hp, half, t, c):
                    lo = (2 * hp + half) * DH
                    if kind == "na":
                        return va[:, c, lo:lo + DH]
                    if kind == "mem":
                        return vm[:, c, lo:lo + DH]
                    if c < 4:
                        return va[:, c, D_A + lo:D_A + lo + DH]
                    return vb[:, t, (c - 4) * P + lo:(c - 4) * P + lo + DH]
                attention(ph, lambda kind: qa if kind == "na" else qm, lambda kind: ka if kind == "na" else kmT, v_of)

                for m in range(KB):
                    for i, (n, o, width) in enumerate((("ba", 0, 3), ("bb", 3, 1), ("bm", 4, 2))):
                        normed_linear(f"g{i}.{m}")
                        if m == 0:
                            pe.wait_ge(*x_low.by(ph, ("o", o + width - 1)))
                        split_linear(ph, f"{n}{m}", lambda k: o_high[:, o + k, :], lambda k: ob_r[:, o + k, :], kb=width)
                for m in range(KB):
                    split_linear(ph, f"out{m}", lambda k: y_high[:, k, :], lambda k: y_r[:, k, :],
                                 first="y" if m == 0 else None)
                    if m >= 2:
                        square_sum(ph, "post_mix", m - 2, big[:, FB - KB + m - 2, :], ones_d)
                for k in range(KB - 2, KB):
                    square_sum(ph, "post_mix", k, big[:, FB - KB + k, :], ones_d)
                for k in range(KB):
                    square_sum(ph, "pre_ffn", k, h[:, k, :], ones_d)
                for j in range(FB):
                    normed_linear(f"a{j}", "pre_ffn" if j == 0 else None)
                    normed_linear(f"b{j}")
                for m in range(KB):
                    split_linear(ph, f"down{m}", lambda k: f_high[k], lambda k: big_r[:, k, :], kb=FB,
                                 first="f" if m == 0 else None)
                    if m >= 2:
                        square_sum(ph, "post_ffn", m - 2, squares_of[(m - 2) % 4], ones_d)
                for k in range(KB - 2, KB):
                    square_sum(ph, "post_ffn", k, squares_of[k % 4], ones_d)

        @block.scalar
        def _(act):
            def full(ph, g):
                act.wait_ge(*filled(ph, g).by(ph, g))
                return lin[:, bank_of[ph.name][g], :], emptied(ph, g)

            def square(ph, st, k, src, dst):
                act.activation(dst, src, ACT.Square).then_inc(*squares.on(ph, (st, k)))

            def root(ph, st, e, n=S, scale=1.0):
                act.wait_ge(*var_full.by(ph, st))
                act.activation(sd[:, 0:n], sums[:, 0, 0:n], ACT.Sqrt, bias=e, scale=scale).then_inc(*sd_ready.on(ph, st))

            def affine_of(ph, st, k, dst, g, b):
                act.wait_ge(*normed.by(ph, (st, k)))
                act.activation(dst, dst, ACT.Identity, bias=b, scale=g).then_inc(*affine.on(ph, (st, k)))

            def attention(ph, extra=None, after=None):
                name = ph.name
                tl = TILES[name]

                def exp(i):
                    kind, hp, half, t = tl[i]
                    n = key_chunks(kind, t) * P
                    p = probs[name][i % 3][:, 0:n]
                    act.wait_ge(*scored.by(ph, i))
                    src = score[:, i % 2, 0:n] if kind == "mem" else p
                    if kind == "mem" and i >= 3:
                        act.wait_ge(*t_done.by(ph, ROUNDS_OF[name][i - 3][-1]))
                    act.activation(p, src, ACT.Exp, bias=stat[:, 0, i % 4:i % 4 + 1],
                                   scale=-1.0 if kind in ("na", "dil") else 1.0,
                                   accum_out=stat[:, 1, i % 4:i % 4 + 1]).then_inc(*exp_done.on(ph, i))

                def out_of(o):
                    kind, hp = OUTS[name][o]
                    last = max(j for j, r in enumerate(ROUNDS[name]) if tl[r[0]][0:2] == (kind, hp))
                    act.wait_ge(*pv_done.by(ph, last))
                    src = attn[:, o % 2, :]
                    if kind == "dil":
                        dst = obb[:, 0, :].rearrange("p (a r) -> p r a", r=4)
                        src = src.rearrange("p (r a) -> p r a", r=4)
                    else:
                        dst = {"fa": y, "na": oa, "mem": om}[kind][:, hp, :]
                    act.copy(dst, src).then_inc(*o_out.on(ph, (kind, hp)))

                ends = {max(i for i, x in enumerate(tl) if x[0:2] == o): n for n, o in enumerate(OUTS[name])}
                for i in range(len(tl) + 4):
                    if extra:
                        extra(i)
                    if i < len(tl):
                        exp(i)
                        if after:
                            after(i)
                    if i - 4 in ends:
                        out_of(ends[i - 4])

            act.dma_start(x[:, :, :], xT_in).then_inc(x_in, 16)
            act.dma_start(vec[:, :], vec_in).then_inc(vec_in_s, 16)
            act.dma_start(consts[:, :], const_in).then_inc(consts_in, 16)
            act.dma_start(wf[:, :, :], small_in).then_inc(consts_in, 16)
            act.dma_start(wr[:, :, :], route_w_in).then_inc(consts_in, 16)
            act.dma_start(route_b[:, :], route_b_in).then_inc(consts_in, 16)
            act.dma_start(mem[:, :, :], memT_in).then_inc(mem_in, 16)
            act.dma_start(dil[:, :, :], dil_in).then_inc(dil_s, 16)

            act.wait_ge(dve_step, 6)
            act.wait_ge(vec_in_s, 16)
            act.activation(silu_c[:, :], vec[:, VEC["c"]:VEC["c"] + KB], ACT.Silu).then_inc(act_step, 1)
            act.wait_ge(*sp_step.by(A, "abs"))
            act.activation(lam[:, 2, :], lam[:, 1, :], ACT.Exp, scale=-1.0).then_inc(*sp_step.on(A, "exp"))
            act.wait_ge(*sp_step.by(A, "exp"))
            act.activation(lam[:, 3, :], lam[:, 2, :], ACT.Ln, bias=eps[:, 2:3]).then_inc(*sp_step.on(A, "ln"))
            for k in range(KB):
                act.wait_ge(*centred.by(A, ("ln1", k)))
                square(A, "ln1", k, h[:, k, :], y[:, k, :])
            root(A, "ln1", eps[:, 0:1])
            act.wait_ge(mem_in, 16)
            for k in range(KB):
                square(A, "mem", k, mem[:, k, :], mem_sq(k))
            act.wait_ge(*rstd_ready.by(A, "ln1"))
            root(A, "mem", eps[:, 1:2], N_MEM)
            act.wait_ge(*mod_ready.by(A, 0))
            for k in range(KB):
                affine_of(A, "ln1", k, h[:, k, :], mod1[:, 8 + k:9 + k], mod[:, k:k + 1])
            act.wait_ge(*f_step.by(A, "abs"))
            act.activation(fl2, fl2, ACT.Exp, scale=-1.0).then_inc(*f_step.on(A, "exp"))
            act.wait_ge(*f_step.by(A, "exp"))
            act.activation(fl2, fl2, ACT.Ln, bias=eps[0:HEADS, 2:3]).then_inc(*f_step.on(A, "ln"))
            act.wait_ge(*pad_done.by(A, 0))
            for m in range(4):
                acc, free = full(A, f"xb{m}")
                act.copy(xbp[m][:, CONV - 1:], acc).then_inc(*free.on(A, f"xb{m}"))
            for m in range(4):
                acc, free = full(A, f"gb{m}")
                act.activation(gg[:, m, :], acc, ACT.Gelu_apprx_tanh).then_inc(*free.on(A, f"gb{m}"))
            for m in range(4):
                acc, free = full(A, f"q{m}")
                act.activation(qT[:, m, :], acc, ACT.Copy, scale=DH ** -0.5).then_inc(*free.on(A, f"q{m}"))
            for n, dst in (("k", kT), ("v", v_tok)):
                for m in range(4):
                    acc, free = full(A, f"{n}{m}")
                    act.copy(dst[:, m, :], acc).then_inc(*free.on(A, f"{n}{m}"))

            for n, dst in (("r", r_), ("i", ig)):
                for m in range(4):
                    acc, free = full(A, f"{n}{m}")
                    act.activation(dst[:, m, :], acc, ACT.Sigmoid,
                                   bias=v_(f"b_{n}g", m)).then_inc(*free.on(A, f"{n}{m}"))
            act.wait_ge(*lin_free[bank_of["A"]["r3"]].by(A, "r3"))
            act.wait_ge(*lin_free[bank_of["A"]["r2"]].by(A, "r2"))
            act.wait_ge(*sp_step.by(A, "nc"))
            for m in range(4):
                act.activation(a_[:, m, :], r_[:, m, :], ACT.Exp,
                               scale=lam[:, 5, m:m + 1]).then_inc(*lru_act.on(A, ("a", m)))
            for m in range(4):
                act.wait_ge(*lru_act.by(A, ("a", m)))
                act.activation(r_[:, m, :], r_[:, m, :], ACT.Tanh,
                               scale=lam[:, 4, m:m + 1]).then_inc(*lru_act.on(A, ("th", m)))
            for m in range(4):
                act.activation(a2[:, m, :], a_[:, m, :], ACT.Square).then_inc(*lru_act.on(A, ("a2", m)))
            for m in range(4):
                act.wait_ge(*lru_dve.by(A, ("u2", m)))
                act.activation(r_[:, m, :], r_[:, m, :], ACT.Sqrt).then_inc(*lru_act.on(A, ("sqrt", m)))
            for k in range(4):
                act.wait_ge(*lru_dve.by(A, ("out", k)))
                square(A, "lru", k, xc[:, k, :], h[:, k, :])
            act.wait_ge(*rstd_ready.by(A, "mem"))
            root(A, "lru", eps[:, 1:2], scale=1.0 / D_ATTN)

            def negcum(i):
                todo = [0, 1] if i == 0 else [i // TT + 1] if i % TT == 0 else []
                for hd in todo:
                    if hd < HEADS:
                        if hd == 0:
                            act.wait_ge(*f_step.by(A, "cum"))
                        if hd >= 2:
                            act.wait_ge(*scored.by(A, TT * (hd - 1) - 1))
                        acc, free = full(A, f"nc{hd}")
                        act.copy(gat[:, hd % 2, :], acc).then_inc(*free.on(A, f"nc{hd}"))
            attention(A, extra=negcum)
            for k in range(4):
                act.wait_ge(*o_out.by(A, ("fa", k)))
                square(A, "attn", k, y[:, k, :], h[:, k, :])
            act.wait_ge(*rstd_ready.by(A, "lru"))
            root(A, "attn", eps[:, 1:2], scale=1.0 / D_ATTN)
            for st in ("ln2", "ln3"):
                src, sq, dst = (x, h, x) if st == "ln2" else (h, y, h)
                for k in range(KB):
                    act.wait_ge(*centred.by(A, (st, k)))
                    square(A, st, k, src[:, k, :], sq[:, k, :])
                root(A, st, eps[:, 0:1])
                if st == "ln3":
                    act.wait_ge(*mod_ready.by(A, 2))
                for k in range(KB):
                    g, b = ((v_("ln1_g", k), v_("ln1_b", k)) if st == "ln2"
                            else (mod1[:, 32 + k:33 + k], mod[:, 24 + k:25 + k]))
                    affine_of(A, st, k, dst[:, k, :], g, b)
            act.wait_ge(*route_sub.by(A, 0))
            act.activation(rtv(1), rtv(1), ACT.Exp).then_inc(*route_exp.on(A, 0))
            for t in range(TT):
                for i in range(2):
                    acc, free = full(A, f"ut{t}.{i}")
                    act.copy(u_tok[:, t, i * S:(i + 1) * S], acc).then_inc(*free.on(A, f"ut{t}.{i}"))

            act.wait_ge(rows_out, 16 * 2 * TT)
            act.dma_start(xt, slots_in[0:P, :]).then_inc(xt_in, 16)

            def expert_tile(ph, e, tile, stored):
                acc, free = full(ph, f"gate{e}")
                act.activation(sil[e % 2], acc, ACT.Silu).then_inc(*free.on(ph, f"gate{e}"))
                for i in range(2):
                    acc, free = full(ph, f"down{e}.{i}")
                    act.copy(yt[:, i, :], acc).then_inc(*free.on(ph, f"down{e}.{i}"))
                    if i == 0:
                        act.wait_ge(*filled(ph, f"xt{e}.1").by(ph, f"xt{e}.1"))
                        act.dma_start(xt, slots_in[bass.ds((tile + 2) * P, P), :]).then_inc(xt_in, 16)
                for i in range(2):
                    act.wait_ge(*emptied(ph, f"down{e}.{i}").by(ph, f"down{e}.{i}"))
                act.dma_start(slots_out[bass.ds(tile * P, P), :],
                              yt.rearrange("p a b -> p (a b)")).then_inc(yt_out, 16)
                act.wait_ge(yt_out, stored)

            act.wait_ge(*lin_full[bank_of["A"]["xt.1"]].by(A, "xt.1"))
            act.dma_start(xt, slots_in[P:2 * P, :]).then_inc(xt_in, 16)
            with act.Fori(0, M_TRIPS) as g:
                for e in range(TILES_PER_TRIP):
                    expert_tile(Phase("M", g), e, g * TILES_PER_TRIP + e,
                                g * (16 * TILES_PER_TRIP) + 16 * (e + 1))
            for b in range(2):
                act.wait_ge(*o_free[b].by(A, ("table", "trips")[b]))
            n_trips = act.value_load(trips[0:1, 0:1], min_val=1, max_val=MAX_TRIPS)
            with act.Fori(0, n_trips) as j:
                for e in range(2):
                    expert_tile(Phase("O", j), e, j * 2 + (EXPERTS + e), j * 32 + 16 * (EXPERTS + e + 1))
            for k in range(KB):
                act.wait_ge(*centred.by(B, ("ln4", k)))
                square(B, "ln4", k, x[:, k, :], h[:, k, :])
            root(B, "ln4", eps[:, 0:1])
            for k in range(KB):
                affine_of(B, "ln4", k, x[:, k, :], v_("ln2_g", k), v_("ln2_b", k))

            def split(ph, chunks):
                for c in chunks:
                    slot, s, v = chunk_value(ph, c)
                    if c >= L_HIGH:
                        act.wait_ge(*used_up(ph, c - L_HIGH))
                    act.wait_ge(s, v)
                    act.copy(ring_r[:, L_RAW + c % L_HIGH, :], ring[:, slot, :]).then_inc(*w_high.on(ph, c))

            def high(ph, n, k, dst, src):
                act.copy(dst, src).then_inc(*x_high.on(ph, (n, k)))
            act.wait_ge(*affine.by(B, ("ln4", KB - 1)))
            for s in range(L_RAW, RING):
                act.wait_ge(spill_in[s], n_trips * 32 + 16)
            with act.Fori(0, LAYERS) as l:
                ph = Phase("L", l)

                def normed_parts(st):
                    for k in range(KB):
                        act.wait_ge(*normed.by(ph, (st, k)))
                        high(ph, st, k, h_r[:, k, :], low[:, k, :])
                act.dma_start(lvec[:, :], lvec_in[l]).then_inc(lvec_s, 16)
                act.dma_start(nab[:, 0, :], na_bias_in[l * NA_HEADS]).then_inc(nab_s, 16)
                for k in range(KB):
                    square(ph, "pre_mix", k, x[:, k, :], h[:, k, :])
                split(ph, range(L_HIGH))
                root(ph, "pre_mix", eps[:, 1:2])
                normed_parts("pre_mix")
                for m in range(14):
                    acc, free = full(ph, f"qk{m}")
                    dst = ([qa[:, i, :] for i in range(3)] + [ka[:, i, :] for i in range(3)]
                           + [qb[:, i, :] for i in range(3)] + [kb[:, i, :] for i in range(3)]
                           + [qm[:, i, :] for i in range(2)])[m]
                    is_q = m < 3 or 6 <= m < 9 or m >= 12
                    act.activation(dst, acc, ACT.Copy, scale=DH ** -0.5 if is_q else 1.0).then_inc(*free.on(ph, f"qk{m}"))
                    split(ph, behind.get(f"qk{m}", []))
                for n, dst, w in ([(f"va{t}", va[:, t, :], S) for t in range(TT)]
                                  + [(f"vb{r}", vb[:, r, :], 2 * P) for r in range(4)]
                                  + [(f"km{m}", kmT[:, m, :], N_MEM) for m in range(2)]
                                  + [(f"vm{t}", vm[:, t, :], D_M) for t in range(2)]):
                    acc, free = full(ph, n)
                    act.copy(dst, acc[:, 0:w]).then_inc(*free.on(ph, n))
                    split(ph, behind.get(n, []))

                def next_bias(i):
                    hd = i // TT + 1
                    if i % TT == 0 and hd < NA_HEADS:
                        act.dma_start(nab[:, hd % 2, :], na_bias_in[l * NA_HEADS + hd]).then_inc(nab_s, 16)
                attention(ph, after=next_bias)
                for k in range(6):
                    act.wait_ge(*o_out.by(ph, OUTS["L"][k]))
                    high(ph, "o", k, o_high[:, k, :], ob[:, k, :])
                for m in range(KB):
                    for i, n in enumerate(("g0.", "g1.", "g2.")):
                        j = 3 * m + i
                        if j >= 2:
                            pm, pi = divmod(j - 2, 3)
                            g = f"{('ba', 'bb', 'bm')[pi]}{pm}"
                            act.wait_ge(*lin_free[bank_of["L"][g]].by(ph, g))
                        acc, free = full(ph, f"{n}{m}")
                        act.activation(gat[:, j % 2, :], acc, ACT.Sigmoid,
                                       bias=lv("b_gate", 8 * i + m)).then_inc(*free.on(ph, f"{n}{m}"))
                        split(ph, behind.get(f"{n}{m}", []) + behind.get(f"{('ba', 'bb', 'bm')[i]}{m}", []))
                    if m >= 1:
                        act.wait_ge(*merged.by(ph, m - 1))
                        high(ph, "y", m - 1, y_high[:, m - 1, :], y[:, m - 1, :])
                act.wait_ge(*merged.by(ph, KB - 1))
                high(ph, "y", KB - 1, y_high[:, KB - 1, :], y[:, KB - 1, :])
                for m in range(KB):
                    acc, free = full(ph, f"out{m}")
                    square(ph, "post_mix", m, acc, big[:, FB - KB + m, :])
                    act.copy(h[:, m, :], acc).then_inc(*free.on(ph, f"out{m}"))
                    if m < KB - 1:
                        split(ph, behind.get(f"out{m}", []))
                root(ph, "post_mix", eps[:, 1:2])
                for k in range(KB):
                    act.wait_ge(*x_new.by(ph, ("post_mix", k)))
                    square(ph, "pre_ffn", k, x[:, k, :], h[:, k, :])
                split(ph, behind.get(f"out{KB - 1}", []))
                root(ph, "pre_ffn", eps[:, 1:2])
                normed_parts("pre_ffn")

                def conv_mid(n, j):
                    f = j if n == "a" else FB + j
                    acc, _ = full(ph, f"{n}{j}")
                    dst = (ffa if n == "a" else ffb)[j % 2]
                    if j >= 2:
                        act.wait_ge(*ff_ready.by(ph, j - 2))
                    act.activation(dst, acc, ACT.Identity, bias=lv("conv_b", f),
                                   scale=lv("conv_w", 2 * FB + f)).then_inc(*conv_c.on(ph, (n, j)))

                def gelu(j):
                    act.wait_ge(*lin_free[bank_of["L"][f"a{j}"]].by(ph, f"a{j}"))
                    act.activation(ffg[j % 2], ffa[j % 2], ACT.Gelu_apprx_tanh).then_inc(*gelu_ready.on(ph, j))
                def f_parts(ks):
                    for k in ks:
                        act.wait_ge(*ff_ready.by(ph, k))
                        high(ph, "f", k, f_high[k], big[:, k, :])
                for j in range(FB):
                    for n in ("a", "b"):
                        conv_mid(n, j)
                        split(ph, behind.get(f"{n}{j}", []))
                    gelu(j)
                    if 1 <= j <= KB:
                        f_parts([j - 1])
                f_parts(range(KB, 2 * KB))
                act.wait_ge(*ff_ready.by(ph, FB - 1))
                f_parts(range(2 * KB, FB))
                for m in range(KB):
                    split(ph, ahead.get(f"down{m}", []))
                    acc, free = full(ph, f"down{m}")
                    square(ph, "post_ffn", m, acc, squares_of[m % 4])
                    act.copy(low[:, m, :], acc).then_inc(*free.on(ph, f"down{m}"))
                    split(ph, behind.get(f"down{m}", []))
                root(ph, "post_ffn", eps[:, 1:2])
                act.wait_ge(*x_new.by(ph, ("post_ffn", KB - 1)))

        @block.vector
        def _(dve):
            steps = [0]

            def step(ins):
                steps[0] += 1
                ins.then_inc(dve_step, 1)
                dve.wait_ge(dve_step, steps[0])

            def full(ph, g):
                dve.wait_ge(*filled(ph, g).by(ph, g))
                return lin[:, bank_of[ph.name][g], :], emptied(ph, g)

            def root_inverse(ph, st, n=S):
                dve.wait_ge(*sd_ready.by(ph, st))
                dve.reciprocal(rstd[:, 0:n], sd[:, 0:n]).then_inc(*rstd_ready.on(ph, st))
                dve.wait_ge(*rstd_ready.by(ph, st))

            def centre(ph, st, src, dst):
                dve.wait_ge(*mean_full.by(ph, st))
                for k in range(KB):
                    dve.tensor_tensor(dst[:, k, :], src[:, k, :], sums[:, 0, :],
                                      ALU.subtract).then_inc(*centred.on(ph, (st, k)))

            def scale_all(ph, st, buf):
                root_inverse(ph, st)
                for k in range(KB):
                    dve.tensor_tensor(buf[:, k, :], buf[:, k, :], rstd[:, :], ALU.mult).then_inc(*normed.on(ph, (st, k)))

            def rms_apply(ph, st, dst, src, g, n_k, n=S):
                root_inverse(ph, st, n)
                for k in range(n_k):
                    dve.scalar_tensor_tensor(dst(k), src(k), g(k), rstd[:, 0:n], ALU.mult,
                                             ALU.mult).then_inc(*normed.on(ph, (st, k)))

            def residual(ph, st, src, g):
                root_inverse(ph, st)
                for k in range(KB):
                    dve.scalar_tensor_tensor(tmp[:, k % 2, :], src[:, k, :], lv(g, k), rstd[:, :], ALU.mult,
                                             ALU.mult).then_inc(*upd.on(ph, (st, k)))
                    dve.wait_ge(*upd.by(ph, (st, k)))
                    dve.tensor_tensor(x[:, k, :], x[:, k, :], tmp[:, k % 2, :], ALU.add).then_inc(*x_new.on(ph, (st, k)))

            ada_chunks = {g[1:]: c for c, g in enumerate(LAST_USE["A"][::PER_CHUNK]) if g[0] == "ada"}

            def ada_rows(g):
                for k in range(KB):
                    slot, s, v = chunk_value(A, ada_chunks[g, k])
                    dve.wait_ge(s, v)
                    w, c = ring[:, slot, :], silu_c[:, k:k + 1]
                    if k == 0:
                        dve.tensor_scalar(ada_sum[g], w, c, None, ALU.mult).then_inc(*ada_step.on(A, (g, k)))
                    else:
                        dve.wait_ge(*ada_step.by(A, (g, k - 1)))
                        dve.scalar_tensor_tensor(ada_sum[g], w, c, ada_sum[g], ALU.mult,
                                                 ALU.add).then_inc(*ada_step.on(A, (g, k)))

            def ada(g):
                acc, free = full(A, f"ada{g}")
                lo = 16 * g
                dve.tensor_tensor(mod[:, lo:lo + 16], acc[:, 0:16],
                                  vec[:, VEC["b_ada"] + lo:VEC["b_ada"] + lo + 16], ALU.add).then_inc(*free.on(A, f"ada{g}"))
                dve.wait_ge(*free.by(A, f"ada{g}"))
                dve.tensor_scalar(mod1[:, lo:lo + 16], mod[:, lo:lo + 16], 1.0, None, ALU.add).then_inc(*mod_ready.on(A, g))

            def attention(ph, extra=None):
                name = ph.name
                tl = TILES[name]

                def inverse(i):
                    dve.wait_ge(*exp_done.by(ph, i))
                    dve.reciprocal(stat[:, 2, i % 4:i % 4 + 1], stat[:, 1, i % 4:i % 4 + 1]).then_inc(*rden_ready.on(ph, i))

                def scores(i):
                    kind, hp, half, t = tl[i]
                    nm, far = stat[:, 0, i % 4:i % 4 + 1], stat[:, 3, i % 4:i % 4 + 1]
                    n = key_chunks(kind, t) * P
                    p = probs[name][i % 3]
                    s = score[:, i % 2, :]
                    if kind == "fa":
                        hd = 2 * hp + half
                        dve.scalar_tensor_tensor(p[:, 0:n], gat[:, hd % 2, 0:n], cumq[:, t, hd:hd + 1], s[:, 0:n],
                                                 ALU.add, ALU.add).then_inc(*score_step.on(ph, (i, 0)))
                        dve.wait_ge(*score_step.by(ph, (i, 0)))
                        dve.tensor_tensor(p[:, n - P:n], p[:, n - P:n], causal, ALU.add).then_inc(*score_step.on(ph, (i, 1)))
                        dve.wait_ge(*score_step.by(ph, (i, 1)))
                        dve.tensor_reduce(nm, p[:, 0:n], AX_X, ALU.max).then_inc(*score_step.on(ph, (i, 2)))
                        dve.wait_ge(*score_step.by(ph, (i, 2)))
                        dve.tensor_scalar(nm, nm, -1.0, None, ALU.mult).then_inc(*scored.on(ph, i))
                    elif kind == "na":
                        hd = 2 * hp + half
                        lo = (2 * TT - 2 - 2 * t) * GRID_W
                        dve.tensor_tensor_reduce(p[:, 0:n], s, nab[:, hd % 2, lo:lo + S], -1.0, BIG, ALU.add, ALU.min,
                                                 nm).then_inc(*scored.on(ph, i))
                    elif kind == "dil":
                        dve.tensor_tensor_reduce(p[:, 0:S], score_flat[:, 0:S], dil[:, half, 3 - t:3 - t + S], -1.0, BIG,
                                                 ALU.add, ALU.min, nm).then_inc(*score_step.on(ph, (i, 0)))
                        dve.tensor_tensor_reduce(p[:, S:n], score_flat[:, S:n], dil[:, half, S + 3:], -1.0, BIG,
                                                 ALU.add, ALU.min, far).then_inc(*score_step.on(ph, (i, 1)))
                        dve.wait_ge(*score_step.by(ph, (i, 1)))
                        dve.tensor_tensor(nm, nm, far, ALU.min).then_inc(*scored.on(ph, i))
                    else:
                        dve.tensor_reduce(nm, s[:, 0:n], AX_X, ALU.max).then_inc(*score_step.on(ph, (i, 0)))
                        dve.wait_ge(*score_step.by(ph, (i, 0)))
                        dve.tensor_scalar(nm, nm, -1.0, None, ALU.mult).then_inc(*scored.on(ph, i))

                def gather(j):
                    i, c0, n = ROUNDS[name][j]
                    dve.wait_ge(*t_done.by(ph, j))
                    if j >= 2:
                        dve.wait_ge(*pv_done.by(ph, j - 2))
                    dve.tensor_copy(probsT[name][j % 2][:, 0:n * P], trans[:, 0, 0:n * P]).then_inc(*pt_ready.on(ph, j))

                n = len(tl)
                for i in range(n + 2):
                    if i < n:
                        kind = tl[i][0]
                        dve.wait_ge(*qk_done.by(ph, i))
                        if kind == "na" and i % TT == 0:
                            dve.wait_ge(*nab_ready.by(ph, i // TT))
                        if kind == "fa" and i % TT == 0:
                            hd = i // TT
                            dve.wait_ge(*lin_free[bank_of["A"][f"nc{hd}"]].by(A, f"nc{hd}"))
                        if i >= 3 and kind != "mem":
                            dve.wait_ge(*t_done.by(ph, ROUNDS_OF[name][i - 3][-1]))
                    if 1 <= i <= n:
                        inverse(i - 1)
                    elif name == "L" and i == 0:
                        dve.memset(stat[:, 3, :], BIG)
                    if i < n:
                        scores(i)
                    if i >= 2:
                        for j in ROUNDS_OF[name][i - 2]:
                            gather(j)

            for dst, val in ((ones_d[:, :], 1.0 / D), (eps[:, 0:1], LN_EPS),
                             (eps[:, 1:2], RMS_EPS), (eps[:, 2:3], 1.0), (one_row, 1.0), (ones[:, :], 1.0)):
                step(dve.memset(dst, val))

            dve.wait_ge(vec_in_s, 16)
            lamv = vec[:, VEC["lam"]:VEC["lam"] + 4]
            dve.tensor_scalar(lam[:, 0, :], lamv, -1.0, None, ALU.mult).then_inc(*sp_step.on(A, "neg"))
            dve.wait_ge(*sp_step.by(A, "neg"))
            dve.tensor_tensor(lam[:, 1, :], lamv, lam[:, 0, :], ALU.max).then_inc(*sp_step.on(A, "abs"))
            dve.wait_ge(x_in, 16)
            centre(A, "ln1", x, h)
            dve.wait_ge(act_step, 1)
            ada_rows(0)
            scale_all(A, "ln1", h)
            dve.wait_ge(*sp_step.by(A, "ln"))
            dve.scalar_tensor_tensor(lam[:, 3, :], lam[:, 0, :], 0.0, lam[:, 3, :], ALU.max,
                                     ALU.add).then_inc(*sp_step.on(A, "sp"))
            dve.wait_ge(*sp_step.by(A, "sp"))
            dve.tensor_scalar(lam[:, 4, :], lam[:, 3, :], LRU_C, None, ALU.mult).then_inc(*sp_step.on(A, "c"))
            dve.tensor_scalar(lam[:, 5, :], lam[:, 3, :], -LRU_C, None, ALU.mult).then_inc(*sp_step.on(A, "nc"))
            rms_apply(A, "mem", lambda k: mem[:, k, :], lambda k: mem[:, k, :], lambda k: v_("mem_g", k), KB, N_MEM)
            ada(0)
            for m in range(4):
                ins = dve.memset(xbp[m][:, 0:CONV - 1], 0.0)
                if m < 3:
                    step(ins)
            ins.then_inc(*pad_done.on(A, 0))
            acc, free = full(A, "f")
            dve.tensor_scalar(fl, acc[0:HEADS, :], v_("b_f")[0:HEADS, :], None, ALU.add).then_inc(*free.on(A, "f"))
            dve.wait_ge(*free.by(A, "f"))
            step(dve.tensor_scalar(fl2, fl, -1.0, None, ALU.mult))
            dve.tensor_tensor(fl2, fl2, fl, ALU.max).then_inc(*f_step.on(A, "abs"))
            dve.wait_ge(*f_step.by(A, "ln"))
            dve.scalar_tensor_tensor(fl2, fl, 0.0, fl2, ALU.min, ALU.subtract).then_inc(*f_step.on(A, "ls"))
            dve.wait_ge(*f_step.by(A, "ls"))
            dve.tensor_tensor_scan(fl, one_row, fl2, 0.0, ALU.mult, ALU.add).then_inc(*f_step.on(A, "cum"))
            dve.wait_ge(*f_step.by(A, "cum"))
            dve.tensor_scalar(ncum, fl, -1.0, None, ALU.mult).then_inc(*f_step.on(A, "neg"))
            for m in range(4):
                b = bank_of["A"][f"xb{m}"]
                dve.wait_ge(*lin_free[b].by(A, f"xb{m}"))
                dve.tensor_scalar(xc[:, m, :], xbp[m][:, 0:S], v_("conv_w", m), v_("conv_b", m), ALU.mult,
                                  ALU.add).then_inc(*conv.on(A, (m, 0)))
                for j in range(1, CONV):
                    dve.wait_ge(*conv.by(A, (m, j - 1)))
                    dve.scalar_tensor_tensor(xc[:, m, :], xbp[m][:, j:j + S], v_("conv_w", 4 * j + m), xc[:, m, :],
                                             ALU.mult, ALU.add).then_inc(*conv.on(A, (m, j)))
            for g in (1, 2):
                ada_rows(g)
            for g in (1, 2):
                ada(g)
            for m in range(4):
                dve.wait_ge(*lru_act.by(A, ("a2", m)))
                dve.scalar_tensor_tensor(r_[:, m, :], a2[:, m, :], 1.0, r_[:, m, :], ALU.add,
                                         ALU.mult).then_inc(*lru_dve.on(A, ("u2", m)))
            for m in range(4):
                dve.tensor_tensor(ig[:, m, :], ig[:, m, :], xc[:, m, :], ALU.mult).then_inc(*lru_dve.on(A, ("igx", m)))
            for m in range(4):
                dve.wait_ge(*lru_dve.by(A, ("igx", m)))
                dve.wait_ge(*lru_act.by(A, ("sqrt", m)))
                dve.tensor_tensor(ig[:, m, :], ig[:, m, :], r_[:, m, :], ALU.mult).then_inc(*lru_dve.on(A, ("u", m)))
            for m in range(4):
                dve.wait_ge(*lru_dve.by(A, ("u", m)))
                dve.tensor_tensor_scan(a2[:, m, :], a_[:, m, :], ig[:, m, :], 0.0, ALU.mult,
                                       ALU.add).then_inc(*lru_dve.on(A, ("scan", m)))
            for m in range(4):
                dve.wait_ge(*lru_dve.by(A, ("scan", m)))
                dve.tensor_tensor(xc[:, m, :], a2[:, m, :], gg[:, m, :], ALU.mult).then_inc(*lru_dve.on(A, ("out", m)))
            rms_apply(A, "lru", lambda k: xc[:, k, :], lambda k: xc[:, k, :], lambda k: v_("g_lru", k), 4)
            acc, free = full(A, "cumT")
            dve.tensor_copy(cumq[:, :, :].rearrange("p a b -> p (a b)"), acc[:, 0:TT * HEADS]).then_inc(*free.on(A, "cumT"))
            dve.wait_ge(*free.by(A, "cumT"))
            dve.wait_ge(zeros_out, 32)
            attention(A)
            rms_apply(A, "attn", lambda k: y[:, k, :], lambda k: y[:, k, :], lambda k: v_("g_attn", k), 4)
            for m in range(KB):
                acc, free = full(A, f"out{m}")
                dve.tensor_scalar(tmp[:, m % 2, :], acc, mod1[:, 16 + m:17 + m], None, ALU.mult).then_inc(*free.on(A, f"out{m}"))
                dve.wait_ge(*free.by(A, f"out{m}"))
                dve.scalar_tensor_tensor(x[:, m, :], x[:, m, :], ALPHA, tmp[:, m % 2, :], ALU.mult,
                                         ALU.add).then_inc(*x_new.on(A, ("mix", m)))
            dve.wait_ge(*x_new.by(A, ("mix", KB - 1)))
            centre(A, "ln2", x, x)
            scale_all(A, "ln2", x)
            centre(A, "ln3", x, h)
            scale_all(A, "ln3", h)
            for half in range(2):
                acc, free = full(A, f"rt{half}")
                dve.tensor_tensor(rtv(0)[:, half * 40:half * 40 + 40], acc[:, 0:40],
                                  route_b[:, half * 40:half * 40 + 40], ALU.add).then_inc(*free.on(A, f"rt{half}"))
            for half in range(2):
                dve.wait_ge(*lin_free[bank_of["A"][f"rt{half}"]].by(A, f"rt{half}"))

            def q4(i):
                return rtv(i).rearrange("p (a b) -> p a b", b=4)

            def col(i, n=20):
                return rtv(i)[:, 0:n]

            def spread(ap, n=20, w=4):
                return ap.unsqueeze(2).to_broadcast([P, n, w])
            step(dve.tensor_reduce(col(2), q4(0), AX_X, ALU.max))
            dve.tensor_tensor(q4(1), q4(0), spread(col(2)), ALU.subtract).then_inc(*route_sub.on(A, 0))
            dve.wait_ge(*route_exp.by(A, 0))
            step(dve.tensor_reduce(col(2), q4(1), AX_X, ALU.add))
            step(dve.reciprocal(col(3), col(2)))
            step(dve.tensor_tensor(q4(4), q4(1), spread(col(3)), ALU.mult))
            step(dve.memset(rtv(5), 0.0))
            for i in range(4):
                for lo, hi, op in ((0, i, ALU.is_gt), (i + 1, 4, ALU.is_ge)):
                    if hi > lo:
                        w = hi - lo
                        step(dve.tensor_tensor(q4(6)[:, :, 0:w], q4(4)[:, :, i:i + 1].to_broadcast([P, 20, w]),
                                               q4(4)[:, :, lo:hi], op))
                        step(dve.tensor_tensor(q4(5)[:, :, lo:hi], q4(5)[:, :, lo:hi], q4(6)[:, :, 0:w], ALU.add))
            step(dve.tensor_scalar(rtv(7), rtv(5), 0.5, None, ALU.is_lt))
            step(dve.tensor_tensor(rtv(7), rtv(7), rtv(4), ALU.mult))
            step(dve.tensor_scalar(rtv(8), rtv(5), 1.5, None, ALU.is_lt))
            step(dve.tensor_tensor(rtv(8), rtv(8), rtv(4), ALU.mult))
            step(dve.tensor_reduce(col(2), q4(8), AX_X, ALU.add))
            step(dve.reciprocal(col(3), col(2)))
            step(dve.tensor_tensor(q4(9), q4(8), spread(col(3)), ALU.mult))

            def by_token(i):
                return rtv(i).rearrange("p (t g j) -> p t g j", t=TT, j=4)
            def experts(i):
                return by_token(i)[:, :, 1:5, :]

            def of_group(i):
                return by_token(i)[:, :, 0, :].unsqueeze(3).to_broadcast([P, TT, 4, 4])

            def r4(i):
                return rw(i).rearrange("p (t g j) -> p t g j", t=TT, j=4)

            def r3(i):
                return rw(i).rearrange("p (t e) -> p t e", t=TT)

            def row(i):
                return rw(i)[:, 0:EXPERTS]

            def per_expert(ap):
                return ap.unsqueeze(1).to_broadcast([P, TT, EXPERTS])
            step(dve.tensor_tensor(r4(3), experts(9), of_group(7), ALU.mult))
            step(dve.tensor_scalar(rtv(10), rtv(5), 0.5, None, ALU.is_lt))
            step(dve.tensor_scalar(rtv(11), rtv(5), 1.5, None, ALU.is_lt))
            step(dve.tensor_tensor(r4(1), experts(10), of_group(10), ALU.mult))
            dve.tensor_tensor(r4(0), experts(11), of_group(10), ALU.mult).then_inc(*route_ready.on(A, "chosen"))
            dve.wait_ge(*route_ready.by(A, "chosen"))
            step(dve.tensor_tensor(rw(2), rw(0), rw(1), ALU.subtract))
            acc, free = full(A, "pos")
            dve.tensor_copy(gat_flat[:, 4 * 64:4 * 64 + 80], acc[:, 0:80]).then_inc(*free.on(A, "pos"))
            dve.wait_ge(*free.by(A, "pos"))
            pos, counts = r3(4), row(5)
            step(dve.tensor_scalar(row(6), counts, float(P), None, ALU.is_gt))
            for k in range(2, TT):
                step(dve.scalar_tensor_tensor(row(6), counts, float(k * P), row(6), ALU.is_gt, ALU.add))
            step(dve.tensor_tensor_scan(row(7), ones[:, 0:EXPERTS], row(6), 0.0, ALU.mult, ALU.add))
            step(dve.tensor_tensor(row(8), row(7), row(6), ALU.subtract))
            step(dve.scalar_tensor_tensor(row(8), row(8), float(P), spill_slot, ALU.mult, ALU.add))
            step(dve.tensor_scalar(rw(9), rw(4), float(P), None, ALU.is_ge))
            step(dve.tensor_tensor(r3(9), r3(9), per_expert(row(8)), ALU.mult))
            step(dve.tensor_tensor(r3(10), pos, per_expert(own_slot), ALU.add))
            step(dve.tensor_tensor(rw(9), rw(9), rw(10), ALU.add))
            for i in range(2):
                for src, dst in ((9, rw(11)[:, i * TT:(i + 1) * TT]), (3, weight[:, i * TT:(i + 1) * TT])):
                    step(dve.tensor_tensor(rw(12), rw(1 + i), rw(src), ALU.mult))
                    step(dve.tensor_reduce(dst, r3(12), AX_X, ALU.add))
            dve.tensor_copy(slots[:, :], rw(11)[:, 0:2 * TT]).then_inc(*route_ready.on(A, "slots"))
            n = 12
            t3 = big[0:1, 0, 0:n * EXPERTS].rearrange("p (a b) -> p a b", a=n)
            step(dve.tensor_tensor(t3, row(7)[0:1, :].unsqueeze(1).to_broadcast([1, n, EXPERTS]),
                                   count_row[0:1, 0:n].unsqueeze(2).to_broadcast([1, n, EXPERTS]), ALU.is_le))
            step(dve.tensor_reduce(rw(13)[0:1, 0:n], t3, AX_X, ALU.add))
            step(dve.tensor_scalar(rw(13)[0:1, 0:n], rw(13)[0:1, 0:n], EXPERTS - 1.0, None, ALU.min))
            dve.tensor_copy(spill[0:1, 0:n], rw(13)[0:1, 0:n]).then_inc(*o_free[0].on(A, "table"))
            total = row(7)[0:1, EXPERTS - 1:EXPERTS]
            acc1 = rw(14)[0:1, 0:1]
            step(dve.tensor_scalar(acc1, total, 2.0, 1.0, ALU.is_gt, ALU.add))
            for k in range(2, MAX_TRIPS):
                step(dve.scalar_tensor_tensor(acc1, total, 2.0 * k, acc1, ALU.is_gt, ALU.add))
            dve.tensor_copy(trips[:, :], acc1).then_inc(*o_free[1].on(A, "trips"))
            dve.wait_ge(*o_free[1].by(A, "trips"))
            n_trips = dve.value_load(trips[0:1, 0:1], min_val=1, max_val=MAX_TRIPS)

            def expert_tile(ph, e):
                acc, free = full(ph, f"up{e}")
                dve.wait_ge(*emptied(ph, f"gate{e}").by(ph, f"gate{e}"))
                dve.tensor_tensor(hid[e % 2], sil[e % 2], acc, ALU.mult).then_inc(*free.on(ph, f"up{e}"))
                turned(ph, f"xt{e}", (e + 1) % 2)

            def turned(ph, g, buf):
                for i in range(2):
                    acc, free = full(ph, f"{g}.{i}")
                    dve.tensor_copy(xg_flat[buf][:, i, :], acc).then_inc(*free.on(ph, f"{g}.{i}"))
            turned(A, "xt", 0)
            with dve.Fori(0, M_TRIPS) as g:
                for e in range(TILES_PER_TRIP):
                    expert_tile(Phase("M", g), e)
            with dve.Fori(0, n_trips) as j:
                for e in range(2):
                    expert_tile(Phase("O", j), e)
            dve.wait_ge(picked_in, 16 * 2 * TT)
            for t in range(TT):
                a, b = picked[:, 2 * t, :], picked[:, 2 * t + 1, :]
                dve.tensor_scalar(a, a, weight[:, t:t + 1], None, ALU.mult).then_inc(*picked_sum.on(B, (t, 0)))
                dve.wait_ge(*picked_sum.by(B, (t, 0)))
                dve.scalar_tensor_tensor(b, b, weight[:, TT + t:TT + t + 1], a, ALU.mult,
                                         ALU.add).then_inc(*picked_sum.on(B, (t, 1)))
            for m in range(KB):
                acc, free = full(B, f"yt{m}")
                dve.tensor_scalar(tmp[:, m % 2, :], acc, mod1[:, 40 + m:41 + m], None, ALU.mult).then_inc(*free.on(B, f"yt{m}"))
                dve.wait_ge(*free.by(B, f"yt{m}"))
                dve.scalar_tensor_tensor(x[:, m, :], x[:, m, :], ALPHA, tmp[:, m % 2, :], ALU.mult,
                                         ALU.add).then_inc(*x_new.on(B, ("ffn", m)))
            dve.wait_ge(*x_new.by(B, ("ffn", KB - 1)))
            centre(B, "ln4", x, x)
            scale_all(B, "ln4", x)
            dve.wait_ge(dil_s, 16)

            def split(ph, chunks):
                for c in chunks:
                    dve.wait_ge(*w_high.by(ph, c))
                    slot = c % L_RAW
                    dve.tensor_tensor(ring_r[:, slot, :], ring[:, slot, :], whole(ring_r[:, L_RAW + c % L_HIGH, :]),
                                      ALU.subtract).then_inc(*w_low.on(ph, c))

            def low_part(ph, n, k, dst, src, high):
                dve.wait_ge(*x_high.by(ph, (n, k)))
                dve.tensor_tensor(dst, src, whole(high), ALU.subtract).then_inc(*x_low.on(ph, (n, k)))
            with dve.Fori(0, LAYERS) as l:
                ph = Phase("L", l)

                def normed_parts(st, g):
                    rms_apply(ph, st, lambda k: low[:, k, :], lambda k: x[:, k, :], lambda k: lv(g, k), KB)
                    for k in range(KB):
                        low_part(ph, st, k, low_r[:, k, :], low[:, k, :], h_r[:, k, :])
                dve.wait_ge(lvec_s, l * 16 + 16)
                split(ph, range(L_HIGH))
                normed_parts("pre_mix", "g_pre_mix")
                for g in LIN["L"][:LIN["L"].index("g0.0")]:
                    split(ph, behind.get(g, []))
                attention(ph)
                for k in range(6):
                    low_part(ph, "o", k, ob_r[:, k, :], ob[:, k, :], o_high[:, k, :])
                for m in range(KB):
                    for i, n in enumerate(("ba", "bb", "bm")):
                        j = 3 * m + i
                        gn = f"g{i}.{m}"
                        split(ph, behind.get(gn, []))
                        dve.wait_ge(*lin_free[bank_of["L"][gn]].by(ph, gn))
                        acc, free = full(ph, f"{n}{m}")
                        dst = y[:, m, :] if i == 0 else tmp[:, i - 1, :]
                        dve.tensor_tensor(dst, acc, gat[:, j % 2, :], ALU.mult).then_inc(*free.on(ph, f"{n}{m}"))
                        dve.wait_ge(*free.by(ph, f"{n}{m}"))
                        if i == 1:
                            dve.tensor_tensor(y[:, m, :], y[:, m, :], tmp[:, 0, :], ALU.add).then_inc(*merge_step.on(ph, m))
                        split(ph, behind.get(f"{n}{m}", []))
                    dve.wait_ge(*merge_step.by(ph, m))
                    dve.tensor_tensor(y[:, m, :], y[:, m, :], tmp[:, 1, :], ALU.add).then_inc(*merged.on(ph, m))
                    if m >= 1:
                        low_part(ph, "y", m - 1, y_r[:, m - 1, :], y[:, m - 1, :], y_high[:, m - 1, :])
                low_part(ph, "y", KB - 1, y_r[:, KB - 1, :], y[:, KB - 1, :], y_high[:, KB - 1, :])
                for m in range(KB - 1):
                    split(ph, behind.get(f"out{m}", []))
                residual(ph, "post_mix", h, "g_post_mix")
                split(ph, behind.get(f"out{KB - 1}", []))
                normed_parts("pre_ffn", "g_pre_ffn")
                for j in range(FB):
                    for n, buf in (("a", ffa), ("b", ffb)):
                        f = j if n == "a" else FB + j
                        acc, free = full(ph, f"{n}{j}")
                        dve.wait_ge(*conv_c.by(ph, (n, j)))
                        t = buf[j % 2]
                        dve.scalar_tensor_tensor(t[:, 1:S], acc[:, 0:S - 1], lv("conv_w", f), t[:, 1:S], ALU.mult,
                                                 ALU.add).then_inc(*conv_l.on(ph, (n, j)))
                        dve.wait_ge(*conv_l.by(ph, (n, j)))
                        dve.scalar_tensor_tensor(t[:, 0:S - 1], acc[:, 1:S], lv("conv_w", 4 * FB + f), t[:, 0:S - 1],
                                                 ALU.mult, ALU.add).then_inc(*free.on(ph, f"{n}{j}"))
                        split(ph, behind.get(f"{n}{j}", []))
                    dve.wait_ge(*gelu_ready.by(ph, j))
                    dve.wait_ge(*lin_free[bank_of["L"][f"b{j}"]].by(ph, f"b{j}"))
                    dve.tensor_tensor(big[:, j, :], ffg[j % 2], ffb[j % 2], ALU.mult).then_inc(*ff_ready.on(ph, j))
                    if 2 <= j <= KB + 1:
                        low_part(ph, "f", j - 2, big_r[:, j - 2, :], big[:, j - 2, :], f_high[j - 2])
                for k in range(KB, FB):
                    low_part(ph, "f", k, big_r[:, k, :], big[:, k, :], f_high[k])
                for m in range(KB):
                    split(ph, ahead.get(f"down{m}", []) + behind.get(f"down{m}", []))
                residual(ph, "post_ffn", low, "g_post_ffn")

        @block.gpsimd
        def _(pool):
            def attention(ph, extra=None):
                for i, (kind, hp, half, t) in enumerate(TILES[ph.name]):
                    if extra:
                        extra(i)
                    n = key_chunks(kind, t) * P
                    p = probs[ph.name][i % 3][:, 0:n]
                    pool.wait_ge(*rden_ready.by(ph, i))
                    pool.tensor_tensor(p, p, stat[:, 2, i % 4:i % 4 + 1].to_broadcast([P, n]),
                                       ALU.mult).then_inc(*p_ready.on(ph, i))

            pool.memset(zeros, 0.0).then_inc(*zeros_ready.on(A, 0))
            pool.wait_ge(*zeros_ready.by(A, 0))
            pool.wait_ge(*conv.by(A, (0, 0)))
            pool.dma_start(slots_in.rearrange("(j p) d -> p j d", p=P),
                           zeros.unsqueeze(1).to_broadcast([P, SLOT_TILES, D])).then_inc(zeros_out, 16)
            pool.dma_start(slots_out[(EXPERTS + 2) * P:, :].rearrange("(j p) d -> p j d", p=P),
                           zeros.unsqueeze(1).to_broadcast([P, 2 * MAX_TRIPS - 2, D])).then_inc(zeros_out, 16)
            attention(A)
            pool.wait_ge(*route_ready.by(A, "slots"))
            pool.wait_ge(zeros_out, 32)
            for t in range(TT):
                for i in range(2):
                    pool.wait_ge(*lin_free[bank_of["A"][f"ut{t}.{i}"]].by(A, f"ut{t}.{i}"))
                for i in range(2):
                    pool.indirect_dma_start(slots_in, bass.IndirectOffsetOnAxis(slots[:, i * TT + t:i * TT + t + 1], 0),
                                            u_tok[:, t, :], None).then_inc(rows_out, 16)
            for b in range(2):
                pool.wait_ge(*o_free[b].by(A, ("table", "trips")[b]))
            n_trips = pool.value_load(trips[0:1, 0:1], min_val=1, max_val=MAX_TRIPS)
            pool.wait_ge(xt_in, n_trips * 32 + 16 * (EXPERTS + 2))
            pool.wait_ge(yt_out, n_trips * 32 + 16 * EXPERTS)
            pool.tensor_tensor(held[:, :], eps[:, 2:3], eps[:, 2:3], ALU.mult)
            for t in range(TT):
                for i in range(2):
                    pool.indirect_dma_start(picked[:, 2 * t + i, :], None, slots_out, bass.IndirectOffsetOnAxis(
                        slots[:, i * TT + t:i * TT + t + 1], 0)).then_inc(picked_in, 16)
            pool.wait_ge(consts_in, 16 * 4)
            with pool.Fori(0, LAYERS) as l:
                ph = Phase("L", l)

                def bias(hd):
                    b = nab[:, hd % 2, :].rearrange("p (a b) -> p a b", b=GRID_W)
                    pool.wait_ge(nab_s, l * (16 * NA_HEADS) + 16 * (hd + 1))
                    pool.tensor_tensor(b, b, window.unsqueeze(1).to_broadcast([P, NA_SLOTS, GRID_W]),
                                       ALU.add).then_inc(*nab_ready.on(ph, hd))

                def next_bias(i):
                    if i == 0:
                        bias(0)
                    if i % TT == 2 and i // TT + 1 < NA_HEADS:
                        bias(i // TT + 1)
                attention(ph, extra=next_bias)

            done = Phase("L", None)
            pool.wait_ge(x_new.sem, x_new.count(done, LAYERS * len(x_new.events["L"])))
            pool.dma_start(out, x[:, :, :]).then_inc(out_done, 16)
            pool.wait_ge(out_done, 16)

        for s in signals:
            s.done()


def stationary(w):
    k, m = w.shape
    return w.reshape(k // P, P, m // P, P).transpose(2, 0, 1, 3).reshape(-1, P, P)


def moving(w):
    k, m = w.shape
    return w.reshape(k // P, P, m // P, P).transpose(0, 2, 1, 3).reshape(-1, P, P)


def by_feature(v):
    return np.ascontiguousarray(v.reshape(-1, P).T)


def weight_stream(i):
    w = i["w_in"][0]
    ada = i["w_ada"][0]
    ends = np.cumsum([D_ATTN, D_ATTN, D_ATTN, HEADS, D_ATTN, D_ATTN])
    q, k, v, _, xb, gb = np.split(w, ends[:-1], axis=1)

    def diagonal(g):
        out = np.zeros((4, P, P), np.float32)
        out[:, :DH, :DH], out[:, DH:, DH:] = g[0::2], g[1::2]
        return out
    rows = [moving(ada[:, i * 2048:(i + 1) * 2048]) for i in range(3)]
    parts = [rows[0]] + [stationary(x) for x in (xb, gb)]
    for j, x in enumerate((q, k)):
        x = stationary(x)
        half = 2 * KB
        parts += [x[:half], rows[1 + j][:4 * PER_CHUNK], x[half:], rows[1 + j][4 * PER_CHUNK:]]
    parts += [moving(v)]
    parts += [diagonal(i["w_rg"][0]), diagonal(i["w_ig"][0]), np.zeros((8, P, P), np.float32)]
    parts += [stationary(i["w_out"][0])]
    for e in range(EXPERTS):
        g, u = (stationary(i[n][0, e]).reshape(EB, KB, P, P) for n in ("w_e_gate", "w_e_up"))
        parts += [g.reshape(-1, P, P), u.reshape(-1, P, P), moving(i["w_e_down"][0, e])]
    for l in range(LAYERS):
        w = i["w_in_2"][l]
        ends = np.cumsum([D_A] * 3 + [D_B] * 3 + [D_M] + [D] * 3)
        q_a, k_a, v_a, q_b, k_b, v_b, q_m, g0, g1, g2 = np.split(w, ends[:-1], axis=1)
        parts += [stationary(x) for x in (q_a, k_a, q_b, k_b, q_m)]
        parts += [moving(np.concatenate([v_a, v_b[:, :P]], axis=1)), moving(v_b[:, P:])]
        parts += [stationary(i["w_mem_kv_2"][l][:, :D_M]), moving(i["w_mem_kv_2"][l][:, D_M:])]
        cols = [stationary(x).reshape(KB, -1, P, P) for x in
                (g0, i["w_br_a_2"][l], g1, i["w_br_b_2"][l], g2, i["w_br_m_2"][l])]
        parts += [np.concatenate(cols, axis=1).reshape(-1, P, P), stationary(i["w_out_2"][l])]
        a, b = (stationary(x).reshape(FB, KB, P, P) for x in np.split(i["w_up_2"][l], 2, axis=1))
        parts += [np.stack([a, b], 1).reshape(-1, P, P), stationary(i["w_down_2"][l])]
    blocks = np.concatenate(parts, axis=0)
    assert blocks.shape[0] == N_CHUNKS * PER_CHUNK, (blocks.shape, N_CHUNKS)
    return np.ascontiguousarray(blocks.reshape(N_CHUNKS, PER_CHUNK, P, P).transpose(0, 2, 1, 3)).reshape(
        N_CHUNKS, P, PER_CHUNK * P)


def window_mask():
    c = np.arange(GRID_W)
    start = np.clip(c - NA_KW // 2, 0, GRID_W - NA_KW)
    inside = (c[None, :] >= start[:, None]) & (c[None, :] < start[:, None] + NA_KW)
    return np.where(inside, 0.0, MASKED).astype(np.float32)


def dilated_bias():
    out = np.full((P, 2, DIL_W), MASKED, np.float32)
    slopes = (2.0 ** (-8.0 * np.arange(1, DIL_HEADS + 1, dtype=np.float32) / DIL_HEADS)).astype(np.float32)
    a = np.arange(P)[:, None]
    for b in range(2):
        for g, (w, d) in enumerate(((128, 1), (512, 4), (2048, 16))):
            dist = np.arange(S + 3)[None, :] - 3 - 4 * a if g == 0 else 4 * (np.arange(P)[None, :] - a)
            ok = (np.abs(dist) <= w // 2) & (dist % d == 0)
            bias = np.where(ok, -slopes[2 * g + b] * np.abs(dist).astype(np.float32), MASKED)
            lo = 0 if g == 0 else S + 3 + (g - 1) * P
            out[:, b, lo:lo + bias.shape[1]] = bias
    return out


def neighborhood_bias(rpb):
    c = np.arange(GRID_W)
    reach = 2 * NA_KW - 1
    pad = np.zeros((*rpb.shape[:3], 2 * GRID_W - 1), np.float32)
    lo = GRID_W - 1 - (NA_KW - 1)
    pad[..., lo:lo + reach] = rpb
    full = pad[..., GRID_W - 1 + c[None, :] - c[:, None]]
    full = full.transpose(0, 1, 3, 2, 4)
    both = np.concatenate([full[:, :, :, 1:], full[:, :, :, :-1]], axis=2)
    return np.ascontiguousarray(both).reshape(-1, P, NA_SLOTS * GRID_W)


def kernel(**inputs):
    import concourse.bacc as bacc
    from concourse.bass_utils import run_bass_kernel_spmd

    i = {n: np.asarray(a) for n, a in inputs.items()}

    def blocks(a):
        return np.ascontiguousarray(a.reshape(-1, P, a.shape[1]).transpose(1, 0, 2))
    vec = np.zeros((P, N_VEC), np.float32)
    for n, a in (("c", i["c"][0]), ("b_ada", i["b_ada"][0]), ("conv_w", i["conv_w"][0].reshape(-1)),
                 ("conv_b", i["conv_b"][0]), ("b_rg", i["b_rg"][0]), ("b_ig", i["b_ig"][0]),
                 ("lam", i["lru_lambda"][0]), ("g_attn", i["g_attn"][0]), ("g_lru", i["g_lru"][0]),
                 ("ln1_g", i["ln1_g"][0]), ("ln1_b", i["ln1_b"][0]), ("ln2_g", i["ln2_g"][0]),
                 ("ln2_b", i["ln2_b"][0]), ("mem_g", i["mem_norm_g_2"])):
        b = by_feature(a)
        vec[:, VEC[n]:VEC[n] + b.shape[1]] = b
    vec[:HEADS, VEC["b_f"]] = i["b_f"][0]
    lvec = np.zeros((LAYERS, P, N_LVEC), np.float32)
    for l in range(LAYERS):
        for n, a in (("g_pre_mix", i["g_pre_mix_2"]), ("b_gate", i["b_gate_2"]), ("g_post_mix", i["g_post_mix_2"]),
                     ("g_pre_ffn", i["g_pre_ffn_2"]), ("conv_w", i["conv_w_2"]), ("conv_b", i["conv_b_2"]),
                     ("g_post_ffn", i["g_post_ffn_2"])):
            b = by_feature(a[l].reshape(-1))
            lvec[l, :, LVEC[n]:LVEC[n] + b.shape[1]] = b
    q, e = np.arange(P), np.arange(EXPERTS)
    rows = np.concatenate([P * e, P * (EXPERTS - 1) - P * e, e])
    const = np.concatenate([np.eye(P, dtype=np.float32),
                            np.where(q[None, :] <= q[:, None], 0.0, MASKED).astype(np.float32),
                            np.where(q[:, None] < q[None, :], 1.0, 0.0).astype(np.float32),
                            np.concatenate([window_mask()] * 2, axis=0),
                            np.tile(rows.astype(np.float32), (P, 1))], axis=1)
    route_w = np.concatenate([i["w_grp"][0], i["w_exp"][0]], axis=1)
    route_b = np.concatenate([i["b_grp"][0], i["b_exp"][0]])
    f0 = 3 * D_ATTN
    arrays = {
        "weights": weight_stream(i),
        "xT": blocks(i["x"][0].T),
        "memT": blocks(i["mem_2"][0].T),
        "vec": vec,
        "lvec": lvec,
        "w_forget": blocks(i["w_in"][0][:, f0:f0 + HEADS]),
        "w_route": blocks(route_w),
        "b_route": np.ascontiguousarray(np.tile(route_b, (P, TT))),
        "na_bias": neighborhood_bias(i["rpb_na_2"]),
        "const": const,
        "dil_bias": dilated_bias(),
    }
    nc = bacc.Bacc("TRN2", target_bir_lowering=False, num_devices=1)
    args = [nc.dram_tensor(f"in_{n}", a.shape, F32, kind="ExternalInput").ap() for n, a in arrays.items()]
    out = nc.dram_tensor("outT", (P, KB, S), F32, kind="ExternalOutput").ap()
    slots_in = nc.dram_tensor("slots_in", (SLOT_TILES * P, D), F32).ap()
    slots_out = nc.dram_tensor("slots_out", ((EXPERTS + 2 * MAX_TRIPS) * P, D), F32).ap()
    build(nc, args[0], slots_in, slots_out, *args[1:], out)
    r = run_bass_kernel_spmd(nc, [{f"in_{n}": a for n, a in arrays.items()}], core_ids=[0])
    got = r.results[0]["outT"]
    return np.ascontiguousarray(got.transpose(2, 1, 0)).reshape(1, S, D)
```

```python
from contextlib import ExitStack

import numpy as np
import concourse.bass as bass
from concourse import mybir

F32 = mybir.dt.float32
F32R = mybir.dt.float32r
U32 = mybir.dt.uint32
ALU = mybir.AluOpType
ACT = mybir.ActivationFunctionType
AX_X = mybir.AxisListType.X

P = 128
S = 512
D = 1024
KB = D // P
TT = S // P
DH = 64
D_ATTN = 512
HEADS = 8
CONV = 4
N_GROUPS, PER_GROUP = 4, 4
EXPERTS = N_GROUPS * PER_GROUP
D_EXPERT = 512
EB = D_EXPERT // P
ALPHA = 2.0 ** 0.25
LN_EPS, RMS_EPS = 1e-5, 1e-6
LRU_C = 8.0
LAYERS = 2
GRID_W = 64
ROWS = S // GRID_W
NA_HEADS, NA_KH, NA_KW = 6, 8, 16
DIL_HEADS, DIL_G = 6, 3
MEM_HEADS, N_MEM = 4, 256
D_A, D_B, D_M = 384, 384, 256
D_FF = 2816
FB = D_FF // P
MASKED = -1e30
BIG = 3.0e38

RING = 6
PER_CHUNK = 16
TILE_GROUPS = [("gate", ""), ("up", ""), ("xt", ".0"), ("down", ".0"), ("xt", ".1"), ("down", ".1")]
TILES_PER_TRIP = 4
TILE_CHUNKS = 3 * EB * KB // PER_CHUNK
MAX_SPILL = (2 * S - 1) // P
MAX_TRIPS = (MAX_SPILL + 1) // 2
SLOT_TILES = EXPERTS + 2 * MAX_TRIPS + 2
GATES = [f"g{j % 3}.{j // 3}" for j in range(3 * KB)]
BRANCHES = [f"{('ba', 'bb', 'bm')[j % 3]}{j // 3}" for j in range(3 * KB)]
BRANCH_BLOCKS = [D_A // P, 1, D_M // P]
GATES_AHEAD = 4
STREAM = {
    "A": [(("ada", 0, k), PER_CHUNK) for k in range(KB)]
    + [x for i, (n, m) in enumerate((n, m) for n in ("xb", "gb") for m in (0, 2)) for x in
       [(f"{n}{m}", KB), (f"{n}{m + 1}", KB)] + [(("ada", 1, 2 * i + k), PER_CHUNK) for k in range(2)]]
    + [(f"{n}{m}", 1) for n in ("r", "i") for m in range(4)] + [("i3", 8)]
    + [(f"{n}{m}", KB) for n in ("q", "k") for m in range(4)] + [("v3", 4 * KB)]
    + [(f"out{m}", KB) for m in range(4)] + [(("ada", 2, k), PER_CHUNK) for k in range(2)]
    + [(f"out{m}", KB) for m in range(4, KB)] + [(("ada", 2, k), PER_CHUNK) for k in range(2, KB)],
    "M": [x for e in range(TILES_PER_TRIP)
          for x in ((f"gate{e}", EB * KB), (f"up{e}", EB * KB), (f"down{e}.1", EB * KB))],
    "L": [(f"qk{m}", KB) for m in range(14)] + [(f"km{m}", KB) for m in range(2)]
    + [("va3", 4 * KB), ("vm1", 2 * KB), ("vb3", 2 * KB)]
    + [(g, KB) for g in GATES[:GATES_AHEAD]]
    + [x for j, b in enumerate(BRANCHES) for x in
       [(b, BRANCH_BLOCKS[j % 3])] + [(g, KB) for g in GATES[j + GATES_AHEAD:j + GATES_AHEAD + 1]]]
    + [(f"out{m}", KB) for m in range(KB)]
    + [(f"{n}{j}", KB) for j in range(FB) for n in ("a", "b")]
    + [(f"down{m}", FB) for m in range(KB)],
}
LIN = {
    "A": ["ada0", "f"] + [f"{n}{m}" for n in ("xb", "gb") for m in range(4)] + ["ada1"]
    + [f"{n}{m}" for n in ("r", "i", "q", "k", "v") for m in range(4)] + ["cumT"]
    + [f"nc{h}" for h in range(HEADS)] + [f"out{m}" for m in range(KB)] + ["ada2", "rt0", "rt1", "pos"]
    + [f"ut{t}.{i}" for t in range(TT) for i in range(2)] + ["xt.0", "xt.1"],
    "M": [f"{n}{e}{i}" for e in range(TILES_PER_TRIP) for n, i in TILE_GROUPS],
    "O": [f"{n}{e}{i}" for e in range(2) for n, i in TILE_GROUPS],
    "B": [f"yt{m}" for m in range(KB)],
    "L": [f"qk{m}" for m in range(14)] + ["km0", "km1"] + [f"va{t}" for t in range(TT)] + ["vm0", "vm1"]
    + [f"vb{r}" for r in range(4)]
    + GATES[:GATES_AHEAD]
    + [x for j, b in enumerate(BRANCHES) for x in [b] + GATES[j + GATES_AHEAD:j + GATES_AHEAD + 1]]
    + [f"out{m}" for m in range(KB)] + [f"{n}{j}" for j in range(FB) for n in ("a", "b")]
    + [f"down{m}" for m in range(KB)],
}
M_TRIPS = EXPERTS // TILES_PER_TRIP
TRIPS = {"A": 1, "M": M_TRIPS, "O": 0, "B": 1, "L": LAYERS}
ORDER = ["A", "M", "O", "B", "L"]
LAST_USE = {ph: [n for n, k in s for _ in range(k)] for ph, s in STREAM.items()}
CHUNKS = {ph: len(b) // PER_CHUNK for ph, b in LAST_USE.items()}
FIRST_CHUNK = {"A": 0, "M": CHUNKS["A"], "L": CHUNKS["A"] + M_TRIPS * CHUNKS["M"]}
RAW = 4
HIGH = RING - RAW
WHOLE = ("ada", "r", "i", "km", "vm")
SPLIT = {ph: [c for c in range(CHUNKS[ph]) if not isinstance(g := LAST_USE[ph][c * PER_CHUNK], tuple)
              and g.rstrip("0123456789") not in WHOLE] for ph in ("A", "L")}
HIGH_SLOT = {ph: {c: RAW + i % HIGH for i, c in enumerate(v)} for ph, v in SPLIT.items()}
FORMER = {ph: dict(zip(v[HIGH:], v)) for ph, v in SPLIT.items()}
assert CHUNKS["L"] % RAW == 0 and len(SPLIT["L"]) % HIGH == 0 and CHUNKS["M"] % RING == 0
MID = [c for c in range(CHUNKS["L"] - 1) if LAST_USE["L"][(c + 1) * PER_CHUNK - 1] == LAST_USE["L"][(c + 1) * PER_CHUNK]
       and LAST_USE["L"][c * PER_CHUNK][:4] == "down"]
N_CHUNKS = FIRST_CHUNK["L"] + LAYERS * CHUNKS["L"]
BLOCK0 = {}
for _ph, _s in STREAM.items():
    _n = 0
    BLOCK0[_ph] = {}
    for _name, _k in _s:
        BLOCK0[_ph].setdefault(_name, _n)
        _n += _k
BLOCK0["A"]["v0"] = BLOCK0["A"]["v3"]
BLOCK0["O"] = BLOCK0["M"]
BLOCK0["L"]["va0"], BLOCK0["L"]["vb0"], BLOCK0["L"]["vm0"] = (BLOCK0["L"][n] for n in ("va3", "vb3", "vm1"))

TILES = {
    "A": [("fa", h // 2, h % 2, t) for h in range(HEADS) for t in range(TT)],
    "L": [("na", h // 2, h % 2, t) for h in range(NA_HEADS) for t in range(TT)]
    + [("dil", 0, b, r) for b in range(2) for r in range(4)]
    + [("mem", h // 2, h % 2, t) for h in range(MEM_HEADS) for t in range(TT)],
}


def key_chunks(kind, t):
    return {"fa": t + 1, "na": 4, "dil": 6, "mem": 2}[kind]


NA_TILES = NA_HEADS * TT
GATES_BETWEEN = GATES_AHEAD - 1
GATE_AT = [0]
for _i in range(len(TILES["L"])):
    GATE_AT.append(GATE_AT[-1] + (1 if _i < NA_TILES else 2))
assert GATE_AT[-1] == GATES_BETWEEN * 3 * KB
GATE_DONE = {next(i for i, n in enumerate(GATE_AT) if n >= 3 * KB * (j + 1)) + 3: j for j in range(GATES_BETWEEN - 1)}
OUT_DONE = {NA_TILES + 6: (0, 1, 2), NA_TILES + 14: (3,), NA_TILES + 22: (4,)}
ROUNDS = {ph: [(i, c, min(4, key_chunks(x[0], x[3]) - c)) for i, x in enumerate(tl)
               for c in range(0, key_chunks(x[0], x[3]), 4)] for ph, tl in TILES.items()}
ROUNDS_OF = {ph: [[j for j, x in enumerate(rs) if x[0] == i] for i in range(len(TILES[ph]))]
             for ph, rs in ROUNDS.items()}
OUTS = {ph: list(dict.fromkeys((x[0], x[1]) for x in tl)) for ph, tl in TILES.items()}

VEC = {}
_at = 0
for _n, _w in (("c", 8), ("b_ada", 48), ("b_f", 1), ("conv_w", 16), ("conv_b", 4), ("b_rg", 4), ("b_ig", 4),
               ("lam", 4), ("g_attn", 4), ("g_lru", 4), ("ln1_g", 8), ("ln1_b", 8), ("ln2_g", 8), ("ln2_b", 8),
               ("mem_g", 8)):
    VEC[_n] = _at
    _at += _w
N_VEC = _at
LVEC = {}
_at = 0
for _n, _w in (("g_pre_mix", 8), ("b_gate", 24), ("g_post_mix", 8), ("g_pre_ffn", 8), ("conv_w", 3 * 2 * FB),
               ("conv_b", 2 * FB), ("g_post_ffn", 8)):
    LVEC[_n] = _at
    _at += _w
N_LVEC = _at

NA_SLOTS = 2 * ROWS - 2
DIL_W = S + 3 + 2 * P


class Phase:

    def __init__(self, name, reg=None):
        self.name, self.reg = name, reg


class Signal:

    def __init__(self, sem, events, unit=1):
        self.sem, self.unit = sem, unit
        self.events = {ph: list(events.get(ph, [])) for ph in ORDER}
        self.index = {ph: {e: i for i, e in enumerate(v)} for ph, v in self.events.items()}
        self.seen = {ph: set() for ph in ORDER}

    def count(self, ph, n):
        base = 0
        for q in ORDER:
            if q == ph.name:
                break
            base += TRIPS[q] * len(self.events[q])
        c = (base + n) * self.unit
        return c if ph.reg is None else ph.reg * (len(self.events[ph.name]) * self.unit) + c

    def by(self, ph, event):
        return self.sem, self.count(ph, self.index[ph.name][event] + 1)

    def before(self, ph, event):
        return self.sem, self.count(ph, self.index[ph.name][event])

    def on(self, ph, event):
        assert event in self.index[ph.name] and event not in self.seen[ph.name], event
        self.seen[ph.name].add(event)
        return self.sem, self.unit

    def done(self):
        for ph in ORDER:
            assert self.seen[ph] == set(self.events[ph]), (self.sem, ph)


def build(nc, weights, slots_in, slots_out, xT_in, memT_in, vec_in, lvec_in, small_in, route_w_in, route_b_in, na_bias_in,
          const_in, dil_in, out):
    with ExitStack() as ctx:
        def sb(name, shape, dt=F32):
            return ctx.enter_context(nc.sbuf_tensor(name, shape, dt))

        def sb_parts(name, shape):
            buf = sb(name, shape)
            at = nc.sbuf_base - 4 * int(np.prod(shape[1:]))
            return buf, nc.alloc_sbuf_tensor_at(name + "_r", shape, F32R, offset=at)

        def sem(name):
            return ctx.enter_context(nc.semaphore(name))

        ring, ring_r = sb_parts("ring", [P, RING, PER_CHUNK * P])
        x = sb("x", [P, KB, S])
        h, h_r = sb_parts("h", [P, KB, S])
        low, low_r = sb_parts("low", [P, KB, S])
        y, y_r = sb_parts("y", [P, KB, S])
        big, big_r = sb_parts("big", [P, FB, S])
        ob, ob_r = sb_parts("ob", [P, 6, S])
        mem = sb("mem", [P, KB, N_MEM])
        nab = sb("nab", [P, 2, NA_SLOTS * GRID_W])
        dil = sb("dil", [P, 2, DIL_W])
        tmp = sb("tmp", [P, 2, S])
        gat = sb("gat", [P, 2, S])
        sd = sb("sd", [P, S])
        rstd = sb("rstd", [P, S])
        consts = sb("consts", [P, 3 * P + GRID_W + 48])
        ones_d = sb("ones_d", [P, P])
        ones = sb("ones", [P, P])
        vec = sb("vec", [P, N_VEC])
        lvec = sb("lvec", [P, N_LVEC])
        wf = sb("wf", [P, KB, HEADS])
        wr = sb("wr", [P, KB, N_GROUPS + EXPERTS])
        route_b = sb("route_b", [P, TT * 20])
        slots = sb("slots", [P, 2 * TT], U32)
        weight = sb("weight", [P, 2 * TT])
        spill = sb("spill", [1, 16], U32)
        trips = sb("trips", [1, 1], U32)
        mod = sb("mod", [P, 48])
        mod1 = sb("mod1", [P, 48])
        silu_c = sb("silu_c", [P, KB])
        lam = sb("lam", [P, 6, 4])
        cumq = sb("cumq", [P, TT, HEADS])
        stat = sb("stat", [P, 4, 4])

        ident = consts[:, 0:P]
        causal = consts[:, P:2 * P]
        earlier = consts[:, 2 * P:3 * P]
        window = consts[:, 3 * P:3 * P + GRID_W]
        own_slot, spill_slot, count_row = (consts[:, 3 * P + GRID_W + 16 * i:3 * P + GRID_W + 16 * (i + 1)]
                                           for i in range(3))

        eps = sb("eps", [P, 3])

        held = sb("held", [P, 1])

        def mem_sq(k):
            return big[:, k // 2, (k % 2) * N_MEM:(k % 2 + 1) * N_MEM]

        def v_(name, i=0):
            return vec[:, VEC[name] + i:VEC[name] + i + 1]

        def lv(name, i=0):
            return lvec[:, LVEC[name] + i:LVEC[name] + i + 1]

        qT, kT = big[:, 0:4, :], big[:, 4:8, :]
        v_tok = big[:, 8:12, :]
        conv_flat = big[:, 12:17, :].rearrange("p a b -> p (a b)")
        CW = S + CONV - 1
        xbp = [conv_flat[:, m * CW:(m + 1) * CW] for m in range(4)]
        gg = big[:, 17:21, :]
        fl = big[0:HEADS, 21, :]
        fl2 = gat[0:HEADS, 0, :]
        one_row = gat[0:HEADS, 1, :]
        ncum = tmp[0:HEADS, 0, :]
        r_, ig = big[:, 8:12, :], big[:, 12:16, :]
        a_, xc = y[:, 0:4, :], y[:, 4:8, :]
        a2 = xc
        ob_flat = ob[:, :, :].rearrange("p a b -> p (a b)")
        y_flat = y[:, :, :].rearrange("p a b -> p (a b)")
        probs = {"A": [ob_flat[:, i * S:(i + 1) * S] for i in range(3)],
                 "L": [y_flat[:, i * 768:(i + 1) * 768] for i in range(3)]}
        probsT = {"A": [ob_flat[:, (3 + i) * S:(4 + i) * S] for i in range(2)],
                  "L": [y_flat[:, 2304 + i * S:2304 + (i + 1) * S] for i in range(2)]}
        rt = tmp[:, :, :].rearrange("p a b -> p (a b)")

        def rtv(i):
            return rt[:, i * 80:(i + 1) * 80]
        gat_flat = gat[:, :, :].rearrange("p a b -> p (a b)")

        def rw(i):
            return gat_flat[:, i * TT * EXPERTS:(i + 1) * TT * EXPERTS]
        u_tok = y[:, :, :].rearrange("p (t a) b -> p t (a b)", t=TT)
        zeros = nab[:, :, :].rearrange("p a b -> p (a b)")[:, 0:D]
        xt = y[:, 0:2, :].rearrange("p a b -> p (a b)")
        xg = [y[:, 4 + 2 * i:6 + 2 * i, :].rearrange("p a (c q) -> p (a c) q", q=P) for i in range(2)]
        xg_flat = [y[:, 4 + 2 * i:6 + 2 * i, :] for i in range(2)]
        hid = [ob[:, i, :] for i in range(2)]
        yt = ob[:, 2:4, :]
        sil = [gat[:, 0, :], gat[:, 1, :]]
        picked = big[:, 0:16, :].rearrange("p (i a) b -> p i (a b)", i=2 * TT)
        ada_sum = ob[:, 2:6, :].rearrange("p a b -> p (a b)")
        qa, ka, qb, kb = big[:, 0:3, :], big[:, 3:6, :], big[:, 6:9, :], big[:, 9:12, :]
        qm = big[:, 12:14, :]
        kmT = big[:, 14, :].rearrange("p (a b) -> p a b", a=2)
        va = big[:, 15:19, :]
        vb = big[:, 19:21, :].rearrange("p a b -> p (a b)").rearrange("p (r n) -> p r n", r=4)
        vm = big[:, 21, :].rearrange("p (a b) -> p a b", a=2)
        oa, obb, om = ob[:, 0:3, :], ob[:, 3:4, :], ob[:, 4:6, :]
        ffa = [ob[:, i, :] for i in range(2)]
        ffb = [ob[:, 2 + i, :] for i in range(2)]
        ffg = [ob[:, 4 + i, :] for i in range(2)]
        o_high, y_high = big_r[:, 0:6, :], big_r[:, 6:6 + KB, :]
        f_high = [b[:, i, :] for b, n in ((y_r, KB), (h_r, KB), (ob_r, 6)) for i in range(n)]
        assert len(f_high) == FB
        gate_of = [gat[:, 0, :], gat[:, 1, :], sd[:, :], rstd[:, :]]
        assert len(gate_of) == GATES_AHEAD
        squares_of = [b[:, i, :] for b in (tmp, gat) for i in range(2)]

        def whole(ap):
            return ap.bitcast(F32)

        def pb(name, n):
            return ctx.enter_context(nc.psum_tensor(name, [P, n, S], F32))
        lin = pb("lin", 2)
        score = pb("score", 2)
        trans = pb("trans", 1)
        attn = pb("attn", 2)
        sums = pb("sums", 1)
        score_flat = score[:, :, :].rearrange("p a b -> p (a b)")

        x_in, mem_in, consts_in, vec_in_s, dil_s, lvec_s, nab_s = (
            sem(n) for n in ("x_in", "mem_in", "consts_in", "vec_in", "dil_in", "lvec_in", "nab_in"))
        out_done = sem("out_done")
        dve_step, act_step, pool_step = sem("dve_step"), sem("act_step"), sem("pool_step")
        chunk_in = [sem(f"chunk_in{s}") for s in range(RING)]
        raw_in = [sem(f"raw_in{s}") for s in range(RAW)]
        bank_of = {ph: {g: i % 2 for i, g in enumerate(gs)} for ph, gs in LIN.items()}
        assert all(len(g) % 2 == 0 for g in LIN.values())
        lin_full = [Signal(sem(f"lin_full{b}"), {ph: g[b::2] for ph, g in LIN.items() if ph != "O"}) for b in range(2)]
        lin_free = [Signal(sem(f"lin_free{b}"), {ph: g[b::2] for ph, g in LIN.items() if ph != "O"}) for b in range(2)]
        o_full = [Signal(sem(f"spill_full{b}"), {"O": LIN["O"][b::2]}) for b in range(2)]
        o_free = [Signal(sem(f"spill_free{b}"), {"A": [("table", "trips")[b]], "O": LIN["O"][b::2]}) for b in range(2)]
        spill_in = [sem(f"spill_in{s}") for s in range(TILE_CHUNKS)]
        zeros_out, rows_out, picked_in = sem("zeros_out"), sem("rows_out"), [sem(f"picked_in{t}") for t in range(TT)]
        xt_in, yt_out = sem("xt_in"), sem("yt_out")
        signals = lin_full + lin_free + o_full + o_free

        def filled(ph, g):
            return (o_full if ph.name == "O" else lin_full)[bank_of[ph.name][g]]

        def emptied(ph, g):
            return (o_free if ph.name == "O" else lin_free)[bank_of[ph.name][g]]

        def signal(name, **events):
            s = Signal(sem(name), events)
            signals.append(s)
            return s

        def each(names, n):
            return [(s, k) for s in names for k in range(n)]
        NA_ = [s for s in ("ln1", "ln2", "ln3")]
        LS = ["pre_mix", "post_mix", "pre_ffn", "post_ffn"]
        squares = signal("squares", A=each(["ln1", "mem"], 8) + each(["lru", "attn"], 4) + each(["ln2", "ln3"], 8),
                         B=each(["ln4"], 8), L=each(LS, 8))
        mean_full = signal("mean_full", A=NA_, B=["ln4"])
        centred = signal("centred", A=each(NA_, 8), B=each(["ln4"], 8))
        var_full = signal("var_full", A=["ln1", "mem", "lru", "attn", "ln2", "ln3"], B=["ln4"], L=LS)
        sd_ready = signal("sd_ready", A=["ln1", "mem", "lru", "attn", "ln2", "ln3"], B=["ln4"], L=LS)
        rstd_ready = signal("rstd_ready", A=["ln1", "mem", "lru", "attn", "ln2", "ln3"], B=["ln4"], L=LS)
        normed = signal("normed", A=each(["ln1", "mem"], 8) + each(["lru", "attn"], 4) + each(["ln2", "ln3"], 8),
                        B=each(["ln4"], 8), L=each(["pre_mix", "pre_ffn"], 8))
        affine = signal("affine", A=each(NA_, 8), B=each(["ln4"], 8))
        x_new = signal("x_new", A=[("mix", k) for k in range(8)], B=[("ffn", k) for k in range(8)],
                       L=each(["post_mix", "post_ffn"], 8))
        mod_ready = signal("mod_ready", A=[0, 1, 2])
        ada_step = signal("ada_step", A=[(g, k) for g in range(3) for k in range(KB)])
        tiles = {ph: list(range(len(t))) for ph, t in TILES.items()}
        rounds = {ph: list(range(len(r))) for ph, r in ROUNDS.items()}
        qk_done = signal("qk_done", **tiles)
        score_step = signal("score_step", A=[(i, s) for i in tiles["A"] for s in range(3)],
                            L=[(i, s) for i in tiles["L"] for s in range({"na": 0, "dil": 2, "mem": 1}[TILES["L"][i][0]])])
        scored = signal("scored", **tiles)
        exp_done = signal("exp_done", **tiles)
        rden_ready = signal("rden_ready", **tiles)
        p_ready = signal("p_ready", **tiles)
        t_done = signal("t_done", **rounds)
        pt_ready = signal("pt_ready", **rounds)
        pv_done = signal("pv_done", **rounds)
        o_out = signal("o_out", **OUTS)
        nab_ready = signal("nab_ready", L=list(range(NA_HEADS)))
        f_step = signal("f_step", A=["abs", "exp", "ln", "ls", "cum", "neg"])
        sp_step = signal("sp_step", A=["neg", "abs", "exp", "ln", "sp", "c", "nc"])
        pad_done = signal("pad_done", A=[0])
        conv = signal("conv", A=[(m, s) for m in range(4) for s in range(CONV)])
        lru_act = signal("lru_act", A=[(s, m) for s in ("a", "th", "a2", "sqrt") for m in range(4)])
        lru_dve = signal("lru_dve", A=[(s, m) for s in ("igx", "u2", "u", "scan", "out") for m in range(4)])
        route_exp = signal("route_exp", A=[0])
        route_sub = signal("route_sub", A=[0])
        zeros_ready = signal("zeros_ready", A=[0])
        route_ready = signal("route_ready", A=["chosen", "slots"])
        picked_sum = signal("picked_sum", B=[(t, i) for t in range(TT) for i in range(2)])
        merge_step = signal("merge_step", L=list(range(KB)))
        merged = signal("merged", L=list(range(KB)))
        square_sums = signal("square_sums", L=[(st, k) for st in ("post_mix", "post_ffn") for k in range(1, KB)])
        upd = signal("upd", L=each(["post_mix", "post_ffn"], 8))
        conv_c = signal("conv_c", L=[(n, j) for j in range(FB) for n in ("a", "b")])
        conv_l = signal("conv_l", L=[(n, j) for j in range(FB) for n in ("a", "b")])
        gelu_ready = signal("gelu_ready", L=list(range(FB)))
        ff_ready = signal("ff_ready", L=list(range(FB)))
        w_high = signal("w_high", **SPLIT)
        w_low = signal("w_low", **SPLIT)
        w_used = signal("w_used", L=MID)
        part = [(n, k) for n, c in (("pre_mix", KB), ("o", 6), ("y", KB), ("pre_ffn", KB), ("f", FB)) for k in range(c)]
        first_part = each(["ln1"], KB) + each(["lru", "attn"], 4)
        x_high = signal("x_high", A=first_part, L=part)
        x_low = signal("x_low", A=first_part, L=part)

        A, B = Phase("A"), Phase("B")

        def chunk_value(ph, c):
            if ph.name == "A":
                return c % RAW, chunk_in[c % RAW], 16 * (c // RAW + 1)
            if ph.name == "O":
                return c % TILE_CHUNKS, spill_in[c % TILE_CHUNKS], ph.reg * 32 + 16 * (c // TILE_CHUNKS + 1)
            if ph.name == "L":
                return c % RAW, raw_in[c % RAW], ph.reg * (16 * CHUNKS["L"] // RAW) + 16 * (c // RAW + 1)
            slot = c % RING
            before = len(range(slot, CHUNKS["A"], RAW)) if slot < RAW else 0
            return slot, chunk_in[slot], ph.reg * (16 * CHUNKS["M"] // RING) + 16 * (before + c // RING + 1)

        def used_up(ph, c):
            if ph.name == "L" and c in MID:
                return w_used.by(ph, c)
            g = LAST_USE[ph.name][(c + 1) * PER_CHUNK - 1]
            if g[0] == "ada":
                return ada_step.by(ph, g[1:])
            return lin_full[bank_of[ph.name][g]].by(ph, g)

        behind, ahead = {}, {}
        for ph, former in FORMER.items():
            for c, f in former.items():
                g = LAST_USE[ph][(f + 1) * PER_CHUNK - 1]
                (ahead if ph == "L" and f in MID else behind).setdefault((ph, g), []).append(c)

        q_chunks = behind.pop(("A", "gb1")) + behind.pop(("A", "gb3"))

        block = ctx.enter_context(nc.Block())

        @block.sync
        def _(sp):
            def load(slot, c):
                sp.dma_start(ring[:, slot, :], weights[c]).then_inc(chunk_in[slot], 16)

            def used(ph, c):
                sp.wait_ge(*used_up(ph, c))

            for c in range(CHUNKS["A"]):
                if c >= RAW:
                    used(A, c - RAW)
                load(c % RAW, c)
            for slot in range(RING):
                used(A, [c for c in range(CHUNKS["A"]) if (c % RAW if slot < RAW else HIGH_SLOT["A"].get(c)) == slot][-1])
                load(slot, FIRST_CHUNK["M"] + slot)
            with sp.Fori(0, M_TRIPS - 1) as g:
                ph = Phase("M", g)
                for c in range(CHUNKS["M"]):
                    used(ph, c)
                    load(c % RING, g * CHUNKS["M"] + (FIRST_CHUNK["M"] + RING + c))

            def used_last(name, c):
                event = LAST_USE[name][(c + 1) * PER_CHUNK - 1]
                s = lin_full[bank_of[name][event]]
                if name == "L" and c in MID:
                    s, event = w_used, c
                former_trips = (TRIPS[name] - 1) * len(s.events[name])
                sp.wait_ge(s.sem, s.count(Phase(name), former_trips + s.index[name][event] + 1))
            for c in range(CHUNKS["M"] - RING):
                used_last("M", c)
                load(c % RING, FIRST_CHUNK["M"] + (M_TRIPS - 1) * CHUNKS["M"] + RING + c)

            def spill_load(tile):
                e = sp.value_load(spill[0:1, bass.ds(tile, 1)], min_val=0, max_val=EXPERTS - 1)
                return lambda s: sp.dma_start(ring[:, s, :], weights[e * TILE_CHUNKS + (FIRST_CHUNK["M"] + s)]).then_inc(
                    spill_in[s], 16)
            for b in range(2):
                sp.wait_ge(*o_free[b].by(A, ("table", "trips")[b]))
            n_trips = sp.value_load(trips[0:1, 0:1], min_val=1, max_val=MAX_TRIPS)
            fetch = spill_load(0)
            for s in range(TILE_CHUNKS):
                used_last("M", [c for c in range(CHUNKS["M"]) if c % RING == s][-1])
                fetch(s)
            with sp.Fori(0, n_trips) as j:
                ph = Phase("O", j)
                for u in range(2):
                    fetch = spill_load(j * 2 + (u + 1))
                    for s in range(TILE_CHUNKS):
                        g = LAST_USE["M"][(u * TILE_CHUNKS + s + 1) * PER_CHUNK - 1]
                        sp.wait_ge(*filled(ph, g).by(ph, g))
                        fetch(s)
            def part_load(l, c):
                sp.dma_start(ring[:, c % RAW, :], weights[l * CHUNKS["L"] + (FIRST_CHUNK["L"] + c)]).then_inc(
                    raw_in[c % RAW], 16)
            for t in range(TT):
                sp.wait_ge(picked_in[t], 16 * 2)
            for c in range(RAW):
                sp.wait_ge(spill_in[c], n_trips * 32 + 16)
                part_load(0, c)
            with sp.Fori(0, LAYERS - 1) as l:
                for c in range(CHUNKS["L"]):
                    used(Phase("L", l), c)
                    part_load(l, RAW + c)
            for c in range(CHUNKS["L"] - RAW):
                used_last("L", c)
                part_load(LAYERS - 1, RAW + c)

        @block.tensor
        def _(pe):
            seen = set()

            def wblock(ph, n, width=P):
                c = n // PER_CHUNK
                slot, s, v = chunk_value(ph, c)
                if (ph.name, c) not in seen:
                    seen.add((ph.name, c))
                    pe.wait_ge(s, v)
                o = (n % PER_CHUNK) * P
                return ring[:, slot, o:o + width]

            def open_bank(ph, g):
                b = bank_of[ph.name][g]
                s, v = emptied(ph, g).before(ph, g)
                if not (isinstance(v, int) and v == 0):
                    pe.wait_ge(s, v)
                return lin[:, b, :]

            def linear(ph, g, rhs, kb=KB, n=S, wait=None):
                acc = open_bank(ph, g)
                n0 = BLOCK0[ph.name][g]
                for k in range(kb):
                    w = wblock(ph, n0 + k)
                    if wait:
                        wait(k)
                    mm = pe.matmul(acc[:, 0:n], w, rhs(k), start=(k == 0), stop=(k == kb - 1))
                mm.then_inc(*lin_full[bank_of[ph.name][g]].on(ph, g))

            def w_parts(ph, n, width=P):
                c = n // PER_CHUNK
                if (ph.name, c) not in seen:
                    seen.add((ph.name, c))
                    pe.wait_ge(*w_low.by(ph, c))
                o = (n % PER_CHUNK) * P
                return ring_r[:, HIGH_SLOT[ph.name][c], o:o + width], ring_r[:, c % RAW, o:o + width]

            def split_linear(ph, g, high, low, kb=KB, first=None):
                acc = open_bank(ph, g)
                n0 = BLOCK0[ph.name][g]
                late = kb == KB
                for k in range(kb):
                    wh, wl = w_parts(ph, n0 + k)
                    if first and (first, k) in x_high.index[ph.name]:
                        pe.wait_ge(*x_high.by(ph, (first, k)))
                    pe.matmul(acc, wh, high(k), start=(k == 0), stop=False)
                    mm = pe.matmul(acc, wl, high(k), start=False, stop=False)
                    if not late:
                        if first and (first, k) in x_low.index[ph.name]:
                            pe.wait_ge(*x_low.by(ph, (first, k)))
                        mm = pe.matmul(acc, wh, low(k), start=False, stop=(k == kb - 1))
                        c = (n0 + k) // PER_CHUNK
                        if ph.name == "L" and c in MID and (n0 + k + 1) % PER_CHUNK == 0:
                            mm.then_inc(*w_used.on(ph, c))
                if late:
                    for k in range(kb):
                        wh, _ = w_parts(ph, n0 + k)
                        if first and (first, k) in x_low.index[ph.name]:
                            pe.wait_ge(*x_low.by(ph, (first, k)))
                        mm = pe.matmul(acc, wh, low(k), start=False, stop=(k == kb - 1))
                mm.then_inc(*lin_full[bank_of[ph.name][g]].on(ph, g))

            def split_tokens(ph, g, n0, tok, n):
                acc = open_bank(ph, g)
                for k in range(KB):
                    wh, wl = w_parts(ph, n0 + k * (n // P), n)
                    pe.matmul(acc[:, 0:n], tok(h_r, k), wh, start=(k == 0), stop=False)
                    pe.matmul(acc[:, 0:n], tok(h_r, k), wl, start=False, stop=False)
                    mm = pe.matmul(acc[:, 0:n], tok(low_r, k), wh, start=False, stop=(k == KB - 1))
                mm.then_inc(*lin_full[bank_of[ph.name][g]].on(ph, g))

            def tokens(ph, g, n0, lhs, n):
                acc = open_bank(ph, g)
                for k in range(KB):
                    for b in range(0, n, P):
                        w = wblock(ph, n0 + k * (n // P) + b // P)
                    w = wblock(ph, n0 + k * (n // P), n)
                    mm = pe.matmul(acc[:, 0:n], lhs(k), w, start=(k == 0), stop=(k == KB - 1))
                mm.then_inc(*lin_full[bank_of[ph.name][g]].on(ph, g))

            def mean_sum(ph, st, src, wait):
                for k in range(KB):
                    wait(k)
                    mm = pe.matmul(sums[:, 0, :], ones_d[:, :], src[:, k, :], start=(k == 0), stop=(k == KB - 1))
                mm.then_inc(*mean_full.on(ph, st))

            def square_sum(ph, st, k, src, ones, n_k=KB, n=S):
                pe.wait_ge(*squares.by(ph, (st, k)))
                mm = pe.matmul(sums[:, 0, 0:n], ones[:, :], src, start=(k == 0), stop=(k == n_k - 1))
                if k == n_k - 1:
                    mm.then_inc(*var_full.on(ph, st))

            def last_sum(ph, st, src):
                pe.wait_ge(*square_sums.by(ph, (st, KB - 1)))
                pe.matmul(sums[:, 0, :], ones_d[:, :], src, start=True, stop=True).then_inc(*var_full.on(ph, st))

            def attention(ph, q_of, k_of, v_of, extra=None, between=None):
                name = ph.name
                tl, rs = TILES[name], ROUNDS[name]

                def qk(i):
                    kind, hp, half, t = tl[i]
                    lo = DH * half
                    if i >= 1 and (kind == "dil" or tl[i - 1][0] == "dil"):
                        pe.wait_ge(*scored.by(ph, i - 1))
                    elif i >= 2 and kind == "mem" and tl[i - 2][0] == "mem":
                        pe.wait_ge(*exp_done.by(ph, i - 2))
                    elif i >= 2:
                        pe.wait_ge(*scored.by(ph, i - 2))
                    if kind == "dil":
                        for g in range(DIL_G):
                            q = qb[lo:lo + DH, g, t::4]
                            k = kb[lo:lo + DH, g, :] if g == 0 else kb[lo:lo + DH, g, t::4]
                            o = score_flat[:, 0:S] if g == 0 else score_flat[:, S + (g - 1) * P:S + g * P]
                            mm = pe.matmul(o, q, k, start=True, stop=True)
                    else:
                        n = key_chunks(kind, t) * P
                        mm = pe.matmul(score[:, i % 2, 0:n], q_of(kind)[lo:lo + DH, hp, t * P:(t + 1) * P],
                                       k_of(kind)[lo:lo + DH, hp, 0:n], start=True, stop=True)
                    mm.then_inc(*qk_done.on(ph, i))

                def turn(j):
                    i, c0, n = rs[j]
                    if c0 == 0:
                        pe.wait_ge(*p_ready.by(ph, i))
                    if j >= 1:
                        pe.wait_ge(*pt_ready.by(ph, j - 1))
                    for c in range(n):
                        mm = pe.transpose(trans[:, 0, c * P:(c + 1) * P],
                                          probs[name][i % 3][:, (c0 + c) * P:(c0 + c + 1) * P], ident)
                    mm.then_inc(*t_done.on(ph, j))

                def pv(j):
                    i, c0, n = rs[j]
                    kind, hp, half, t = tl[i]
                    o = OUTS[name].index((kind, hp))
                    if o >= 2 and c0 == 0:
                        pe.wait_ge(*o_out.by(ph, OUTS[name][o - 2]))
                    pe.wait_ge(*pt_ready.by(ph, j))
                    total = key_chunks(kind, t)
                    lo = DH * half
                    for c in range(n):
                        mm = pe.matmul(attn[lo:lo + DH, o % 2, t * P:(t + 1) * P], v_of(kind, hp, half, t, c0 + c),
                                       probsT[name][j % 2][:, c * P:(c + 1) * P],
                                       start=(c0 + c == 0), stop=(c0 + c == total - 1))
                    mm.then_inc(*pv_done.on(ph, j))

                n = len(tl)
                for i in range(n + 3):
                    if extra and i < n:
                        extra(i)
                    if i < n:
                        qk(i)
                    if 2 <= i < n + 2:
                        for j in ROUNDS_OF[name][i - 2]:
                            turn(j)
                            if between and rs[j][1] == 0:
                                between(i - 2)
                            if j >= 1:
                                pv(j - 1)
                pv(len(rs) - 1)

            pe.wait_ge(dve_step, 6)
            pe.wait_ge(x_in, 16)
            mean_sum(A, "ln1", x, lambda k: None)
            pe.wait_ge(*centred.by(A, ("ln1", 7)))
            for k in range(KB):
                square_sum(A, "ln1", k, y[:, k, :], ones_d)
            pe.wait_ge(*sd_ready.by(A, "ln1"))

            def ada(g):
                acc = open_bank(A, f"ada{g}")
                pe.wait_ge(*ada_step.by(A, (g, KB - 1)))
                for m in range(16):
                    mm = pe.matmul(acc[:, m:m + 1], ada_sum[:, m * P:(m + 1) * P], ones[:, 0:1], start=True, stop=True)
                mm.then_inc(*lin_full[bank_of["A"][f"ada{g}"]].on(A, f"ada{g}"))

            ada(0)
            pe.wait_ge(consts_in, 16 * 4)
            acc = open_bank(A, "f")
            for k in range(KB):
                pe.wait_ge(*affine.by(A, ("ln1", k)))
                mm = pe.matmul(acc[0:HEADS, :], wf[:, k, :], low[:, k, :], start=(k == 0), stop=(k == KB - 1))
            mm.then_inc(*lin_full[bank_of["A"]["f"]].on(A, "f"))
            def first_linear(g, first=None):
                split_linear(A, g, lambda k: h_r[:, k, :], lambda k: low_r[:, k, :], first=first)
            for n in ("xb", "gb"):
                for m in range(4):
                    first_linear(f"{n}{m}", "ln1" if (n, m) == ("xb", 0) else None)
                if n == "xb":
                    for k in range(KB):
                        square_sum(A, "mem", k, mem_sq(k), ones_d, n=N_MEM)
            ada(1)
            for n in ("r", "i"):
                for m in range(4):
                    linear(A, f"{n}{m}", lambda k: xc[:, m, :], kb=1,
                           wait=lambda k: pe.wait_ge(*conv.by(A, (m, CONV - 1))))
            for n in ("q", "k"):
                for m in range(4):
                    first_linear(f"{n}{m}")
            for t in range(TT):
                split_tokens(A, f"v{t}", BLOCK0["A"]["v3"], lambda b, k: b[:, k, t * P:(t + 1) * P], 512)
            for k in range(4):
                square_sum(A, "lru", k, ig[:, k, :], ones, n_k=4)
            acc = open_bank(A, "cumT")
            pe.wait_ge(*f_step.by(A, "cum"))
            for t in range(TT):
                mm = pe.transpose(acc[:, t * HEADS:(t + 1) * HEADS], fl[:, t * P:(t + 1) * P], ident[0:HEADS, 0:HEADS])
            mm.then_inc(*lin_full[bank_of["A"]["cumT"]].on(A, "cumT"))

            def negcum(i):
                todo = [0, 1] if i == 0 else [i // TT + 1] if i % TT == 0 else []
                for hd in todo:
                    if hd < HEADS:
                        acc = open_bank(A, f"nc{hd}")
                        if hd == 0:
                            pe.wait_ge(*f_step.by(A, "neg"))
                        pe.matmul(acc, ident[0:HEADS, hd:hd + 1].to_broadcast([HEADS, P]), ncum,
                                  start=True, stop=True).then_inc(*lin_full[bank_of["A"][f"nc{hd}"]].on(A, f"nc{hd}"))

            pe.wait_ge(*lin_free[bank_of["A"]["v2"]].by(A, "v2"))
            pe.wait_ge(*lin_free[bank_of["A"]["v3"]].by(A, "v3"))
            attention(A, lambda kind: qT, lambda kind: kT,
                      lambda kind, hp, half, t, c: v_tok[:, c, (2 * hp + half) * DH:(2 * hp + half + 1) * DH],
                      extra=negcum)
            for k in range(4):
                square_sum(A, "attn", k, low[:, k, :], ones, n_k=4)
            pe.wait_ge(*x_low.by(A, ("lru", 3)))
            for m in range(KB):
                split_linear(A, f"out{m}", lambda k: h_r[:, k, :], lambda k: y_r[:, k, :],
                             first="attn" if m == 0 else None)
            for st, src in (("ln2", x), ("ln3", x)):
                ev = (lambda k: x_new.by(A, ("mix", k))) if st == "ln2" else (lambda k: affine.by(A, ("ln2", k)))
                mean_sum(A, st, src, lambda k: pe.wait_ge(*ev(k)))
                pe.wait_ge(*centred.by(A, (st, 7)))
                for k in range(KB):
                    square_sum(A, st, k, (h if st == "ln2" else y)[:, k, :], ones_d)
                if st == "ln2":
                    ada(2)
            for half in range(2):
                acc = open_bank(A, f"rt{half}")
                for t in range(2):
                    for k in range(KB):
                        if half == 0 and t == 0:
                            pe.wait_ge(*affine.by(A, ("ln3", k)))
                        tok = (2 * half + t) * P
                        mm = pe.matmul(acc[:, t * 20:(t + 1) * 20], h[:, k, tok:tok + P], wr[:, k, :],
                                       start=(k == 0), stop=(k == KB - 1))
                mm.then_inc(*lin_full[bank_of["A"][f"rt{half}"]].on(A, f"rt{half}"))
            acc = open_bank(A, "pos")
            pe.wait_ge(*route_ready.by(A, "chosen"))
            for t in range(TT + 1):
                for q in range(min(t + 1, TT)):
                    mm = pe.matmul(acc[:, t * EXPERTS:(t + 1) * EXPERTS], earlier if q == t else ones[:, :],
                                   rw(0)[:, q * EXPERTS:(q + 1) * EXPERTS], start=(q == 0), stop=(q == min(t, TT - 1)))
            mm.then_inc(*filled(A, "pos").on(A, "pos"))
            for t in range(TT):
                for i in range(2):
                    g = f"ut{t}.{i}"
                    acc = open_bank(A, g)
                    for c in range(4):
                        mm = pe.transpose(acc[:, c * P:(c + 1) * P], h[:, 4 * i + c, t * P:(t + 1) * P], ident)
                    mm.then_inc(*filled(A, g).on(A, g))

            def turn_rows(ph, g, i):
                acc = open_bank(ph, g)
                for c in range(4):
                    mm = pe.transpose(acc[:, c * P:(c + 1) * P], xt[:, (4 * i + c) * P:(4 * i + c + 1) * P], ident)
                mm.then_inc(*filled(ph, g).on(ph, g))

            def expert_tile(ph, e, rows):
                for n in ("gate", "up"):
                    acc = open_bank(ph, f"{n}{e}")
                    n0 = BLOCK0[ph.name][f"{n}{e}"]
                    for m in range(EB):
                        for k in range(KB):
                            mm = pe.matmul(acc[:, m * P:(m + 1) * P], wblock(ph, n0 + m * KB + k), xg[e % 2][:, k, :],
                                           start=(k == 0), stop=(k == KB - 1))
                    mm.then_inc(*filled(ph, f"{n}{e}").on(ph, f"{n}{e}"))
                pe.wait_ge(*rows)
                n0 = BLOCK0[ph.name][f"down{e}.1"]
                for i in range(2):
                    turn_rows(ph, f"xt{e}.{i}", i)
                    g = f"down{e}.{i}"
                    acc = open_bank(ph, g)
                    if i == 0:
                        pe.wait_ge(*emptied(ph, f"up{e}").by(ph, f"up{e}"))
                    for k in range(EB):
                        mm = pe.matmul(acc, hid[e % 2][:, k * P:(k + 1) * P], wblock(ph, n0 + k * KB + 4 * i, 4 * P),
                                       start=(k == 0), stop=(k == EB - 1))
                    mm.then_inc(*filled(ph, g).on(ph, g))

            pe.wait_ge(xt_in, 16)
            for i in range(2):
                turn_rows(A, f"xt.{i}", i)
            pe.wait_ge(*emptied(A, "xt.1").by(A, "xt.1"))
            with pe.Fori(0, M_TRIPS) as g:
                ph = Phase("M", g)
                for e in range(TILES_PER_TRIP):
                    expert_tile(ph, e, (xt_in, g * (16 * TILES_PER_TRIP) + 16 * (e + 2)))
            for b in range(2):
                pe.wait_ge(*o_free[b].by(A, ("table", "trips")[b]))
            n_trips = pe.value_load(trips[0:1, 0:1], min_val=1, max_val=MAX_TRIPS)
            for s in lin_free:
                pe.wait_ge(s.sem, s.count(Phase("M"), M_TRIPS * len(s.events["M"])))
            with pe.Fori(0, n_trips) as j:
                ph = Phase("O", j)
                for e in range(2):
                    expert_tile(ph, e, (xt_in, j * 32 + 16 * (EXPERTS + e + 2)))
            for m in range(KB):
                acc = open_bank(B, f"yt{m}")
                for t in range(TT):
                    if m == 0:
                        pe.wait_ge(*picked_sum.by(B, (t, 1)))
                    mm = pe.transpose(acc[:, t * P:(t + 1) * P], picked[:, 2 * t + 1, m * P:(m + 1) * P], ident)
                mm.then_inc(*filled(B, f"yt{m}").on(B, f"yt{m}"))
            mean_sum(B, "ln4", x, lambda k: pe.wait_ge(*x_new.by(B, ("ffn", k))))
            pe.wait_ge(*centred.by(B, ("ln4", 7)))
            for k in range(KB):
                square_sum(B, "ln4", k, h[:, k, :], ones_d)

            with pe.Fori(0, LAYERS) as l:
                ph = Phase("L", l)
                for k in range(KB):
                    square_sum(ph, "pre_mix", k, h[:, k, :], ones_d)
                def normed_linear(g, first=None):
                    split_linear(ph, g, lambda k: h_r[:, k, :], lambda k: low_r[:, k, :], first=first)
                for m in range(14):
                    normed_linear(f"qk{m}", "pre_mix" if m == 0 else None)
                for m in range(2):
                    linear(ph, f"km{m}", lambda k: mem[:, k, :], n=N_MEM)
                for t in range(TT):
                    split_tokens(ph, f"va{t}", BLOCK0["L"]["va3"], lambda b, k: b[:, k, t * P:(t + 1) * P], 512)
                for t in range(2):
                    tokens(ph, f"vm{t}", BLOCK0["L"]["vm1"], lambda k: mem[:, k, t * P:(t + 1) * P], 256)
                for r in range(4):
                    split_tokens(ph, f"vb{r}", BLOCK0["L"]["vb3"], lambda b, k: b[:, k, r::4], 256)
                pe.wait_ge(*lin_free[bank_of["L"]["vb2"]].by(ph, "vb2"))
                pe.wait_ge(*lin_free[bank_of["L"]["vb3"]].by(ph, "vb3"))

                def v_of(kind, hp, half, t, c):
                    lo = (2 * hp + half) * DH
                    if kind == "na":
                        return va[:, c, lo:lo + DH]
                    if kind == "mem":
                        return vm[:, c, lo:lo + DH]
                    if c < 4:
                        return va[:, c, D_A + lo:D_A + lo + DH]
                    return vb[:, t, (c - 4) * P + lo:(c - 4) * P + lo + DH]
                def gate_product(n):
                    g, i = GATES[n // (3 * KB)], n % (3 * KB)
                    acc = open_bank(ph, g) if i == 0 else lin[:, bank_of["L"][g], :]
                    late = i >= 2 * KB
                    k = i - 2 * KB if late else i // 2
                    w = w_parts(ph, BLOCK0["L"][g] + k)[0 if late else i % 2]
                    mm = pe.matmul(acc, w, (low_r if late else h_r)[:, k, :], start=(i == 0), stop=(i == 3 * KB - 1))
                    if i == 3 * KB - 1:
                        mm.then_inc(*lin_full[bank_of["L"][g]].on(ph, g))

                def gate_products(i):
                    for n in range(GATE_AT[i], GATE_AT[i + 1]):
                        gate_product(n)
                attention(ph, lambda kind: qa if kind == "na" else qm, lambda kind: ka if kind == "na" else kmT, v_of,
                          between=gate_products)

                for g in GATES[GATES_BETWEEN:GATES_AHEAD]:
                    normed_linear(g)
                for j, g in enumerate(BRANCHES):
                    width = BRANCH_BLOCKS[j % 3]
                    o = sum(BRANCH_BLOCKS[:j % 3])
                    if j < 3:
                        pe.wait_ge(*x_low.by(ph, ("o", o + width - 1)))
                    split_linear(ph, g, lambda k: o_high[:, o + k, :], lambda k: ob_r[:, o + k, :], kb=width)
                    if j + GATES_AHEAD < len(GATES):
                        normed_linear(GATES[j + GATES_AHEAD])
                for m in range(KB):
                    split_linear(ph, f"out{m}", lambda k: y_high[:, k, :], lambda k: y_r[:, k, :],
                                 first="y" if m == 0 else None)
                last_sum(ph, "post_mix", big[:, FB - 1, :])
                for k in range(KB):
                    square_sum(ph, "pre_ffn", k, h[:, k, :], ones_d)
                for j in range(FB):
                    normed_linear(f"a{j}", "pre_ffn" if j == 0 else None)
                    normed_linear(f"b{j}")
                for m in range(KB):
                    split_linear(ph, f"down{m}", lambda k: f_high[k], lambda k: big_r[:, k, :], kb=FB,
                                 first="f" if m == 0 else None)
                last_sum(ph, "post_ffn", squares_of[(KB - 1) % 4])

        @block.scalar
        def _(act):
            def full(ph, g):
                act.wait_ge(*filled(ph, g).by(ph, g))
                return lin[:, bank_of[ph.name][g], :], emptied(ph, g)

            def square(ph, st, k, src, dst):
                act.activation(dst, src, ACT.Square).then_inc(*squares.on(ph, (st, k)))

            def root(ph, st, e, n=S, scale=1.0):
                act.wait_ge(*var_full.by(ph, st))
                act.activation(sd[:, 0:n], sums[:, 0, 0:n], ACT.Sqrt, bias=e, scale=scale).then_inc(*sd_ready.on(ph, st))

            def affine_of(ph, st, k, dst, g, b, src=None):
                act.wait_ge(*normed.by(ph, (st, k)))
                act.activation(dst, dst if src is None else src, ACT.Identity, bias=b, scale=g).then_inc(*affine.on(ph, (st, k)))

            def attention(ph, extra=None, after=None):
                name = ph.name
                tl = TILES[name]

                def exp(i):
                    kind, hp, half, t = tl[i]
                    n = key_chunks(kind, t) * P
                    p = probs[name][i % 3][:, 0:n]
                    act.wait_ge(*scored.by(ph, i))
                    src = score[:, i % 2, 0:n] if kind == "mem" else p
                    if kind == "mem" and i >= 3:
                        act.wait_ge(*t_done.by(ph, ROUNDS_OF[name][i - 3][-1]))
                    act.activation(p, src, ACT.Exp, bias=stat[:, 0, i % 4:i % 4 + 1],
                                   scale=-1.0 if kind in ("na", "dil") else 1.0,
                                   accum_out=stat[:, 1, i % 4:i % 4 + 1]).then_inc(*exp_done.on(ph, i))

                def out_of(o):
                    kind, hp = OUTS[name][o]
                    last = max(j for j, r in enumerate(ROUNDS[name]) if tl[r[0]][0:2] == (kind, hp))
                    act.wait_ge(*pv_done.by(ph, last))
                    src = attn[:, o % 2, :]
                    if kind == "dil":
                        dst = obb[:, 0, :].rearrange("p (a r) -> p r a", r=4)
                        src = src.rearrange("p (r a) -> p r a", r=4)
                    else:
                        dst = {"fa": y, "na": oa, "mem": om}[kind][:, hp, :]
                    act.copy(dst, src).then_inc(*o_out.on(ph, (kind, hp)))

                ends = {max(i for i, x in enumerate(tl) if x[0:2] == o): n for n, o in enumerate(OUTS[name])}
                for i in range(len(tl) + 4):
                    if extra:
                        extra(i)
                    if i < len(tl):
                        exp(i)
                        if after:
                            after(i)
                    if i - 4 in ends:
                        out_of(ends[i - 4])

            def split(ph, chunks):
                for c in chunks:
                    slot, s, v = chunk_value(ph, c)
                    if c in FORMER[ph.name]:
                        act.wait_ge(*used_up(ph, FORMER[ph.name][c]))
                    act.wait_ge(s, v)
                    act.copy(ring_r[:, HIGH_SLOT[ph.name][c], :], ring[:, slot, :]).then_inc(*w_high.on(ph, c))

            def high(ph, n, k, dst, src):
                act.copy(dst, src).then_inc(*x_high.on(ph, (n, k)))

            act.dma_start(x[:, :, :], xT_in).then_inc(x_in, 16)
            act.dma_start(vec[:, :], vec_in).then_inc(vec_in_s, 16)
            act.dma_start(consts[:, :], const_in).then_inc(consts_in, 16)
            act.dma_start(wf[:, :, :], small_in).then_inc(consts_in, 16)
            act.dma_start(wr[:, :, :], route_w_in).then_inc(consts_in, 16)
            act.dma_start(route_b[:, :], route_b_in).then_inc(consts_in, 16)
            act.dma_start(mem[:, :, :], memT_in).then_inc(mem_in, 16)
            act.dma_start(dil[:, :, :], dil_in).then_inc(dil_s, 16)

            act.wait_ge(dve_step, 6)
            act.wait_ge(vec_in_s, 16)
            act.activation(silu_c[:, :], vec[:, VEC["c"]:VEC["c"] + KB], ACT.Silu).then_inc(act_step, 1)
            act.wait_ge(*sp_step.by(A, "abs"))
            act.activation(lam[:, 2, :], lam[:, 1, :], ACT.Exp, scale=-1.0).then_inc(*sp_step.on(A, "exp"))
            act.wait_ge(*sp_step.by(A, "exp"))
            act.activation(lam[:, 3, :], lam[:, 2, :], ACT.Ln, bias=eps[:, 2:3]).then_inc(*sp_step.on(A, "ln"))
            for k in range(KB):
                act.wait_ge(*centred.by(A, ("ln1", k)))
                square(A, "ln1", k, h[:, k, :], y[:, k, :])
            root(A, "ln1", eps[:, 0:1])
            split(A, SPLIT["A"][:1])
            act.wait_ge(*mod_ready.by(A, 0))
            for k in range(KB):
                affine_of(A, "ln1", k, low[:, k, :], mod1[:, 8 + k:9 + k], mod[:, k:k + 1], src=h[:, k, :])
            for k in range(KB):
                act.wait_ge(*affine.by(A, ("ln1", k)))
                high(A, "ln1", k, h_r[:, k, :], low[:, k, :])
            split(A, SPLIT["A"][1:HIGH])
            act.wait_ge(*f_step.by(A, "abs"))
            act.activation(fl2, fl2, ACT.Exp, scale=-1.0).then_inc(*f_step.on(A, "exp"))
            act.wait_ge(*f_step.by(A, "exp"))
            act.activation(fl2, fl2, ACT.Ln, bias=eps[0:HEADS, 2:3]).then_inc(*f_step.on(A, "ln"))
            act.wait_ge(*pad_done.by(A, 0))
            act.wait_ge(mem_in, 16)
            for k in range(KB):
                square(A, "mem", k, mem[:, k, :], mem_sq(k))
            for m in range(4):
                acc, free = full(A, f"xb{m}")
                act.copy(xbp[m][:, CONV - 1:], acc).then_inc(*free.on(A, f"xb{m}"))
                split(A, behind.get(("A", f"xb{m}"), []))
            act.wait_ge(*rstd_ready.by(A, "ln1"))
            root(A, "mem", eps[:, 1:2], N_MEM)
            for m in range(4):
                acc, free = full(A, f"gb{m}")
                act.activation(gg[:, m, :], acc, ACT.Gelu_apprx_tanh).then_inc(*free.on(A, f"gb{m}"))
            split(A, q_chunks[:1])
            for n, dst in (("r", r_), ("i", ig)):
                for m in range(4):
                    acc, free = full(A, f"{n}{m}")
                    act.activation(dst[:, m, :], acc, ACT.Sigmoid,
                                   bias=v_(f"b_{n}g", m)).then_inc(*free.on(A, f"{n}{m}"))
            act.wait_ge(*lin_free[bank_of["A"]["r3"]].by(A, "r3"))
            act.wait_ge(*lin_free[bank_of["A"]["r2"]].by(A, "r2"))
            act.wait_ge(*sp_step.by(A, "nc"))
            for m in range(4):
                act.activation(a_[:, m, :], r_[:, m, :], ACT.Exp,
                               scale=lam[:, 5, m:m + 1]).then_inc(*lru_act.on(A, ("a", m)))
            for m in range(4):
                act.wait_ge(*lru_act.by(A, ("a", m)))
                act.activation(r_[:, m, :], r_[:, m, :], ACT.Tanh,
                               scale=lam[:, 4, m:m + 1]).then_inc(*lru_act.on(A, ("th", m)))
            split(A, q_chunks[1:])
            for m in range(4):
                act.wait_ge(*lru_dve.by(A, ("igx", m)))
                act.activation(a2[:, m, :], a_[:, m, :], ACT.Square).then_inc(*lru_act.on(A, ("a2", m)))
            for m in range(4):
                acc, free = full(A, f"q{m}")
                act.activation(qT[:, m, :], acc, ACT.Copy, scale=DH ** -0.5).then_inc(*free.on(A, f"q{m}"))
                split(A, behind.get(("A", f"q{m}"), []))
                if m == 1:
                    for i in range(4):
                        act.wait_ge(*lru_dve.by(A, ("u2", i)))
                        act.activation(r_[:, i, :], r_[:, i, :], ACT.Sqrt).then_inc(*lru_act.on(A, ("sqrt", i)))
            for m in range(4):
                acc, free = full(A, f"k{m}")
                act.copy(kT[:, m, :], acc).then_inc(*free.on(A, f"k{m}"))
                split(A, behind.get(("A", f"k{m}"), []))
            act.wait_ge(*lru_dve.by(A, ("u", 3)))
            for m in range(4):
                acc, free = full(A, f"v{m}")
                act.copy(v_tok[:, m, :], acc).then_inc(*free.on(A, f"v{m}"))
            for k in range(4):
                act.wait_ge(*lru_dve.by(A, ("out", k)))
                square(A, "lru", k, xc[:, k, :], ig[:, k, :])
            act.wait_ge(*rstd_ready.by(A, "mem"))
            root(A, "lru", eps[:, 1:2], scale=1.0 / D_ATTN)

            def negcum(i):
                todo = [0, 1] if i == 0 else [i // TT + 1] if i % TT == 0 else []
                for hd in todo:
                    if hd < HEADS:
                        if hd == 0:
                            act.wait_ge(*f_step.by(A, "cum"))
                        if hd >= 2:
                            act.wait_ge(*scored.by(A, TT * (hd - 1) - 1))
                        acc, free = full(A, f"nc{hd}")
                        act.copy(gat[:, hd % 2, :], acc).then_inc(*free.on(A, f"nc{hd}"))
            attention(A, extra=negcum)
            for k in range(4):
                act.wait_ge(*o_out.by(A, ("fa", k)))
                square(A, "attn", k, y[:, k, :], low[:, k, :])
            split(A, behind[("A", "v3")][:1])
            for k in range(4):
                act.wait_ge(*normed.by(A, ("lru", k)))
                high(A, "lru", k, h_r[:, 4 + k, :], xc[:, k, :])
            act.wait_ge(*rstd_ready.by(A, "lru"))
            root(A, "attn", eps[:, 1:2], scale=1.0 / D_ATTN)
            for k in range(4):
                act.wait_ge(*normed.by(A, ("attn", k)))
                high(A, "attn", k, h_r[:, k, :], y[:, k, :])
            split(A, behind[("A", "v3")][1:])
            for m in range(KB):
                split(A, behind.get(("A", f"out{m}"), []))
            for st in ("ln2", "ln3"):
                src, sq, dst = (x, h, x) if st == "ln2" else (h, y, h)
                for k in range(KB):
                    act.wait_ge(*centred.by(A, (st, k)))
                    square(A, st, k, src[:, k, :], sq[:, k, :])
                root(A, st, eps[:, 0:1])
                if st == "ln3":
                    act.wait_ge(*mod_ready.by(A, 2))
                for k in range(KB):
                    g, b = ((v_("ln1_g", k), v_("ln1_b", k)) if st == "ln2"
                            else (mod1[:, 32 + k:33 + k], mod[:, 24 + k:25 + k]))
                    affine_of(A, st, k, dst[:, k, :], g, b)
            act.wait_ge(*route_sub.by(A, 0))
            act.activation(rtv(1), rtv(1), ACT.Exp).then_inc(*route_exp.on(A, 0))
            for t in range(TT):
                for i in range(2):
                    acc, free = full(A, f"ut{t}.{i}")
                    act.copy(u_tok[:, t, i * S:(i + 1) * S], acc).then_inc(*free.on(A, f"ut{t}.{i}"))

            act.wait_ge(rows_out, 16 * 2 * TT)
            act.dma_start(xt, slots_in[0:P, :]).then_inc(xt_in, 16)

            def expert_tile(ph, e, tile, stored):
                acc, free = full(ph, f"gate{e}")
                act.activation(sil[e % 2], acc, ACT.Silu).then_inc(*free.on(ph, f"gate{e}"))
                for i in range(2):
                    acc, free = full(ph, f"down{e}.{i}")
                    act.copy(yt[:, i, :], acc).then_inc(*free.on(ph, f"down{e}.{i}"))
                    if i == 0:
                        act.wait_ge(*filled(ph, f"xt{e}.1").by(ph, f"xt{e}.1"))
                        act.dma_start(xt, slots_in[bass.ds((tile + 2) * P, P), :]).then_inc(xt_in, 16)
                for i in range(2):
                    act.wait_ge(*emptied(ph, f"down{e}.{i}").by(ph, f"down{e}.{i}"))
                act.dma_start(slots_out[bass.ds(tile * P, P), :],
                              yt.rearrange("p a b -> p (a b)")).then_inc(yt_out, 16)
                act.wait_ge(yt_out, stored)

            act.wait_ge(*lin_full[bank_of["A"]["xt.1"]].by(A, "xt.1"))
            act.dma_start(xt, slots_in[P:2 * P, :]).then_inc(xt_in, 16)
            with act.Fori(0, M_TRIPS) as g:
                for e in range(TILES_PER_TRIP):
                    expert_tile(Phase("M", g), e, g * TILES_PER_TRIP + e,
                                g * (16 * TILES_PER_TRIP) + 16 * (e + 1))
            for b in range(2):
                act.wait_ge(*o_free[b].by(A, ("table", "trips")[b]))
            n_trips = act.value_load(trips[0:1, 0:1], min_val=1, max_val=MAX_TRIPS)
            with act.Fori(0, n_trips) as j:
                for e in range(2):
                    expert_tile(Phase("O", j), e, j * 2 + (EXPERTS + e), j * 32 + 16 * (EXPERTS + e + 1))
            for k in range(KB):
                act.wait_ge(*centred.by(B, ("ln4", k)))
                square(B, "ln4", k, x[:, k, :], h[:, k, :])
            root(B, "ln4", eps[:, 0:1])
            for k in range(KB):
                affine_of(B, "ln4", k, x[:, k, :], v_("ln2_g", k), v_("ln2_b", k))

            act.wait_ge(*affine.by(B, ("ln4", KB - 1)))
            for s in range(RAW, RING):
                act.wait_ge(spill_in[s], n_trips * 32 + 16)
            with act.Fori(0, LAYERS) as l:
                ph = Phase("L", l)

                def normed_parts(st):
                    for k in range(KB):
                        act.wait_ge(*normed.by(ph, (st, k)))
                        high(ph, st, k, h_r[:, k, :], low[:, k, :])
                act.dma_start(lvec[:, :], lvec_in[l]).then_inc(lvec_s, 16)
                act.dma_start(nab[:, 0, :], na_bias_in[l * NA_HEADS]).then_inc(nab_s, 16)
                for k in range(KB):
                    square(ph, "pre_mix", k, x[:, k, :], h[:, k, :])
                split(ph, SPLIT["L"][:HIGH])
                root(ph, "pre_mix", eps[:, 1:2])
                normed_parts("pre_mix")
                for m in range(14):
                    acc, free = full(ph, f"qk{m}")
                    dst = ([qa[:, i, :] for i in range(3)] + [ka[:, i, :] for i in range(3)]
                           + [qb[:, i, :] for i in range(3)] + [kb[:, i, :] for i in range(3)]
                           + [qm[:, i, :] for i in range(2)])[m]
                    is_q = m < 3 or 6 <= m < 9 or m >= 12
                    act.activation(dst, acc, ACT.Copy, scale=DH ** -0.5 if is_q else 1.0).then_inc(*free.on(ph, f"qk{m}"))
                    split(ph, behind.get(("L", f"qk{m}"), []))
                for n, dst, w in ([(f"km{m}", kmT[:, m, :], N_MEM) for m in range(2)]
                                  + [(f"va{t}", va[:, t, :], S) for t in range(TT)]
                                  + [(f"vm{t}", vm[:, t, :], D_M) for t in range(2)]
                                  + [(f"vb{r}", vb[:, r, :], 2 * P) for r in range(4)]):
                    acc, free = full(ph, n)
                    act.copy(dst, acc[:, 0:w]).then_inc(*free.on(ph, n))
                    split(ph, behind.get(("L", n), []))

                def next_bias(i):
                    hd = i // TT + 1
                    if i % TT == 0 and hd < NA_HEADS:
                        act.dma_start(nab[:, hd % 2, :], na_bias_in[l * NA_HEADS + hd]).then_inc(nab_s, 16)
                def gate(j):
                    g = GATES[j]
                    if j >= GATES_AHEAD:
                        b = BRANCHES[j - GATES_AHEAD]
                        act.wait_ge(*lin_free[bank_of["L"][b]].by(ph, b))
                    acc, free = full(ph, g)
                    act.activation(gate_of[j % GATES_AHEAD], acc, ACT.Sigmoid,
                                   bias=lv("b_gate", 8 * (j % 3) + j // 3)).then_inc(*free.on(ph, g))
                    if j >= GATES_BETWEEN:
                        split(ph, behind.get(("L", g), []))

                def between(i):
                    next_bias(i)
                    if i in GATE_DONE:
                        gate(GATE_DONE[i])
                    out_parts(OUT_DONE.get(i, ()))

                def out_parts(ks):
                    for k in ks:
                        act.wait_ge(*o_out.by(ph, OUTS["L"][k]))
                        high(ph, "o", k, o_high[:, k, :], ob[:, k, :])
                attention(ph, after=between)
                for g in GATES[:GATES_BETWEEN]:
                    split(ph, behind.get(("L", g), []))
                out_parts((5,))
                for j in range(GATES_BETWEEN - 1, GATES_AHEAD):
                    gate(j)
                for j, b in enumerate(BRANCHES):
                    split(ph, behind.get(("L", b), []))
                    if j + GATES_AHEAD < len(GATES):
                        gate(j + GATES_AHEAD)
                    m = j // 3
                    if j % 3 == 2 and m >= 1:
                        act.wait_ge(*merged.by(ph, m - 1))
                        high(ph, "y", m - 1, y_high[:, m - 1, :], y[:, m - 1, :])
                act.wait_ge(*merged.by(ph, KB - 1))
                high(ph, "y", KB - 1, y_high[:, KB - 1, :], y[:, KB - 1, :])
                for m in range(KB):
                    acc, free = full(ph, f"out{m}")
                    square(ph, "post_mix", m, acc, big[:, FB - KB + m, :])
                    act.copy(h[:, m, :], acc).then_inc(*free.on(ph, f"out{m}"))
                    if m < KB - 1:
                        split(ph, behind.get(("L", f"out{m}"), []))
                root(ph, "post_mix", eps[:, 1:2])
                for k in range(KB):
                    act.wait_ge(*x_new.by(ph, ("post_mix", k)))
                    square(ph, "pre_ffn", k, x[:, k, :], h[:, k, :])
                split(ph, behind.get(("L", f"out{KB - 1}"), []))
                root(ph, "pre_ffn", eps[:, 1:2])
                normed_parts("pre_ffn")

                def conv_mid(n, j):
                    f = j if n == "a" else FB + j
                    acc, _ = full(ph, f"{n}{j}")
                    dst = (ffa if n == "a" else ffb)[j % 2]
                    if j >= 2:
                        act.wait_ge(*ff_ready.by(ph, j - 2))
                    act.activation(dst, acc, ACT.Identity, bias=lv("conv_b", f),
                                   scale=lv("conv_w", 2 * FB + f)).then_inc(*conv_c.on(ph, (n, j)))

                def gelu(j):
                    act.wait_ge(*lin_free[bank_of["L"][f"a{j}"]].by(ph, f"a{j}"))
                    act.activation(ffg[j % 2], ffa[j % 2], ACT.Gelu_apprx_tanh).then_inc(*gelu_ready.on(ph, j))
                def f_parts(ks):
                    for k in ks:
                        act.wait_ge(*ff_ready.by(ph, k))
                        high(ph, "f", k, f_high[k], big[:, k, :])
                for j in range(FB):
                    for n in ("a", "b"):
                        conv_mid(n, j)
                        split(ph, behind.get(("L", f"{n}{j}"), []))
                    gelu(j)
                    if 1 <= j <= KB:
                        f_parts([j - 1])
                f_parts(range(KB, 2 * KB))
                act.wait_ge(*ff_ready.by(ph, FB - 1))
                f_parts(range(2 * KB, FB))
                for m in range(KB):
                    split(ph, ahead.get(("L", f"down{m}"), []))
                    acc, free = full(ph, f"down{m}")
                    if m >= 4:
                        act.wait_ge(*square_sums.by(ph, ("post_ffn", m - 3)))
                    square(ph, "post_ffn", m, acc, squares_of[m % 4])
                    act.copy(low[:, m, :], acc).then_inc(*free.on(ph, f"down{m}"))
                    split(ph, behind.get(("L", f"down{m}"), []))
                root(ph, "post_ffn", eps[:, 1:2])
                act.wait_ge(*x_new.by(ph, ("post_ffn", KB - 1)))

        @block.vector
        def _(dve):
            steps = [0]

            def step(ins):
                steps[0] += 1
                ins.then_inc(dve_step, 1)
                dve.wait_ge(dve_step, steps[0])

            def full(ph, g):
                dve.wait_ge(*filled(ph, g).by(ph, g))
                return lin[:, bank_of[ph.name][g], :], emptied(ph, g)

            def root_inverse(ph, st, n=S):
                dve.wait_ge(*sd_ready.by(ph, st))
                dve.reciprocal(rstd[:, 0:n], sd[:, 0:n]).then_inc(*rstd_ready.on(ph, st))
                dve.wait_ge(*rstd_ready.by(ph, st))

            def centre(ph, st, src, dst):
                dve.wait_ge(*mean_full.by(ph, st))
                for k in range(KB):
                    dve.tensor_tensor(dst[:, k, :], src[:, k, :], sums[:, 0, :],
                                      ALU.subtract).then_inc(*centred.on(ph, (st, k)))

            def scale_all(ph, st, buf):
                root_inverse(ph, st)
                for k in range(KB):
                    dve.tensor_tensor(buf[:, k, :], buf[:, k, :], rstd[:, :], ALU.mult).then_inc(*normed.on(ph, (st, k)))

            def rms_apply(ph, st, dst, src, g, n_k, n=S):
                root_inverse(ph, st, n)
                for k in range(n_k):
                    dve.scalar_tensor_tensor(dst(k), src(k), g(k), rstd[:, 0:n], ALU.mult,
                                             ALU.mult).then_inc(*normed.on(ph, (st, k)))

            def residual(ph, st, src, g):
                root_inverse(ph, st)
                for k in range(KB):
                    dve.scalar_tensor_tensor(tmp[:, k % 2, :], src[:, k, :], lv(g, k), rstd[:, :], ALU.mult,
                                             ALU.mult).then_inc(*upd.on(ph, (st, k)))
                    dve.wait_ge(*upd.by(ph, (st, k)))
                    dve.tensor_tensor(x[:, k, :], x[:, k, :], tmp[:, k % 2, :], ALU.add).then_inc(*x_new.on(ph, (st, k)))

            ada_chunks = {g[1:]: c for c, g in enumerate(LAST_USE["A"][::PER_CHUNK]) if g[0] == "ada"}

            def ada_rows(g, ks=range(KB)):
                for k in ks:
                    slot, s, v = chunk_value(A, ada_chunks[g, k])
                    dve.wait_ge(s, v)
                    w, c = ring[:, slot, :], silu_c[:, k:k + 1]
                    if k == 0:
                        dve.tensor_scalar(ada_sum, w, c, None, ALU.mult).then_inc(*ada_step.on(A, (g, k)))
                    else:
                        dve.wait_ge(*ada_step.by(A, (g, k - 1)))
                        dve.scalar_tensor_tensor(ada_sum, w, c, ada_sum, ALU.mult,
                                                 ALU.add).then_inc(*ada_step.on(A, (g, k)))

            def ada(g):
                acc, free = full(A, f"ada{g}")
                lo = 16 * g
                dve.tensor_tensor(mod[:, lo:lo + 16], acc[:, 0:16],
                                  vec[:, VEC["b_ada"] + lo:VEC["b_ada"] + lo + 16], ALU.add).then_inc(*free.on(A, f"ada{g}"))
                dve.wait_ge(*free.by(A, f"ada{g}"))
                dve.tensor_scalar(mod1[:, lo:lo + 16], mod[:, lo:lo + 16], 1.0, None, ALU.add).then_inc(*mod_ready.on(A, g))

            def attention(ph, extra=None):
                name = ph.name
                tl = TILES[name]

                def inverse(i):
                    dve.wait_ge(*exp_done.by(ph, i))
                    dve.reciprocal(stat[:, 2, i % 4:i % 4 + 1], stat[:, 1, i % 4:i % 4 + 1]).then_inc(*rden_ready.on(ph, i))

                def scores(i):
                    kind, hp, half, t = tl[i]
                    nm, far = stat[:, 0, i % 4:i % 4 + 1], stat[:, 3, i % 4:i % 4 + 1]
                    n = key_chunks(kind, t) * P
                    p = probs[name][i % 3]
                    s = score[:, i % 2, :]
                    if kind == "fa":
                        hd = 2 * hp + half
                        dve.scalar_tensor_tensor(p[:, 0:n], gat[:, hd % 2, 0:n], cumq[:, t, hd:hd + 1], s[:, 0:n],
                                                 ALU.add, ALU.add).then_inc(*score_step.on(ph, (i, 0)))
                        dve.wait_ge(*score_step.by(ph, (i, 0)))
                        dve.tensor_tensor(p[:, n - P:n], p[:, n - P:n], causal, ALU.add).then_inc(*score_step.on(ph, (i, 1)))
                        dve.wait_ge(*score_step.by(ph, (i, 1)))
                        dve.tensor_reduce(nm, p[:, 0:n], AX_X, ALU.max).then_inc(*score_step.on(ph, (i, 2)))
                        dve.wait_ge(*score_step.by(ph, (i, 2)))
                        dve.tensor_scalar(nm, nm, -1.0, None, ALU.mult).then_inc(*scored.on(ph, i))
                    elif kind == "na":
                        hd = 2 * hp + half
                        lo = (2 * TT - 2 - 2 * t) * GRID_W
                        dve.tensor_tensor_reduce(p[:, 0:n], s, nab[:, hd % 2, lo:lo + S], -1.0, BIG, ALU.add, ALU.min,
                                                 nm).then_inc(*scored.on(ph, i))
                    elif kind == "dil":
                        dve.tensor_tensor_reduce(p[:, 0:S], score_flat[:, 0:S], dil[:, half, 3 - t:3 - t + S], -1.0, BIG,
                                                 ALU.add, ALU.min, nm).then_inc(*score_step.on(ph, (i, 0)))
                        dve.tensor_tensor_reduce(p[:, S:n], score_flat[:, S:n], dil[:, half, S + 3:], -1.0, BIG,
                                                 ALU.add, ALU.min, far).then_inc(*score_step.on(ph, (i, 1)))
                        dve.wait_ge(*score_step.by(ph, (i, 1)))
                        dve.tensor_tensor(nm, nm, far, ALU.min).then_inc(*scored.on(ph, i))
                    else:
                        dve.tensor_reduce(nm, s[:, 0:n], AX_X, ALU.max).then_inc(*score_step.on(ph, (i, 0)))
                        dve.wait_ge(*score_step.by(ph, (i, 0)))
                        dve.tensor_scalar(nm, nm, -1.0, None, ALU.mult).then_inc(*scored.on(ph, i))

                def gather(j):
                    i, c0, n = ROUNDS[name][j]
                    dve.wait_ge(*t_done.by(ph, j))
                    if j >= 2:
                        dve.wait_ge(*pv_done.by(ph, j - 2))
                    dve.tensor_copy(probsT[name][j % 2][:, 0:n * P], trans[:, 0, 0:n * P]).then_inc(*pt_ready.on(ph, j))

                n = len(tl)
                for i in range(n + 2):
                    if i < n:
                        kind = tl[i][0]
                        dve.wait_ge(*qk_done.by(ph, i))
                        if kind == "na" and i % TT == 0:
                            dve.wait_ge(*nab_ready.by(ph, i // TT))
                        if kind == "fa" and i % TT == 0:
                            hd = i // TT
                            dve.wait_ge(*lin_free[bank_of["A"][f"nc{hd}"]].by(A, f"nc{hd}"))
                        if i >= 3 and kind != "mem":
                            dve.wait_ge(*t_done.by(ph, ROUNDS_OF[name][i - 3][-1]))
                    if 1 <= i <= n:
                        inverse(i - 1)
                    elif name == "L" and i == 0:
                        dve.memset(stat[:, 3, :], BIG)
                    if i < n:
                        scores(i)
                    if i >= 2:
                        for j in ROUNDS_OF[name][i - 2]:
                            gather(j)
                    if extra:
                        extra(i)

            def split(ph, chunks):
                for c in chunks:
                    dve.wait_ge(*w_high.by(ph, c))
                    slot = c % RAW
                    dve.tensor_tensor(ring_r[:, slot, :], ring[:, slot, :], whole(ring_r[:, HIGH_SLOT[ph.name][c], :]),
                                      ALU.subtract).then_inc(*w_low.on(ph, c))

            def low_part(ph, n, k, dst, src, high):
                dve.wait_ge(*x_high.by(ph, (n, k)))
                dve.tensor_tensor(dst, src, whole(high), ALU.subtract).then_inc(*x_low.on(ph, (n, k)))

            for dst, val in ((ones_d[:, :], 1.0 / D), (eps[:, 0:1], LN_EPS),
                             (eps[:, 1:2], RMS_EPS), (eps[:, 2:3], 1.0), (one_row, 1.0), (ones[:, :], 1.0)):
                step(dve.memset(dst, val))

            dve.wait_ge(vec_in_s, 16)
            lamv = vec[:, VEC["lam"]:VEC["lam"] + 4]
            dve.tensor_scalar(lam[:, 0, :], lamv, -1.0, None, ALU.mult).then_inc(*sp_step.on(A, "neg"))
            dve.wait_ge(*sp_step.by(A, "neg"))
            dve.tensor_tensor(lam[:, 1, :], lamv, lam[:, 0, :], ALU.max).then_inc(*sp_step.on(A, "abs"))
            dve.wait_ge(x_in, 16)
            centre(A, "ln1", x, h)
            dve.wait_ge(act_step, 1)
            ada_rows(0)
            scale_all(A, "ln1", h)
            dve.wait_ge(*sp_step.by(A, "ln"))
            dve.scalar_tensor_tensor(lam[:, 3, :], lam[:, 0, :], 0.0, lam[:, 3, :], ALU.max,
                                     ALU.add).then_inc(*sp_step.on(A, "sp"))
            dve.wait_ge(*sp_step.by(A, "sp"))
            dve.tensor_scalar(lam[:, 4, :], lam[:, 3, :], LRU_C, None, ALU.mult).then_inc(*sp_step.on(A, "c"))
            dve.tensor_scalar(lam[:, 5, :], lam[:, 3, :], -LRU_C, None, ALU.mult).then_inc(*sp_step.on(A, "nc"))
            ada(0)
            split(A, SPLIT["A"][:1])
            for m in range(4):
                ins = dve.memset(xbp[m][:, 0:CONV - 1], 0.0)
                if m < 3:
                    step(ins)
            ins.then_inc(*pad_done.on(A, 0))
            acc, free = full(A, "f")
            dve.tensor_scalar(fl, acc[0:HEADS, :], v_("b_f")[0:HEADS, :], None, ALU.add).then_inc(*free.on(A, "f"))
            dve.wait_ge(*free.by(A, "f"))
            for k in range(KB):
                low_part(A, "ln1", k, low_r[:, k, :], low[:, k, :], h_r[:, k, :])
            split(A, SPLIT["A"][1:HIGH])
            step(dve.tensor_scalar(fl2, fl, -1.0, None, ALU.mult))
            dve.tensor_tensor(fl2, fl2, fl, ALU.max).then_inc(*f_step.on(A, "abs"))
            dve.wait_ge(*f_step.by(A, "ln"))
            dve.scalar_tensor_tensor(fl2, fl, 0.0, fl2, ALU.min, ALU.subtract).then_inc(*f_step.on(A, "ls"))
            dve.wait_ge(*f_step.by(A, "ls"))
            dve.tensor_tensor_scan(fl, one_row, fl2, 0.0, ALU.mult, ALU.add).then_inc(*f_step.on(A, "cum"))
            dve.wait_ge(*f_step.by(A, "cum"))
            dve.tensor_scalar(ncum, fl, -1.0, None, ALU.mult).then_inc(*f_step.on(A, "neg"))
            ada_rows(1, range(2))
            for m in range(4):
                b = bank_of["A"][f"xb{m}"]
                dve.wait_ge(*lin_free[b].by(A, f"xb{m}"))
                dve.tensor_scalar(xc[:, m, :], xbp[m][:, 0:S], v_("conv_w", m), v_("conv_b", m), ALU.mult,
                                  ALU.add).then_inc(*conv.on(A, (m, 0)))
                for j in range(1, CONV):
                    dve.wait_ge(*conv.by(A, (m, j - 1)))
                    dve.scalar_tensor_tensor(xc[:, m, :], xbp[m][:, j:j + S], v_("conv_w", 4 * j + m), xc[:, m, :],
                                             ALU.mult, ALU.add).then_inc(*conv.on(A, (m, j)))
                split(A, behind.get(("A", f"xb{m}"), []))
                if m == 1:
                    ada_rows(1, range(2, 4))
            ada_rows(1, range(4, KB))
            ada(1)
            split(A, q_chunks[:1])
            rms_apply(A, "mem", lambda k: mem[:, k, :], lambda k: mem[:, k, :], lambda k: v_("mem_g", k), KB, N_MEM)
            for m in range(4):
                dve.wait_ge(*emptied(A, f"i{m}").by(A, f"i{m}"))
                dve.tensor_tensor(ig[:, m, :], ig[:, m, :], xc[:, m, :], ALU.mult).then_inc(*lru_dve.on(A, ("igx", m)))
            split(A, q_chunks[1:])
            for m in range(4):
                dve.wait_ge(*lru_act.by(A, ("a2", m)))
                dve.scalar_tensor_tensor(r_[:, m, :], a2[:, m, :], 1.0, r_[:, m, :], ALU.add,
                                         ALU.mult).then_inc(*lru_dve.on(A, ("u2", m)))
            split(A, behind[("A", "q1")])
            for m in range(4):
                dve.wait_ge(*lru_dve.by(A, ("igx", m)))
                dve.wait_ge(*lru_act.by(A, ("sqrt", m)))
                dve.tensor_tensor(ig[:, m, :], ig[:, m, :], r_[:, m, :], ALU.mult).then_inc(*lru_dve.on(A, ("u", m)))
            for m in range(4):
                dve.wait_ge(*lru_dve.by(A, ("u", m)))
                dve.tensor_tensor_scan(a2[:, m, :], a_[:, m, :], ig[:, m, :], 0.0, ALU.mult,
                                       ALU.add).then_inc(*lru_dve.on(A, ("scan", m)))
            for m in range(4):
                dve.wait_ge(*lru_dve.by(A, ("scan", m)))
                dve.tensor_tensor(xc[:, m, :], a2[:, m, :], gg[:, m, :], ALU.mult).then_inc(*lru_dve.on(A, ("out", m)))
            for g in ("q3", "k1", "k3"):
                split(A, behind[("A", g)])
            rms_apply(A, "lru", lambda k: xc[:, k, :], lambda k: xc[:, k, :], lambda k: v_("g_lru", k), 4)
            acc, free = full(A, "cumT")
            dve.tensor_copy(cumq[:, :, :].rearrange("p a b -> p (a b)"), acc[:, 0:TT * HEADS]).then_inc(*free.on(A, "cumT"))
            dve.wait_ge(*free.by(A, "cumT"))
            attention(A)
            split(A, behind[("A", "v3")][:1])
            for k in range(4):
                low_part(A, "lru", k, y_r[:, 4 + k, :], xc[:, k, :], h_r[:, 4 + k, :])
            rms_apply(A, "attn", lambda k: y[:, k, :], lambda k: y[:, k, :], lambda k: v_("g_attn", k), 4)
            for k in range(4):
                low_part(A, "attn", k, y_r[:, k, :], y[:, k, :], h_r[:, k, :])
            split(A, behind[("A", "v3")][1:])
            ada_rows(2, range(2))
            for m in range(KB):
                acc, free = full(A, f"out{m}")
                dve.tensor_scalar(tmp[:, m % 2, :], acc, mod1[:, 16 + m:17 + m], None, ALU.mult).then_inc(*free.on(A, f"out{m}"))
                dve.wait_ge(*free.by(A, f"out{m}"))
                dve.scalar_tensor_tensor(x[:, m, :], x[:, m, :], ALPHA, tmp[:, m % 2, :], ALU.mult,
                                         ALU.add).then_inc(*x_new.on(A, ("mix", m)))
                split(A, behind.get(("A", f"out{m}"), []))
                if m in (4, 6):
                    ada_rows(2, range(2, 4) if m == 4 else range(4, 5))
            dve.wait_ge(*x_new.by(A, ("mix", KB - 1)))
            centre(A, "ln2", x, x)
            ada_rows(2, range(5, KB))
            scale_all(A, "ln2", x)
            ada(2)
            centre(A, "ln3", x, h)
            scale_all(A, "ln3", h)
            for half in range(2):
                acc, free = full(A, f"rt{half}")
                dve.tensor_tensor(rtv(0)[:, half * 40:half * 40 + 40], acc[:, 0:40],
                                  route_b[:, half * 40:half * 40 + 40], ALU.add).then_inc(*free.on(A, f"rt{half}"))
            for half in range(2):
                dve.wait_ge(*lin_free[bank_of["A"][f"rt{half}"]].by(A, f"rt{half}"))

            def q4(i):
                return rtv(i).rearrange("p (a b) -> p a b", b=4)

            def col(i, n=20):
                return rtv(i)[:, 0:n]

            def spread(ap, n=20, w=4):
                return ap.unsqueeze(2).to_broadcast([P, n, w])
            step(dve.tensor_reduce(col(2), q4(0), AX_X, ALU.max))
            dve.tensor_tensor(q4(1), q4(0), spread(col(2)), ALU.subtract).then_inc(*route_sub.on(A, 0))
            dve.wait_ge(*route_exp.by(A, 0))
            step(dve.tensor_reduce(col(2), q4(1), AX_X, ALU.add))
            step(dve.reciprocal(col(3), col(2)))
            step(dve.tensor_tensor(q4(4), q4(1), spread(col(3)), ALU.mult))
            step(dve.memset(rtv(5), 0.0))
            for i in range(4):
                for lo, hi, op in ((0, i, ALU.is_gt), (i + 1, 4, ALU.is_ge)):
                    if hi > lo:
                        w = hi - lo
                        step(dve.tensor_tensor(q4(6)[:, :, 0:w], q4(4)[:, :, i:i + 1].to_broadcast([P, 20, w]),
                                               q4(4)[:, :, lo:hi], op))
                        step(dve.tensor_tensor(q4(5)[:, :, lo:hi], q4(5)[:, :, lo:hi], q4(6)[:, :, 0:w], ALU.add))
            step(dve.tensor_scalar(rtv(7), rtv(5), 0.5, None, ALU.is_lt))
            step(dve.tensor_tensor(rtv(7), rtv(7), rtv(4), ALU.mult))
            step(dve.tensor_scalar(rtv(8), rtv(5), 1.5, None, ALU.is_lt))
            step(dve.tensor_tensor(rtv(8), rtv(8), rtv(4), ALU.mult))
            step(dve.tensor_reduce(col(2), q4(8), AX_X, ALU.add))
            step(dve.reciprocal(col(3), col(2)))
            step(dve.tensor_tensor(q4(9), q4(8), spread(col(3)), ALU.mult))

            def by_token(i):
                return rtv(i).rearrange("p (t g j) -> p t g j", t=TT, j=4)
            def experts(i):
                return by_token(i)[:, :, 1:5, :]

            def of_group(i):
                return by_token(i)[:, :, 0, :].unsqueeze(3).to_broadcast([P, TT, 4, 4])

            def r4(i):
                return rw(i).rearrange("p (t g j) -> p t g j", t=TT, j=4)

            def r3(i):
                return rw(i).rearrange("p (t e) -> p t e", t=TT)

            def row(i):
                return rw(i)[:, 0:EXPERTS]

            def per_expert(ap):
                return ap.unsqueeze(1).to_broadcast([P, TT, EXPERTS])
            step(dve.tensor_tensor(r4(3), experts(9), of_group(7), ALU.mult))
            step(dve.tensor_scalar(rtv(10), rtv(5), 0.5, None, ALU.is_lt))
            step(dve.tensor_scalar(rtv(11), rtv(5), 1.5, None, ALU.is_lt))
            step(dve.tensor_tensor(r4(1), experts(10), of_group(10), ALU.mult))
            dve.tensor_tensor(r4(0), experts(11), of_group(10), ALU.mult).then_inc(*route_ready.on(A, "chosen"))
            dve.wait_ge(*route_ready.by(A, "chosen"))
            step(dve.tensor_tensor(rw(2), rw(0), rw(1), ALU.subtract))
            acc, free = full(A, "pos")
            dve.tensor_copy(gat_flat[:, 4 * 64:4 * 64 + 80], acc[:, 0:80]).then_inc(*free.on(A, "pos"))
            dve.wait_ge(*free.by(A, "pos"))
            pos, counts = r3(4), row(5)
            step(dve.tensor_scalar(row(6), counts, float(P), None, ALU.is_gt))
            for k in range(2, TT):
                step(dve.scalar_tensor_tensor(row(6), counts, float(k * P), row(6), ALU.is_gt, ALU.add))
            step(dve.tensor_tensor_scan(row(7), ones[:, 0:EXPERTS], row(6), 0.0, ALU.mult, ALU.add))
            step(dve.tensor_tensor(row(8), row(7), row(6), ALU.subtract))
            step(dve.scalar_tensor_tensor(row(8), row(8), float(P), spill_slot, ALU.mult, ALU.add))
            step(dve.tensor_scalar(rw(9), rw(4), float(P), None, ALU.is_ge))
            step(dve.tensor_tensor(r3(9), r3(9), per_expert(row(8)), ALU.mult))
            step(dve.tensor_tensor(r3(10), pos, per_expert(own_slot), ALU.add))
            step(dve.tensor_tensor(rw(9), rw(9), rw(10), ALU.add))
            for i in range(2):
                for src, dst in ((9, rw(11)[:, i * TT:(i + 1) * TT]), (3, weight[:, i * TT:(i + 1) * TT])):
                    step(dve.tensor_tensor(rw(12), rw(1 + i), rw(src), ALU.mult))
                    step(dve.tensor_reduce(dst, r3(12), AX_X, ALU.add))
            dve.tensor_copy(slots[:, :], rw(11)[:, 0:2 * TT]).then_inc(*route_ready.on(A, "slots"))
            n = 12
            t3 = big[0:1, 0, 0:n * EXPERTS].rearrange("p (a b) -> p a b", a=n)
            step(dve.tensor_tensor(t3, row(7)[0:1, :].unsqueeze(1).to_broadcast([1, n, EXPERTS]),
                                   count_row[0:1, 0:n].unsqueeze(2).to_broadcast([1, n, EXPERTS]), ALU.is_le))
            step(dve.tensor_reduce(rw(13)[0:1, 0:n], t3, AX_X, ALU.add))
            step(dve.tensor_scalar(rw(13)[0:1, 0:n], rw(13)[0:1, 0:n], EXPERTS - 1.0, None, ALU.min))
            dve.tensor_copy(spill[0:1, 0:n], rw(13)[0:1, 0:n]).then_inc(*o_free[0].on(A, "table"))
            total = row(7)[0:1, EXPERTS - 1:EXPERTS]
            acc1 = rw(14)[0:1, 0:1]
            step(dve.tensor_scalar(acc1, total, 2.0, 1.0, ALU.is_gt, ALU.add))
            for k in range(2, MAX_TRIPS):
                step(dve.scalar_tensor_tensor(acc1, total, 2.0 * k, acc1, ALU.is_gt, ALU.add))
            dve.tensor_copy(trips[:, :], acc1).then_inc(*o_free[1].on(A, "trips"))
            dve.wait_ge(*o_free[1].by(A, "trips"))
            n_trips = dve.value_load(trips[0:1, 0:1], min_val=1, max_val=MAX_TRIPS)

            def expert_tile(ph, e):
                acc, free = full(ph, f"up{e}")
                dve.wait_ge(*emptied(ph, f"gate{e}").by(ph, f"gate{e}"))
                dve.tensor_tensor(hid[e % 2], sil[e % 2], acc, ALU.mult).then_inc(*free.on(ph, f"up{e}"))
                turned(ph, f"xt{e}", (e + 1) % 2)

            def turned(ph, g, buf):
                for i in range(2):
                    acc, free = full(ph, f"{g}.{i}")
                    dve.tensor_copy(xg_flat[buf][:, i, :], acc).then_inc(*free.on(ph, f"{g}.{i}"))
            turned(A, "xt", 0)
            with dve.Fori(0, M_TRIPS) as g:
                for e in range(TILES_PER_TRIP):
                    expert_tile(Phase("M", g), e)
            with dve.Fori(0, n_trips) as j:
                for e in range(2):
                    expert_tile(Phase("O", j), e)
            for t in range(TT):
                dve.wait_ge(picked_in[t], 16 * 2)
                a, b = picked[:, 2 * t, :], picked[:, 2 * t + 1, :]
                dve.tensor_scalar(a, a, weight[:, t:t + 1], None, ALU.mult).then_inc(*picked_sum.on(B, (t, 0)))
                dve.wait_ge(*picked_sum.by(B, (t, 0)))
                dve.scalar_tensor_tensor(b, b, weight[:, TT + t:TT + t + 1], a, ALU.mult,
                                         ALU.add).then_inc(*picked_sum.on(B, (t, 1)))
            for m in range(KB):
                acc, free = full(B, f"yt{m}")
                dve.tensor_scalar(tmp[:, m % 2, :], acc, mod1[:, 40 + m:41 + m], None, ALU.mult).then_inc(*free.on(B, f"yt{m}"))
                dve.wait_ge(*free.by(B, f"yt{m}"))
                dve.scalar_tensor_tensor(x[:, m, :], x[:, m, :], ALPHA, tmp[:, m % 2, :], ALU.mult,
                                         ALU.add).then_inc(*x_new.on(B, ("ffn", m)))
            dve.wait_ge(*x_new.by(B, ("ffn", KB - 1)))
            centre(B, "ln4", x, x)
            scale_all(B, "ln4", x)
            dve.wait_ge(dil_s, 16)

            with dve.Fori(0, LAYERS) as l:
                ph = Phase("L", l)

                def normed_parts(st, g):
                    rms_apply(ph, st, lambda k: low[:, k, :], lambda k: x[:, k, :], lambda k: lv(g, k), KB)
                    for k in range(KB):
                        low_part(ph, st, k, low_r[:, k, :], low[:, k, :], h_r[:, k, :])
                def add_squares(st, k, square, former):
                    if k >= 1:
                        if k >= 2:
                            dve.wait_ge(*square_sums.by(ph, (st, k - 1)))
                        dve.wait_ge(*squares.by(ph, (st, k)))
                        dve.tensor_tensor(square, square, former, ALU.add).then_inc(*square_sums.on(ph, (st, k)))
                dve.wait_ge(lvec_s, l * 16 + 16)
                split(ph, SPLIT["L"][:HIGH])
                normed_parts("pre_mix", "g_pre_mix")
                for g in LIN["L"][:LIN["L"].index(GATES[0])]:
                    split(ph, behind.get(("L", g), []))

                def between(i):
                    out_parts(OUT_DONE.get(i, ()))

                def out_parts(ks):
                    for k in ks:
                        low_part(ph, "o", k, ob_r[:, k, :], ob[:, k, :], o_high[:, k, :])
                attention(ph, extra=between)
                for g in GATES[:GATES_BETWEEN]:
                    split(ph, behind.get(("L", g), []))
                out_parts((5,))
                for g in GATES[GATES_BETWEEN:GATES_AHEAD]:
                    split(ph, behind.get(("L", g), []))
                for m in range(KB):
                    for i, n in enumerate(("ba", "bb", "bm")):
                        j = 3 * m + i
                        gn = f"g{i}.{m}"
                        dve.wait_ge(*lin_free[bank_of["L"][gn]].by(ph, gn))
                        acc, free = full(ph, f"{n}{m}")
                        dst = y[:, m, :] if i == 0 else tmp[:, i - 1, :]
                        dve.tensor_tensor(dst, acc, gate_of[j % GATES_AHEAD], ALU.mult).then_inc(*free.on(ph, f"{n}{m}"))
                        dve.wait_ge(*free.by(ph, f"{n}{m}"))
                        if i == 1:
                            dve.tensor_tensor(y[:, m, :], y[:, m, :], tmp[:, 0, :], ALU.add).then_inc(*merge_step.on(ph, m))
                        split(ph, behind.get(("L", f"{n}{m}"), []))
                        for g in GATES[j + GATES_AHEAD:j + GATES_AHEAD + 1]:
                            split(ph, behind.get(("L", g), []))
                    dve.wait_ge(*merge_step.by(ph, m))
                    dve.tensor_tensor(y[:, m, :], y[:, m, :], tmp[:, 1, :], ALU.add).then_inc(*merged.on(ph, m))
                    if m >= 1:
                        low_part(ph, "y", m - 1, y_r[:, m - 1, :], y[:, m - 1, :], y_high[:, m - 1, :])
                low_part(ph, "y", KB - 1, y_r[:, KB - 1, :], y[:, KB - 1, :], y_high[:, KB - 1, :])
                for m in range(KB):
                    add_squares("post_mix", m, big[:, FB - KB + m, :], big[:, FB - KB + m - 1, :])
                    if m < KB - 1:
                        split(ph, behind.get(("L", f"out{m}"), []))
                residual(ph, "post_mix", h, "g_post_mix")
                split(ph, behind.get(("L", f"out{KB - 1}"), []))
                normed_parts("pre_ffn", "g_pre_ffn")
                for j in range(FB):
                    for n, buf in (("a", ffa), ("b", ffb)):
                        f = j if n == "a" else FB + j
                        acc, free = full(ph, f"{n}{j}")
                        dve.wait_ge(*conv_c.by(ph, (n, j)))
                        t = buf[j % 2]
                        dve.scalar_tensor_tensor(t[:, 1:S], acc[:, 0:S - 1], lv("conv_w", f), t[:, 1:S], ALU.mult,
                                                 ALU.add).then_inc(*conv_l.on(ph, (n, j)))
                        dve.wait_ge(*conv_l.by(ph, (n, j)))
                        dve.scalar_tensor_tensor(t[:, 0:S - 1], acc[:, 1:S], lv("conv_w", 4 * FB + f), t[:, 0:S - 1],
                                                 ALU.mult, ALU.add).then_inc(*free.on(ph, f"{n}{j}"))
                        split(ph, behind.get(("L", f"{n}{j}"), []))
                    dve.wait_ge(*gelu_ready.by(ph, j))
                    dve.wait_ge(*lin_free[bank_of["L"][f"b{j}"]].by(ph, f"b{j}"))
                    dve.tensor_tensor(big[:, j, :], ffg[j % 2], ffb[j % 2], ALU.mult).then_inc(*ff_ready.on(ph, j))
                    if 2 <= j <= KB + 1:
                        low_part(ph, "f", j - 2, big_r[:, j - 2, :], big[:, j - 2, :], f_high[j - 2])
                for k in range(KB, FB):
                    low_part(ph, "f", k, big_r[:, k, :], big[:, k, :], f_high[k])
                for m in range(KB):
                    split(ph, ahead.get(("L", f"down{m}"), []))
                    add_squares("post_ffn", m, squares_of[m % 4], squares_of[(m - 1) % 4])
                    split(ph, behind.get(("L", f"down{m}"), []))
                residual(ph, "post_ffn", low, "g_post_ffn")

        @block.gpsimd
        def _(pool):
            def attention(ph, extra=None):
                for i, (kind, hp, half, t) in enumerate(TILES[ph.name]):
                    if extra:
                        extra(i)
                    n = key_chunks(kind, t) * P
                    p = probs[ph.name][i % 3][:, 0:n]
                    pool.wait_ge(*rden_ready.by(ph, i))
                    pool.tensor_tensor(p, p, stat[:, 2, i % 4:i % 4 + 1].to_broadcast([P, n]),
                                       ALU.mult).then_inc(*p_ready.on(ph, i))

            pool.memset(zeros, 0.0).then_inc(*zeros_ready.on(A, 0))
            pool.wait_ge(*zeros_ready.by(A, 0))
            pool.wait_ge(*lin_full[bank_of["A"]["v2"]].by(A, "v2"))
            pool.dma_start(slots_in.rearrange("(j p) d -> p j d", p=P),
                           zeros.unsqueeze(1).to_broadcast([P, SLOT_TILES, D])).then_inc(zeros_out, 16)
            pool.dma_start(slots_out[(EXPERTS + 2) * P:, :].rearrange("(j p) d -> p j d", p=P),
                           zeros.unsqueeze(1).to_broadcast([P, 2 * MAX_TRIPS - 2, D])).then_inc(zeros_out, 16)
            attention(A)
            pool.wait_ge(*route_ready.by(A, "slots"))
            pool.wait_ge(zeros_out, 32)
            for t in range(TT):
                for i in range(2):
                    pool.wait_ge(*lin_free[bank_of["A"][f"ut{t}.{i}"]].by(A, f"ut{t}.{i}"))
                for i in range(2):
                    pool.indirect_dma_start(slots_in, bass.IndirectOffsetOnAxis(slots[:, i * TT + t:i * TT + t + 1], 0),
                                            u_tok[:, t, :], None).then_inc(rows_out, 16)
            for b in range(2):
                pool.wait_ge(*o_free[b].by(A, ("table", "trips")[b]))
            n_trips = pool.value_load(trips[0:1, 0:1], min_val=1, max_val=MAX_TRIPS)
            pool.wait_ge(xt_in, n_trips * 32 + 16 * (EXPERTS + 2))
            pool.wait_ge(yt_out, n_trips * 32 + 16 * EXPERTS)
            pool.tensor_tensor(held[:, :], eps[:, 2:3], eps[:, 2:3], ALU.mult)
            for t in range(TT):
                for i in range(2):
                    pool.indirect_dma_start(picked[:, 2 * t + i, :], None, slots_out, bass.IndirectOffsetOnAxis(
                        slots[:, i * TT + t:i * TT + t + 1], 0)).then_inc(picked_in[t], 16)
            pool.wait_ge(consts_in, 16 * 4)
            with pool.Fori(0, LAYERS) as l:
                ph = Phase("L", l)

                def bias(hd):
                    b = nab[:, hd % 2, :].rearrange("p (a b) -> p a b", b=GRID_W)
                    pool.wait_ge(nab_s, l * (16 * NA_HEADS) + 16 * (hd + 1))
                    pool.tensor_tensor(b, b, window.unsqueeze(1).to_broadcast([P, NA_SLOTS, GRID_W]),
                                       ALU.add).then_inc(*nab_ready.on(ph, hd))

                def next_bias(i):
                    if i == 0:
                        bias(0)
                    if i % TT == 2 and i // TT + 1 < NA_HEADS:
                        bias(i // TT + 1)
                attention(ph, extra=next_bias)

            done = Phase("L", None)
            pool.wait_ge(x_new.sem, x_new.count(done, LAYERS * len(x_new.events["L"])))
            pool.dma_start(out, x[:, :, :]).then_inc(out_done, 16)
            pool.wait_ge(out_done, 16)

        for s in signals:
            s.done()


def stationary(w):
    k, m = w.shape
    return w.reshape(k // P, P, m // P, P).transpose(2, 0, 1, 3).reshape(-1, P, P)


def moving(w):
    k, m = w.shape
    return w.reshape(k // P, P, m // P, P).transpose(0, 2, 1, 3).reshape(-1, P, P)


def by_feature(v):
    return np.ascontiguousarray(v.reshape(-1, P).T)


def weight_stream(i):
    w = i["w_in"][0]
    ada = i["w_ada"][0]
    ends = np.cumsum([D_ATTN, D_ATTN, D_ATTN, HEADS, D_ATTN, D_ATTN])
    q, k, v, _, xb, gb = np.split(w, ends[:-1], axis=1)

    def diagonal(g):
        out = np.zeros((4, P, P), np.float32)
        out[:, :DH, :DH], out[:, DH:, DH:] = g[0::2], g[1::2]
        return out
    rows = [moving(ada[:, i * 2048:(i + 1) * 2048]) for i in range(3)]
    pairs = np.concatenate([stationary(xb), stationary(gb)]).reshape(4, PER_CHUNK, P, P)
    xb_gb = np.concatenate([pairs, rows[1].reshape(4, 2 * PER_CHUNK, P, P)], axis=1).reshape(-1, P, P)
    w_out = stationary(i["w_out"][0])
    parts = [rows[0], xb_gb]
    parts += [diagonal(i["w_rg"][0]), diagonal(i["w_ig"][0]), np.zeros((8, P, P), np.float32)]
    parts += [stationary(q), stationary(k), moving(v)]
    parts += [w_out[:4 * KB], rows[2][:2 * PER_CHUNK], w_out[4 * KB:], rows[2][2 * PER_CHUNK:]]
    for e in range(EXPERTS):
        g, u = (stationary(i[n][0, e]).reshape(EB, KB, P, P) for n in ("w_e_gate", "w_e_up"))
        parts += [g.reshape(-1, P, P), u.reshape(-1, P, P), moving(i["w_e_down"][0, e])]
    for l in range(LAYERS):
        w = i["w_in_2"][l]
        ends = np.cumsum([D_A] * 3 + [D_B] * 3 + [D_M] + [D] * 3)
        q_a, k_a, v_a, q_b, k_b, v_b, q_m, g0, g1, g2 = np.split(w, ends[:-1], axis=1)
        parts += [stationary(x) for x in (q_a, k_a, q_b, k_b, q_m)]
        parts += [stationary(i["w_mem_kv_2"][l][:, :D_M]), moving(np.concatenate([v_a, v_b[:, :P]], axis=1))]
        parts += [moving(i["w_mem_kv_2"][l][:, D_M:]), moving(v_b[:, P:])]
        gate, branch = ([stationary(x).reshape(KB, -1, P, P) for x in xs] for xs in
                        ((g0, g1, g2), (i["w_br_a_2"][l], i["w_br_b_2"][l], i["w_br_m_2"][l])))
        gate, branch = ([xs[j % 3][j // 3] for j in range(3 * KB)] for xs in (gate, branch))
        parts += gate[:GATES_AHEAD]
        for j in range(3 * KB):
            parts += [branch[j]] + gate[j + GATES_AHEAD:j + GATES_AHEAD + 1]
        parts += [stationary(i["w_out_2"][l])]
        a, b = (stationary(x).reshape(FB, KB, P, P) for x in np.split(i["w_up_2"][l], 2, axis=1))
        parts += [np.stack([a, b], 1).reshape(-1, P, P), stationary(i["w_down_2"][l])]
    blocks = np.concatenate(parts, axis=0)
    assert blocks.shape[0] == N_CHUNKS * PER_CHUNK, (blocks.shape, N_CHUNKS)
    return np.ascontiguousarray(blocks.reshape(N_CHUNKS, PER_CHUNK, P, P).transpose(0, 2, 1, 3)).reshape(
        N_CHUNKS, P, PER_CHUNK * P)


def window_mask():
    c = np.arange(GRID_W)
    start = np.clip(c - NA_KW // 2, 0, GRID_W - NA_KW)
    inside = (c[None, :] >= start[:, None]) & (c[None, :] < start[:, None] + NA_KW)
    return np.where(inside, 0.0, MASKED).astype(np.float32)


def dilated_bias():
    out = np.full((P, 2, DIL_W), MASKED, np.float32)
    slopes = (2.0 ** (-8.0 * np.arange(1, DIL_HEADS + 1, dtype=np.float32) / DIL_HEADS)).astype(np.float32)
    a = np.arange(P)[:, None]
    for b in range(2):
        for g, (w, d) in enumerate(((128, 1), (512, 4), (2048, 16))):
            dist = np.arange(S + 3)[None, :] - 3 - 4 * a if g == 0 else 4 * (np.arange(P)[None, :] - a)
            ok = (np.abs(dist) <= w // 2) & (dist % d == 0)
            bias = np.where(ok, -slopes[2 * g + b] * np.abs(dist).astype(np.float32), MASKED)
            lo = 0 if g == 0 else S + 3 + (g - 1) * P
            out[:, b, lo:lo + bias.shape[1]] = bias
    return out


def neighborhood_bias(rpb):
    c = np.arange(GRID_W)
    reach = 2 * NA_KW - 1
    pad = np.zeros((*rpb.shape[:3], 2 * GRID_W - 1), np.float32)
    lo = GRID_W - 1 - (NA_KW - 1)
    pad[..., lo:lo + reach] = rpb
    full = pad[..., GRID_W - 1 + c[None, :] - c[:, None]]
    full = full.transpose(0, 1, 3, 2, 4)
    both = np.concatenate([full[:, :, :, 1:], full[:, :, :, :-1]], axis=2)
    return np.ascontiguousarray(both).reshape(-1, P, NA_SLOTS * GRID_W)


def kernel(**inputs):
    import concourse.bacc as bacc
    from concourse.bass_utils import run_bass_kernel_spmd

    i = {n: np.asarray(a) for n, a in inputs.items()}

    def blocks(a):
        return np.ascontiguousarray(a.reshape(-1, P, a.shape[1]).transpose(1, 0, 2))
    vec = np.zeros((P, N_VEC), np.float32)
    for n, a in (("c", i["c"][0]), ("b_ada", i["b_ada"][0]), ("conv_w", i["conv_w"][0].reshape(-1)),
                 ("conv_b", i["conv_b"][0]), ("b_rg", i["b_rg"][0]), ("b_ig", i["b_ig"][0]),
                 ("lam", i["lru_lambda"][0]), ("g_attn", i["g_attn"][0]), ("g_lru", i["g_lru"][0]),
                 ("ln1_g", i["ln1_g"][0]), ("ln1_b", i["ln1_b"][0]), ("ln2_g", i["ln2_g"][0]),
                 ("ln2_b", i["ln2_b"][0]), ("mem_g", i["mem_norm_g_2"])):
        b = by_feature(a)
        vec[:, VEC[n]:VEC[n] + b.shape[1]] = b
    vec[:HEADS, VEC["b_f"]] = i["b_f"][0]
    lvec = np.zeros((LAYERS, P, N_LVEC), np.float32)
    for l in range(LAYERS):
        for n, a in (("g_pre_mix", i["g_pre_mix_2"]), ("b_gate", i["b_gate_2"]), ("g_post_mix", i["g_post_mix_2"]),
                     ("g_pre_ffn", i["g_pre_ffn_2"]), ("conv_w", i["conv_w_2"]), ("conv_b", i["conv_b_2"]),
                     ("g_post_ffn", i["g_post_ffn_2"])):
            b = by_feature(a[l].reshape(-1))
            lvec[l, :, LVEC[n]:LVEC[n] + b.shape[1]] = b
    q, e = np.arange(P), np.arange(EXPERTS)
    rows = np.concatenate([P * e, P * (EXPERTS - 1) - P * e, e])
    const = np.concatenate([np.eye(P, dtype=np.float32),
                            np.where(q[None, :] <= q[:, None], 0.0, MASKED).astype(np.float32),
                            np.where(q[:, None] < q[None, :], 1.0, 0.0).astype(np.float32),
                            np.concatenate([window_mask()] * 2, axis=0),
                            np.tile(rows.astype(np.float32), (P, 1))], axis=1)
    route_w = np.concatenate([i["w_grp"][0], i["w_exp"][0]], axis=1)
    route_b = np.concatenate([i["b_grp"][0], i["b_exp"][0]])
    f0 = 3 * D_ATTN
    arrays = {
        "weights": weight_stream(i),
        "xT": blocks(i["x"][0].T),
        "memT": blocks(i["mem_2"][0].T),
        "vec": vec,
        "lvec": lvec,
        "w_forget": blocks(i["w_in"][0][:, f0:f0 + HEADS]),
        "w_route": blocks(route_w),
        "b_route": np.ascontiguousarray(np.tile(route_b, (P, TT))),
        "na_bias": neighborhood_bias(i["rpb_na_2"]),
        "const": const,
        "dil_bias": dilated_bias(),
    }
    nc = bacc.Bacc("TRN2", target_bir_lowering=False, num_devices=1)
    args = [nc.dram_tensor(f"in_{n}", a.shape, F32, kind="ExternalInput").ap() for n, a in arrays.items()]
    out = nc.dram_tensor("outT", (P, KB, S), F32, kind="ExternalOutput").ap()
    slots_in = nc.dram_tensor("slots_in", (SLOT_TILES * P, D), F32).ap()
    slots_out = nc.dram_tensor("slots_out", ((EXPERTS + 2 * MAX_TRIPS) * P, D), F32).ap()
    build(nc, args[0], slots_in, slots_out, *args[1:], out)
    r = run_bass_kernel_spmd(nc, [{f"in_{n}": a for n, a in arrays.items()}], core_ids=[0])
    got = r.results[0]["outT"]
    return np.ascontiguousarray(got.transpose(2, 1, 0)).reshape(1, S, D)
```
